# Optimizing a Trainium2 kernel written in Bass

```python
import math
import jax, jax.numpy as jnp
from jax import lax
import numpy as np

D_MODEL = 1024
BATCH = 1
SEQ = 1024
DEPTH = 1
DEC_BATCH = 8
DEC_SEQ = 4
PAST_LEN = 1024
PAGE_SIZE = 128

MIX_WIDTH = D_MODEL
ATTN_WIDTH = MIX_WIDTH // 2
CONV_WIDTH = MIX_WIDTH - ATTN_WIDTH
N_HEADS = 4
N_SUB = 2 * N_HEADS
HEAD_DIM = ATTN_WIDTH // N_SUB
CONV_K = 3
ROPE_THETA = 10000.0
Q_BLOCK = 128
PROJ_COLS = 3 * ATTN_WIDTH + 3 * CONV_WIDTH
N_GROUPS = 4
EXP_PER_GROUP = 8
N_EXPERTS = N_GROUPS * EXP_PER_GROUP
TOP_K_EXP = 2
D_EXPERT = D_MODEL // 4
NORM_EPS = 1e-6
SUBLN_EPS = 1e-5

kernel_name = 'hymba_diffattn_shortconv_hmoe_adaln_step'

def _rmsnorm(x, g, eps=NORM_EPS):
    xf = x.astype(jnp.float32)
    y = xf * lax.rsqrt(jnp.mean(xf * xf, axis=-1, keepdims=True) + eps)
    return (y * g.astype(jnp.float32)).astype(x.dtype)

def _rope(x, pos):
    d = x.shape[-1]
    inv = 1.0 / (ROPE_THETA ** (jnp.arange(0, d, 2, dtype=jnp.float32) / d))
    ang = pos.astype(jnp.float32)[:, None] * inv[None, :]
    ang = jnp.concatenate([ang, ang], axis=-1)
    cos = jnp.cos(ang)[None, :, None, :]
    sin = jnp.sin(ang)[None, :, None, :]
    xf = x.astype(jnp.float32)
    rot = jnp.concatenate([-xf[..., d // 2:], xf[..., :d // 2]], axis=-1)
    return (xf * cos + rot * sin).astype(x.dtype)

def _diff_weights(s, lam):
    p = jax.nn.softmax(s, axis=-1)
    b, _, q, k = p.shape
    p = p.reshape(b, N_HEADS, 2, q, k)
    return p[:, :, 0] - lam * p[:, :, 1]

def _diff_attn_prompt(q, k, v, lam):
    b, s_len = q.shape[0], q.shape[1]
    nb = s_len // Q_BLOCK
    scale = HEAD_DIM ** -0.5
    qb = q.reshape(b, nb, Q_BLOCK, N_SUB, HEAD_DIM).transpose(1, 0, 2, 3, 4)
    k_pos = jnp.arange(s_len)

    def block(args):
        q_blk, i = args
        s = jnp.einsum('bqhd,bkhd->bhqk', q_blk, k, preferred_element_type=jnp.float32) * scale
        q_pos = i * Q_BLOCK + jnp.arange(Q_BLOCK)
        s = jnp.where(k_pos[None, :] <= q_pos[:, None], s, -jnp.inf)
        a = _diff_weights(s, lam)
        return jnp.einsum('bhqk,bkhe->bqhe', a.astype(v.dtype), v,
                          preferred_element_type=jnp.float32).astype(v.dtype)

    out = lax.map(block, (qb, jnp.arange(nb)))
    return out.transpose(1, 0, 2, 3, 4).reshape(b, s_len, N_HEADS, 2 * HEAD_DIM)

def _diff_attn_sample(q, k, v, k_past, v_past, lam):
    l_new, p_len = q.shape[1], k_past.shape[1]
    scale = HEAD_DIM ** -0.5
    s_past = jnp.einsum('bqhd,bkhd->bhqk', q, k_past, preferred_element_type=jnp.float32) * scale
    s_new = jnp.einsum('bqhd,bkhd->bhqk', q, k, preferred_element_type=jnp.float32) * scale
    causal = jnp.tril(jnp.ones((l_new, l_new), dtype=bool))
    s_new = jnp.where(causal, s_new, -jnp.inf)
    a = _diff_weights(jnp.concatenate([s_past, s_new], axis=-1), lam).astype(v.dtype)
    out = (jnp.einsum('bhqk,bkhe->bqhe', a[..., :p_len], v_past, preferred_element_type=jnp.float32)
           + jnp.einsum('bhqk,bkhe->bqhe', a[..., p_len:], v, preferred_element_type=jnp.float32))
    return out.astype(v.dtype)

def _hier_moe(h, w_rg, b_rg, w_re, b_re, w_gate, w_up, w_down):
    b, l, d = h.shape
    t = h.reshape(-1, d)
    grp_prob = jax.nn.softmax((t @ w_rg + b_rg).astype(jnp.float32), axis=-1)
    g_p, g_idx = lax.top_k(grp_prob, 1)
    e_logits = (t @ w_re + b_re).astype(jnp.float32).reshape(-1, N_GROUPS, EXP_PER_GROUP)
    in_grp = jnp.take_along_axis(e_logits, g_idx[:, :, None], axis=1)[:, 0]
    e_val, e_idx = lax.top_k(in_grp, TOP_K_EXP)
    e_w = jax.nn.softmax(e_val, axis=-1) * g_p
    eid = g_idx * EXP_PER_GROUP + e_idx
    combine = jnp.sum(jax.nn.one_hot(eid, N_EXPERTS, dtype=jnp.float32) * e_w[..., None], axis=1)
    out = jnp.zeros((t.shape[0], d), jnp.float32)
    for e in range(N_EXPERTS):
        hid = jax.nn.silu(t @ w_gate[e]) * (t @ w_up[e])
        out = out + combine[:, e:e + 1] * (hid @ w_down[e]).astype(jnp.float32)
    return out.astype(h.dtype).reshape(b, l, d)

def _layer(x, c, pos, conv_prev, k_past, v_past, lam_init,
           w_ada, b_ada, ln_mix, w_in, lam_q1, lam_k1, lam_q2, lam_k2, subln_g, w_conv, w_out,
           ln_ffn, w_rg, b_rg, w_re, b_re, w_gate, w_up, w_down):
    b, l, _ = x.shape
    mod = (jax.nn.silu(c) @ w_ada + b_ada)[:, None, :]
    sh_a, sc_a, g_a, sh_f, sc_f, g_f = jnp.split(mod, 6, axis=-1)

    h = _rmsnorm(x, ln_mix) * (1 + sc_a) + sh_a
    proj = h @ w_in
    cuts = [ATTN_WIDTH, 2 * ATTN_WIDTH, 3 * ATTN_WIDTH,
            3 * ATTN_WIDTH + CONV_WIDTH, 3 * ATTN_WIDTH + 2 * CONV_WIDTH]
    q, k, v, bg, cg, u = jnp.split(proj, cuts, axis=-1)

    q = _rope(q.reshape(b, l, N_SUB, HEAD_DIM), pos)
    k = _rope(k.reshape(b, l, N_SUB, HEAD_DIM), pos)
    v = v.reshape(b, l, N_HEADS, 2 * HEAD_DIM)
    f32 = jnp.float32
    lam = (jnp.exp(jnp.sum(lam_q1.astype(f32) * lam_k1.astype(f32)))
           - jnp.exp(jnp.sum(lam_q2.astype(f32) * lam_k2.astype(f32))) + lam_init)
    if k_past is None:
        att = _diff_attn_prompt(q, k, v, lam)
    else:
        att = _diff_attn_sample(q, k, v, k_past, v_past, lam)
    att = (_rmsnorm(att, subln_g, SUBLN_EPS) * (1.0 - lam_init)).reshape(b, l, ATTN_WIDTH)

    cu = cg * u
    padded = jnp.concatenate([conv_prev.astype(cu.dtype), cu], axis=1)
    conv = lax.conv_general_dilated(padded, w_conv[:, None, :].astype(cu.dtype), window_strides=(1,),
                                    padding='VALID', dimension_numbers=('NWC', 'WIO', 'NWC'),
                                    feature_group_count=CONV_WIDTH)
    conv_out = bg * conv
    new_conv = padded[:, -(CONV_K - 1):]

    mix = jnp.concatenate([att, conv_out], axis=-1) @ w_out
    x = x + g_a * mix

    h2 = _rmsnorm(x, ln_ffn) * (1 + sc_f) + sh_f
    x = x + g_f * _hier_moe(h2, w_rg, b_rg, w_re, b_re, w_gate, w_up, w_down)
    return x, k, v, new_conv

def setup_inputs(seed: int = 0) -> dict:
    key = jax.random.key(seed)
    ks = jax.random.split(key, 32)
    f32 = jnp.float32

    def nrm(k, shape, s):
        return jax.random.normal(k, shape, f32) * s

    n_pages = PAST_LEN // PAGE_SIZE
    n_used = DEC_BATCH * n_pages
    n_phys = n_used + (n_used + 3) // 4
    page_table = jax.random.permutation(ks[5], n_phys)[:n_used].reshape(DEC_BATCH, n_pages).astype(jnp.int32)
    return {
        'x_prompt': nrm(ks[0], (BATCH, SEQ, D_MODEL), 1.0),
        'x_sample': nrm(ks[1], (DEC_BATCH, DEC_SEQ, D_MODEL), 1.0),
        'cache_k': nrm(ks[2], (DEPTH, n_phys, PAGE_SIZE, N_SUB, HEAD_DIM), 1.0),
        'cache_v': nrm(ks[3], (DEPTH, n_phys, PAGE_SIZE, N_HEADS, 2 * HEAD_DIM), 1.0),
        'state_conv': nrm(ks[4], (DEPTH, DEC_BATCH, CONV_K - 1, CONV_WIDTH), 1.0),
        'page_table': page_table,
        'c_prompt': nrm(ks[6], (BATCH, D_MODEL), 1.0),
        'c_sample': nrm(ks[7], (DEC_BATCH, D_MODEL), 1.0),
        'w_ada': nrm(ks[8], (DEPTH, D_MODEL, 6 * D_MODEL), 0.5 * D_MODEL ** -0.5),
        'b_ada': nrm(ks[9], (DEPTH, 6 * D_MODEL), 0.02),
        'ln_mix': 1.0 + nrm(ks[10], (DEPTH, D_MODEL), 0.02),
        'w_in': nrm(ks[11], (DEPTH, D_MODEL, PROJ_COLS), D_MODEL ** -0.5),
        'lam_q1': nrm(ks[12], (DEPTH, HEAD_DIM), 0.1),
        'lam_k1': nrm(ks[13], (DEPTH, HEAD_DIM), 0.1),
        'lam_q2': nrm(ks[14], (DEPTH, HEAD_DIM), 0.1),
        'lam_k2': nrm(ks[15], (DEPTH, HEAD_DIM), 0.1),
        'subln_g': 1.0 + nrm(ks[16], (DEPTH, 2 * HEAD_DIM), 0.02),
        'w_conv': nrm(ks[17], (DEPTH, CONV_K, CONV_WIDTH), CONV_K ** -0.5),
        'w_out': nrm(ks[18], (DEPTH, MIX_WIDTH, D_MODEL), MIX_WIDTH ** -0.5),
        'ln_ffn': 1.0 + nrm(ks[19], (DEPTH, D_MODEL), 0.02),
        'w_router_grp': nrm(ks[20], (DEPTH, D_MODEL, N_GROUPS), D_MODEL ** -0.5),
        'b_router_grp': nrm(ks[21], (DEPTH, N_GROUPS), 0.01),
        'w_router_exp': nrm(ks[22], (DEPTH, D_MODEL, N_EXPERTS), D_MODEL ** -0.5),
        'b_router_exp': nrm(ks[23], (DEPTH, N_EXPERTS), 0.01),
        'w_gate': nrm(ks[24], (DEPTH, N_EXPERTS, D_MODEL, D_EXPERT), D_MODEL ** -0.5),
        'w_up': nrm(ks[25], (DEPTH, N_EXPERTS, D_MODEL, D_EXPERT), D_MODEL ** -0.5),
        'w_down': nrm(ks[26], (DEPTH, N_EXPERTS, D_EXPERT, D_MODEL), D_EXPERT ** -0.5),
        'ln_final': 1.0 + nrm(ks[27], (D_MODEL,), 0.02),
    }

def reference(x_prompt, x_sample, cache_k, cache_v, state_conv, page_table, c_prompt, c_sample,
              w_ada, b_ada, ln_mix, w_in, lam_q1, lam_k1, lam_q2, lam_k2, subln_g, w_conv, w_out,
              ln_ffn, w_router_grp, b_router_grp, w_router_exp, b_router_exp, w_gate, w_up, w_down,
              ln_final):
    b_p, s_p = x_prompt.shape[0], x_prompt.shape[1]
    b_s, s_s = x_sample.shape[0], x_sample.shape[1]
    past = page_table.shape[1] * cache_k.shape[2]
    pos_p = jnp.arange(s_p, dtype=jnp.int32)
    pos_s = past + jnp.arange(s_s, dtype=jnp.int32)

    xp, xs = x_prompt, x_sample
    kp_l, vp_l, cp_l, ks_l, vs_l, cs_l = [], [], [], [], [], []
    for l in range(DEPTH):
        lam_init = 0.8 - 0.6 * math.exp(-0.3 * l)
        wl = (w_ada[l], b_ada[l], ln_mix[l], w_in[l], lam_q1[l], lam_k1[l], lam_q2[l], lam_k2[l],
              subln_g[l], w_conv[l], w_out[l], ln_ffn[l], w_router_grp[l], b_router_grp[l],
              w_router_exp[l], b_router_exp[l], w_gate[l], w_up[l], w_down[l])
        conv0 = jnp.zeros((b_p, CONV_K - 1, CONV_WIDTH), xp.dtype)
        xp, kp, vp, cp = _layer(xp, c_prompt, pos_p, conv0, None, None, lam_init, *wl)
        k_past = cache_k[l, page_table].reshape(b_s, past, N_SUB, HEAD_DIM)
        v_past = cache_v[l, page_table].reshape(b_s, past, N_HEADS, 2 * HEAD_DIM)
        xs, ksm, vsm, csm = _layer(xs, c_sample, pos_s, state_conv[l], k_past, v_past, lam_init, *wl)
        kp_l.append(kp); vp_l.append(vp); cp_l.append(cp)
        ks_l.append(ksm); vs_l.append(vsm); cs_l.append(csm)

    y_prompt = _rmsnorm(xp, ln_final)
    y_sample = _rmsnorm(xs, ln_final)
    k_prompt = jnp.stack(kp_l); v_prompt = jnp.stack(vp_l); conv_prompt = jnp.stack(cp_l)
    k_sample = jnp.stack(ks_l); v_sample = jnp.stack(vs_l); conv_sample = jnp.stack(cs_l)
    return (y_prompt, y_sample, k_prompt, v_prompt, conv_prompt, k_sample, v_sample, conv_sample)


_drawn_inputs = setup_inputs


def setup_inputs(seed=0):
    import zlib

    import numpy as np

    out = dict(_drawn_inputs(seed))
    spreads = {}
    factors = {'lam_q1': 4.039,
     'lam_q2': 8.0,
     'lam_k2': 2.991,
     'subln_g': 8.0,
     'ln_ffn': 3.622,
     'b_router_grp': 8.0,
     'b_router_exp': 8.0,
     'ln_final': 3.104}
    for name, (base, spread) in spreads.items():
        noise = np.random.default_rng([zlib.crc32(name.encode()), seed]).standard_normal(out[name].shape)
        drawn = base * np.exp(spread * noise) if base else spread * noise
        out[name] = __import__('jax').numpy.asarray(drawn.astype(out[name].dtype))
    for name, factor in factors.items():
        out[name] = (out[name] * factor).astype(out[name].dtype)
    return out
```

```python
from contextlib import ExitStack

import concourse.bass as bass
import numpy as np
from concourse import mybir

F32 = mybir.dt.float32
I32 = mybir.dt.int32
ALU = mybir.AluOpType
ACT = mybir.ActivationFunctionType
AX_X = mybir.AxisListType.X

P = 128
D = 1024
DC = D // P
SEQ = 1024
NSEQ, LNEW = 8, 4
NSAMP = NSEQ * LNEW
NT = SEQ // P + 1
TOK = SEQ + NSAMP
AW = 512
HEADS, SUBS, HD = 4, 8, 64
PAGES = 8
NG, EPG = 4, 8
NE = NG * EPG
FE = 256
FC = FE // P
MAXT = 2 * TOK // P + NE
MAXT += MAXT % 2
TCOLS = MAXT + 2
LAM_INIT = 0.2
NORM_EPS, SUBLN_EPS = 1e-6, 1e-5
SCALE = HD ** -0.5
NEG = -1e30
TB = TOK // 3
CUW = 2 + SEQ + NSEQ * (2 + LNEW)

_C = {}
_n = 0
for _name, _w in (("ident", P), ("mask", P), ("upper", P), ("iota", P), ("rope", NT * 96),
                  ("tokid", NT), ("valid", NT), ("dmask", LNEW), ("pair", 16), ("sub0", 1), ("sub1", 1),
                  ("half", 1)):
    _C[_name] = (_n, _n + _w)
    _n += _w
NCONST = _n


def constants():
    c = np.zeros((P, NCONST), np.float32)

    def put(name, v):
        a, b = _C[name]
        c[:v.shape[0], a:b] = v.reshape(v.shape[0], -1)

    i = np.arange(P)
    put("ident", np.eye(P, dtype=np.float32))
    put("mask", np.where(i[None, :] <= i[:, None], 0.0, NEG).astype(np.float32))
    put("upper", (i[:, None] < i[None, :]).astype(np.float32))
    put("iota", np.broadcast_to(i[None, :], (P, P)).astype(np.float32))
    pos = np.zeros((NT, P), np.float32)
    pos[:NT - 1] = np.arange(SEQ).reshape(NT - 1, P)
    pos[NT - 1, :NSAMP] = PAGES * P + np.arange(NSAMP) % LNEW
    exponent = (np.arange(0, HD, 2, dtype=np.float32) / np.float32(HD)).astype(np.float64)
    inv = (np.float32(1.0) / (10000.0 ** exponent).astype(np.float32)).astype(np.float32)
    ang = (pos[:, :, None] * inv[None, None, :]).astype(np.float32)
    table = np.concatenate([np.cos(ang), -np.sin(ang), np.sin(ang)], axis=-1).astype(np.float32)
    put("rope", np.ascontiguousarray(table.transpose(1, 0, 2)))
    tok = np.arange(NT)[None, :] * P + i[:, None]
    ok = tok < TOK
    put("tokid", np.where(ok, tok, 0).astype(np.float32))
    put("valid", ok.astype(np.float32))
    r = np.arange(SUBS * LNEW)
    put("dmask", np.where(np.arange(LNEW)[None, :] <= (r % LNEW)[:, None], 0.0, NEG).astype(np.float32))
    cols = np.arange(HEADS * LNEW)
    put("pair", ((r // (2 * LNEW))[:, None] * LNEW + (r % LNEW)[:, None] == cols[None, :]).astype(np.float32))
    put("sub0", ((r // LNEW) % 2 == 0).astype(np.float32)[:, None])
    put("sub1", ((r // LNEW) % 2 == 1).astype(np.float32)[:, None])
    put("half", np.full((P, 1), -0.5, np.float32))
    return c


def build(nc, consts, x_prompt, x_sample, cache_k, cache_v, state_conv, page_table, c_prompt, c_sample,
          w_ada, b_ada, ln_mix, w_in, lam_q1, lam_k1, lam_q2, lam_k2, subln_g, w_conv, w_out,
          ln_ffn, w_router_grp, b_router_grp, w_router_exp, b_router_exp, w_gate, w_up, w_down, ln_final,
          y_prompt, y_sample, k_prompt, v_prompt, conv_prompt, k_sample, v_sample, conv_sample,
          mod_dram, h2_dram, ys_dram):
    x_p = x_prompt.rearrange("b s d -> (b s) d")
    x_s = x_sample.rearrange("b s d -> (b s) d")
    kc = cache_k.rearrange("l n p h d -> (l n) p (h d)")
    vc = cache_v.rearrange("l n p h d -> (l n) p (h d)")
    y_p = y_prompt.rearrange("b s d -> (b s) d")
    y_s = y_sample.rearrange("b s d -> (b s) d")
    kp_out = k_prompt.rearrange("l b s h d -> (l b s) (h d)")
    vp_out = v_prompt.rearrange("l b s h d -> (l b s) (h d)")
    ks_out = k_sample.rearrange("l b s h d -> (l b s) (h d)")
    vs_out = v_sample.rearrange("l b s h d -> (l b s) (h d)")
    cp_out = conv_prompt.rearrange("l b s c -> (l b s) c")
    cs_out = conv_sample.rearrange("l b s c -> (l b s) c")
    w_ada_v = w_ada[0].rearrange("(c p) n -> p c n", p=P)
    w_in_v = w_in[0].rearrange("(c p) n -> p c n", p=P)
    w_out_v = w_out[0].rearrange("(c p) n -> p c n", p=P)
    gate_v = w_gate[0].rearrange("e (p c) n -> e p c n", c=DC)
    up_v = w_up[0].rearrange("e (p c) n -> e p c n", c=DC)
    down_v = w_down[0].rearrange("e (p c) n -> e p c n", c=FC)

    with ExitStack() as ctx:
        K = 1024

        def at(name, off_bytes, shape, dt=F32):
            return nc.alloc_sbuf_tensor_at(name, shape, dt, offset=BASE + off_bytes)

        BASE = -(-nc.sbuf_base // 64) * 64
        psum = ctx.enter_context(nc.psum_tensor("psum", [P, 8, 512], F32))

        def sem(name):
            return ctx.enter_context(nc.semaphore(name))

        O_AB, O_X, O_W, O_H, O_VKQ, O_MA = 8 * K, 24 * K, 60 * K, 108 * K, 141 * K, 189 * K
        cst = at("cst", 0, [P, NCONST])
        small = at("small", NCONST * 4 + 32 - (NCONST * 4) % 32, [P, 224])
        kTs = at("kTs", 6 * K + 960, [P, HEADS, NSAMP])
        qTs = at("qTs", 7 * K + 448, [P, HEADS, NSAMP])

        def C(name, rows=P):
            a, b = _C[name]
            return cst[0:rows, a:b]

        ident = C("ident")
        rope = C("rope").rearrange("p (t c) -> p t c", t=NT)
        shift_p = at("shift_p", O_AB, [P, D]); scale_p = at("scale_p", O_AB + 4 * K, [P, D])
        shift_s = at("shift_s", O_AB + 8 * K, [P, D]); scale_s = at("scale_s", O_AB + 12 * K, [P, D])
        wada = [at(f"wada{i}", O_W + 16 * K * i, [P, DC, 512]) for i in range(3)]
        cond = at("cond", O_H, [NSEQ + 1, D]); cth = at("cth", O_H + 4 * K, [NSEQ + 1, D])
        condT = at("condT", O_H + 8 * K, [P, DC, NSEQ + 1])
        mod = at("mod", O_X, [NSEQ + 1, 6 * D])
        bada = at("bada", O_VKQ, [NSEQ + 1, 6 * D])
        lnm = at("lnm", O_VKQ + 24 * K, [NSEQ + 1, D]); lnf = at("lnf", O_VKQ + 28 * K, [NSEQ + 1, D])
        lamv = at("lamv", O_VKQ + 32 * K, [P, 4, HD]); gsub = small[:, 96:224]
        wqkv = at("wqkv", O_W, [P, DC, 3 * AW])
        hT = at("hT", O_H, [P, DC, TOK])
        xin = [at(f"xin{i}", O_X + 4 * K * i, [P, D]) for i in range(2)]
        hrow = [at(f"hrow{i}", O_X + 8 * K + 4 * K * i, [P, D]) for i in range(2)]
        qrow = [at(f"qrow{i}", O_X + 16 * K + 2 * K * i, [P, AW]) for i in range(2)]
        krow = [at(f"krow{i}", O_X + 20 * K + 2 * K * i, [P, AW]) for i in range(2)]
        ropet = at("ropet", O_X + 24 * K, [P, AW]); junk = at("junk", O_X + 26 * K, [P, D])
        vs_row = at("vs_row", O_X + 30 * K, [P, AW])
        v_sb = at("v_sb", O_VKQ, [P, NT - 1, AW])
        kT = at("kT", O_VKQ + 16 * K, [P, HEADS, SEQ]); qT = at("qT", O_VKQ + 32 * K, [P, HEADS, SEQ])
        wcv = [at(f"wcv{i}", O_W + 12 * K * i, [P, DC, 3, P]) for i in range(2)]
        cg_sb = at("cg_sb", O_W + 24 * K, [P, TB]); bg_sb = at("bg_sb", O_W + 25 * K + 512, [P, TOK])
        mixC = at("mixC", O_W + 31 * K + 512, [P, 4, TOK])
        cuT = at("cuT", O_X, [P, 4, CUW])
        ctmp = at("ctmp", O_X + 17 * K, [P, TOK])
        state_sb = at("state_sb", O_X + 22 * K, [2 * NSEQ, AW]); wcvT = at("wcvT", O_X + 24 * K, [P, 4, 4])
        wconv_sb = at("wconv_sb", O_X + 25 * K, [3, AW]); ncT = at("ncT", O_X + 27 * K, [P, 4, 18])
        nc_row = at("nc_row", O_X + 28 * K, [18, AW])
        pexp = at("pexp", O_H, [P, 2, SEQ])
        pexp2 = at("pexp2", O_H + 8 * K, [P, 2, SEQ])
        adiff = at("adiff", O_H + 16 * K, [P, SEQ])
        adT = at("adT", O_H + 20 * K, [P, SEQ // P, P])
        qz = [at(f"qz{i}", O_H + 24 * K + 4 * K * i, [P, 2, HEADS, P]) for i in range(2)]
        ajunk = at("ajunk", O_H + 32 * K, [P, P])
        attrow = at("attrow", O_X + 34 * K, [P, AW])
        mixA = at("mixA", O_MA, [P, 4, TOK])
        kseq = [at(f"kseq{i}", O_W + 8 * K * i, [P, 4, AW]) for i in range(3)]
        vseq = [at(f"vseq{i}", O_X + 16 * K * i, [P, PAGES, AW]) for i in range(2)]
        vnew = [at("vnew0", O_W + 28 * K + 512, [LNEW, AW]), at("vnew1", O_X + 32 * K, [LNEW, AW])]
        qbd = at("qbd", O_W + 24 * K, [P, NSEQ, 4, 32])
        kTp = [at(f"kTp{i}", O_H + 24 * K + 2 * K * i, [P, 4, P]) for i in range(2)]
        pdec = [at(f"pdec{i}", O_H + 4 * K * i + 512 * i, [32, PAGES * P + LNEW]) for i in range(2)]
        aTs = [at(f"aTs{i}", O_H + 9 * K + 5 * K * i, [P, PAGES + 1, P]) for i in range(2)]
        snew = [at(f"snew{i}", O_H + 19 * K + 64 * i, [32, LNEW]) for i in range(2)]
        pairs = [at(f"pairs{i}", O_H + 19 * K + 128 + 64 * i, [32, 16]) for i in range(2)]
        orow = at("orow", O_H + 20 * K, [NSAMP, HEADS, P])
        pt_sb = at("pt_sb", O_W + 28 * K, [1, NSEQ * PAGES], I32)
        wout = at("wout", O_VKQ, [P, DC, D])
        wrt = at("wrt", O_VKQ + 32 * K, [P, DC, NG + NE]); brt = at("brt", O_VKQ + 34 * K, [P, NG + NE])
        logit = at("logit", O_VKQ + 35 * K, [P, NT, NG + NE])
        gate_ap = at("gate_ap", O_W, [P, D]); gate_as = at("gate_as", O_W + 4 * K, [P, D])
        x1 = at("x1", O_X, [P, NT, D])
        h2row = [at(f"h2row{i}", O_H + 4 * K * i, [P, D]) for i in range(2)]
        h2T = [at(f"h2T{i}", O_H + 8 * K + 4 * K * i, [P, DC, P]) for i in range(2)]
        ojunk = at("ojunk", O_H + 16 * K, [P, D])
        otmp = at("otmp", O_H + 31 * K, [P, 512])
        rt = at("rt", O_H, [P, 3300])
        grid = at("grid", O_W + 20 * K, [1, TCOLS * NE])
        lsel = [at(f"lsel{i}", O_W + 16 * K + 512 * i, [P, P]) for i in range(4)]
        hsel = [at(f"hsel{i}", O_W + 18 * K + 256 * i, [P, TCOLS]) for i in range(4)]
        slot_i = at("slot_i", O_VKQ + 37 * K, [P, NT, 2], I32)
        rowidx = at("rowidx", O_VKQ + 38 * K, [P, TCOLS], I32)
        plan = at("plan", O_VKQ + 39 * K, [1, TCOLS + 2], I32)
        cw = at("cw", O_VKQ + 40 * K, [P, 2, NT])
        wgu = [at(f"wgu{i}", O_W + 16 * K * i, [P, 2, DC, FE]) for i in range(2)]
        wdn = [at(f"wdn{i}", O_W + 32 * K + 8 * K * i, [P, FC, D]) for i in range(2)]
        idx1 = [at(f"idx{i}", O_VKQ + 41 * K + 32 * i, [P, 1], I32) for i in range(2)]
        xg = [at(f"xg{i}", O_H + 4 * K * i, [P, D]) for i in range(2)]
        xgT = [at(f"xgT{i}", O_H + 8 * K + 4 * K * i, [P, DC, P]) for i in range(2)]
        th = [at(f"th{i}", O_H + 16 * K + K * i, [P, FE]) for i in range(2)]
        hid = [at(f"hid{i}", O_H + 18 * K + K * i, [P, FE]) for i in range(2)]
        hidT = [at(f"hidT{i}", O_H + 20 * K + K * i, [P, FC, P]) for i in range(2)]
        gated = [at(f"gated{i}", O_H + (22, 31)[i] * K, [P, FE]) for i in range(2)]
        yrow = [at(f"yrow{i}", O_H + 23 * K + 4 * K * i, [P, D]) for i in range(2)]
        gate_fp = at("gate_fp", O_AB, [P, D]); gate_fs = at("gate_fs", O_AB + 4 * K, [P, D])
        lnfin = at("lnfin", O_AB + 8 * K, [P, D])
        yg = [[at(f"yg{i}_{k}", O_W + 8 * K * i + 4 * K * k, [P, D]) for k in range(2)] for i in range(3)]
        fin = [at(f"fin{i}", O_W + 24 * K + 4 * K * i, [P, D]) for i in range(2)]
        fjunk = at("fjunk", O_W + 32 * K, [P, D])

        ssq, rstd = small[:, 0:9], small[:, 9:18]
        neglam = small[:, 18:19]
        nm, ls, rl = small[:, 20:24], small[:, 24:28], small[:, 28:30]
        ratio = small[:, 30:31]
        r1s = [small[:, 32:36], small[:, 89:93]]
        hss, hrs, hsc = small[:, 36:40], small[:, 40:44], small[:, 44:48]
        lsum = small[:, 48:52]
        dmx, dl, dr = small[0:32, 52:57], small[0:32, 57:60], small[0:32, 60:64]
        sgn = small[0:32, 64:65]
        ss2, rs2 = small[:, 66:75], small[:, 75:84]

        R, off = {}, 0
        for name, n in (("ohs", NT * NE), ("oh1", NT * NE), ("oh2", NT * NE), ("el", NT * NE), ("ta", NT * NE), ("tb", NT * NE),
                        ("base", NT * NE), ("gm", NT), ("gs", NT * NG), ("ge", NT * NG), ("gsum", NT), ("gp", NT),
                        ("eq4", NT * NG), ("ohg", NT * NG), ("pen", NT * NG), ("mn", NT), ("m1", NT), ("m2", NT), ("dd", NT), ("ee", NT),
                        ("ws", NT), ("cnt", NE), ("nt", NE), ("inca", NE), ("incb", NE), ("first", NE), ("slot", 2 * NT),
                        ("lo", 2 * NT), ("hi", 2 * NT), ("tfl", TCOLS)):
            R[name] = rt[:, off:off + n]
            off += n
        assert off <= 3300
        ones = at("ones", O_H + 15 * K, [P, P])
        slot_lo = at("slot_lo", O_H + 14 * K, [P, 2 * NT], I32)
        slot_hi = at("slot_hi", O_H + 14 * K + 128, [P, 2 * NT], I32)

        names = """const_in cond_in bias_in wada_in0 wada_in1 wada_in2 cond_th cond_act condT_ps condT_sb ada_ps ada_sb
        mod_out mix_rows_in lam_in lam_exp lam_done wqkv_in x_in0 x_in1 ssq_done rstd_done h_done hT_ps hT_sb q_ps k_ps v_ps
        q_done k_done v_done qT_ps kT_ps qT_sb kT_sb kv_out0 kv_out1 wcv_in0 wcv_in1 state_in state_ps state_sb_s
        cv_ps cg_sb_s bg_sb_s cu_done conv_done nc_ps nc_sb nc_out pad_done ncT_done
        qz_done s_ps mask_done nmax_done exp_done ratio_done adiff_done adT_ps adT_sb o_ps ssqh_done rstdh_done att_done attT_ps attT_sb
        dscore_ps page_in kseq_in0 kseq_in1 kseq_in2 vseq_in0 vseq_in1 kp_ps kp_sb qbd_done ds_ps dnew_done dmax_done dexp_done pair_done
        da_ps da_sb do_ps oT_sb oN_ps ssqs_done rstds_done atts_done attsT_ps attsT_sb
        wout_in ffn_rows_in gate_rows_in xres_in mix_ps x1_done ssq2_done rstd2_done h2_done h2_out0 h2_out1 h2T_ps h2T_sb lg_ps lg_done
        gexp_in gexp_done wexp_in wexp_done oh_done cnt_ps sel_done map_ps plan_done
        wgu_in0 wgu_in1 wdn_in0 wdn_in1 idx_done xg_in0 xg_in1 xg_sched fill_out xgT_ps xgT_sb gu_ps th_done hid_done hidT_ps hidT_sb y_ps y_done y_out0 y_out1
        fin_rows_in yg_in0 yg_in1 yg_in2 comb_done ssq3_done rstd3_done fin_done fin_out0 fin_out1
        dve_step act_step pool_step m_dve_step""".split()
        S = {n: sem(n) for n in names}

        block = ctx.enter_context(nc.Block())

        def rows(t):
            return P if t < NT - 1 else NSAMP

        def mixT(c, lo, n):
            return (mixA if c < 4 else mixC)[:, c % 4, lo:lo + n]

        MOD = {"shift_a": 0, "scale_a": 1, "gate_a": 2, "shift_f": 3, "scale_f": 4, "gate_f": 5}

        def load_mod(eng, name, dst_p, dst_s, s):
            a = MOD[name] * D
            eng.dma_start(dst_p[:, :], mod_dram[0, a:a + D].partition_broadcast(P)).then_inc(s, 16)
            for i in range(NSEQ):
                eng.dma_start(dst_s[LNEW * i:LNEW * i + LNEW, :],
                              mod_dram[1 + i, a:a + D].partition_broadcast(LNEW)).then_inc(s, 16)

        ROWSEMS = 16 * (1 + NSEQ)
        W = S

        @block.sync
        def _(sp):
            sp.dma_start(cst[:, :], consts).then_inc(S["const_in"], 16)
            sp.dma_start(cond[0:1, :], c_prompt).then_inc(S["cond_in"], 16)
            sp.dma_start(cond[1:NSEQ + 1, :], c_sample).then_inc(S["cond_in"], 16)
            for b in range(12):
                if b >= 3:
                    sp.wait_ge(W["ada_ps"], b - 2)
                sp.dma_start(wada[b % 3][:, :, :], w_ada_v[:, :, 512 * b:512 * b + 512]).then_inc(S[f"wada_in{b % 3}"], 16)
                if b == 0:
                    sp.dma_start(bada[:, :], b_ada[0].partition_broadcast(NSEQ + 1)).then_inc(S["bias_in"], 16)
                    sp.dma_start(lnm[:, :], ln_mix[0].partition_broadcast(NSEQ + 1)).then_inc(S["bias_in"], 16)
                    sp.dma_start(lnf[:, :], ln_ffn[0].partition_broadcast(NSEQ + 1)).then_inc(S["bias_in"], 16)
                    for i, v in enumerate((lam_q1, lam_k1, lam_q2, lam_k2)):
                        sp.dma_start(lamv[:, i, :], v[0].partition_broadcast(P)).then_inc(S["lam_in"], 16)
                    sp.dma_start(gsub, subln_g[0].partition_broadcast(P)).then_inc(S["lam_in"], 16)
            sp.wait_ge(W["ada_ps"], 12)
            sp.dma_start(wqkv[:, :, :], w_in_v[:, :, 0:3 * AW]).then_inc(S["wqkv_in"], 16)
            sp.wait_ge(W["mod_out"], 16)
            load_mod(sp, "shift_a", shift_p, shift_s, S["mix_rows_in"])
            load_mod(sp, "scale_a", scale_p, scale_s, S["mix_rows_in"])
            for t in range(NT):
                if t >= 2:
                    sp.wait_ge(W["h_done"], t - 1)
                src = x_p[P * t:P * t + P, :] if t < NT - 1 else x_s
                sp.dma_start(xin[t % 2][0:rows(t), :], src).then_inc(S[f"x_in{t % 2}"], 16)
            sp.wait_ge(W["v_ps"], NT)
            for i in range(4):
                if i >= 2:
                    sp.wait_ge(W["cv_ps"], 3 * (i - 1))
                for j in range(3):
                    a = 3 * AW + j * AW + P * i
                    sp.dma_start(wcv[i % 2][:, :, j, :], w_in_v[:, :, a:a + P]).then_inc(S[f"wcv_in{i % 2}"], 16)
                if i == 0:
                    sp.wait_ge(W["kT_ps"], NT)
                    sp.wait_ge(W["kv_out0"], 32 * 5)
                    sp.wait_ge(W["kv_out1"], 32 * 4)
                    sp.wait_ge(W["rstd_done"], NT)
                    sp.dma_start(state_sb[:, :], state_conv.rearrange("l b s c -> (l b s) c")).then_inc(S["state_in"], 16)
                    sp.dma_start(wconv_sb[:, :], w_conv[0]).then_inc(S["state_in"], 16)
            sp.wait_ge(W["cv_ps"], 12)
            sp.wait_ge(W["conv_done"], 8)
            sp.dma_start(pt_sb[:, :], page_table.rearrange("b n -> (b n)").rearrange("(a n) -> a n", a=1)).then_inc(S["page_in"], 16)
            sp.wait_ge(W["page_in"], 16)
            sp.wait_ge(W["nc_out"], 32)
            for s in range(NSEQ):
                if s >= 2:
                    sp.wait_ge(W["do_ps"], s - 1)
                for g in range(2):
                    n = 2 * s + g
                    if n >= 3:
                        sp.wait_ge(W["kp_ps"], 4 * (n - 2))
                    for j in range(4):
                        p = 4 * g + j
                        page = sp.value_load(pt_sb[0:1, s * PAGES + p:s * PAGES + p + 1], min_val=0, max_val=kc.shape[0] - 1)
                        sp.dma_start(kseq[n % 3][:, j, :], kc[bass.ds(page, 1)].rearrange("o p c -> p (o c)")).then_inc(S[f"kseq_in{n % 3}"], 16)
                        sp.dma_start(vseq[s % 2][:, p, :], vc[bass.ds(page, 1)].rearrange("o p c -> p (o c)")).then_inc(S[f"vseq_in{s % 2}"], 16)
                sp.dma_start(vnew[s % 2][:, :], vs_out[LNEW * s:LNEW * s + LNEW, :]).then_inc(S[f"vseq_in{s % 2}"], 16)
            sp.wait_ge(W["o_ps"], 32)
            sp.dma_start(wout[:, :, :], w_out_v).then_inc(S["wout_in"], 16)
            sp.dma_start(wrt[:, :, 0:NG], w_router_grp[0].rearrange("(c p) n -> p c n", p=P)).then_inc(S["wout_in"], 16)
            sp.dma_start(wrt[:, :, NG:NG + NE], w_router_exp[0].rearrange("(c p) n -> p c n", p=P)).then_inc(S["wout_in"], 16)
            sp.dma_start(brt[:, 0:NG], b_router_grp[0].partition_broadcast(P)).then_inc(S["wout_in"], 16)
            sp.dma_start(brt[:, NG:NG + NE], b_router_exp[0].partition_broadcast(P)).then_inc(S["wout_in"], 16)
            load_mod(sp, "shift_f", shift_p, shift_s, S["ffn_rows_in"])
            load_mod(sp, "scale_f", scale_p, scale_s, S["ffn_rows_in"])
            sp.wait_ge(W["kp_ps"], 64)
            load_mod(sp, "gate_a", gate_ap, gate_as, S["gate_rows_in"])
            sp.wait_ge(W["do_ps"], NSEQ)
            for t in range(NT):
                if t == NT - 1:
                    sp.wait_ge(W["attsT_ps"], 1)
                src = x_p[P * t:P * t + P, :] if t < NT - 1 else x_s
                sp.dma_start(x1[0:rows(t), t, :], src).then_inc(S["xres_in"], 16)
            sp.wait_ge(W["h2_done"], NT)
            load_mod(sp, "gate_f", gate_fp, gate_fs, S["fin_rows_in"])
            sp.dma_start(lnfin[:, :], ln_final.partition_broadcast(P)).then_inc(S["fin_rows_in"], 16)
            sp.wait_ge(W["plan_done"], 3)
            npair = sp.value_load(plan[0:1, TCOLS:TCOLS + 1], min_val=1, max_val=MAXT // 2)
            with sp.Fori(0, npair) as i:
                for b in range(2):
                    e = sp.value_load(plan[0:1, bass.ds(2 * i + b, 1)], min_val=0, max_val=NE - 1)
                    sp.wait_ge(W["gu_ps"], 2 * i + b + 1)
                    sp.dma_start(wgu[b][:, 0, :, :], gate_v[bass.ds(e, 1)].rearrange("o p c n -> p (o c) n")).then_inc(S[f"wgu_in{b}"], 16)
                    sp.dma_start(wgu[b][:, 1, :, :], up_v[bass.ds(e, 1)].rearrange("o p c n -> p (o c) n")).then_inc(S[f"wgu_in{b}"], 16)
                    sp.wait_ge(W["y_ps"], 2 * i + b + 1)
                    sp.dma_start(wdn[b][:, :, :], down_v[bass.ds(e, 1)].rearrange("o p c n -> p (o c) n")).then_inc(S[f"wdn_in{b}"], 16)
            for t in range(NT):
                sp.wait_ge(W["fin_done"], t + 1)
                dst = y_p[P * t:P * t + P, :] if t < NT - 1 else y_s
                sp.dma_start(dst, fin[t % 2][0:rows(t), :]).then_inc(S[f"fin_out{t % 2}"], 16)
            sp.wait_ge(W["fin_out0"], 16 * 5)
            sp.wait_ge(W["fin_out1"], 16 * 4)
            sp.wait_ge(W["kv_out0"], 32 * 5)
            sp.wait_ge(W["kv_out1"], 32 * 4)
            sp.wait_ge(W["nc_out"], 32)

        def bank(b, n=512, rows_=P):
            return psum[0:rows_, b, 0:n]

        def page_scores(pe, s, p):
            n = s * PAGES + p
            pe.wait_ge(W["kp_sb"], n + 1)
            if p == 0 and s >= 2:
                pe.wait_ge(W["dexp_done"], 2 * s - 2)
            for c in range(4):
                last = nc.tensor.matmul(psum[0:32, 2 * (s % 2) + p // 4, P * (p % 4):P * (p % 4) + P], qbd[:, s, c, :], kTp[n % 2][:, c, :],
                                        start=(c == 0), stop=(c == 3))
            last.then_inc(S["dscore_ps"], 1)

        @block.tensor
        def _(pe):
            mm, tr = nc.tensor.matmul, nc.tensor.transpose
            pe.sem_inc(S["gu_ps"], 2)
            pe.sem_inc(S["y_ps"], 2)
            pe.sem_inc(S["xgT_ps"], 2)

            pe.wait_ge(W["const_in"], 16)
            pe.wait_ge(W["cond_act"], 1)
            cT = bank(7, DC * 9).rearrange("p (c s) -> p c s", c=DC)
            for c in range(DC):
                last = tr(cT[:, c, :], cond[:, P * c:P * c + P], ident[0:9, 0:9])
            last.then_inc(S["condT_ps"], 1)
            pe.wait_ge(W["condT_sb"], 1)
            for b in range(12):
                pe.wait_ge(W[f"wada_in{b % 3}"], 16 * (b // 3 + 1))
                if b >= 2:
                    pe.wait_ge(W["ada_sb"], b - 1)
                for c in range(DC):
                    last = mm(psum[0:9, b % 2, :], condT[:, c, :], wada[b % 3][:, c, :], start=(c == 0), stop=(c == DC - 1))
                last.then_inc(S["ada_ps"], 1)

            def x_transposes(t):
                pe.wait_ge(W["h_done"], t + 1)
                if t >= 1:
                    pe.wait_ge(W["hT_sb"], t)
                n = rows(t)
                for c in range(DC):
                    last = tr(psum[:, c // 4, P * (c % 4):P * (c % 4) + n], hrow[t % 2][0:n, P * c:P * c + P], ident[0:n, 0:n])
                last.then_inc(S["hT_ps"], 1)

            def qk_transposes(t):
                n = rows(t)
                for name, src, b in (("q", qrow, 5), ("k", krow, 6)):
                    pe.wait_ge(W[f"{name}_done"], t + 1)
                    if t >= 1:
                        pe.wait_ge(W[f"{name}T_sb"], t)
                    for h in range(HEADS):
                        last = tr(psum[:, b, P * h:P * h + n], src[t % 2][0:n, P * h:P * h + P], ident[0:n, 0:n])
                    last.then_inc(S[f"{name}T_ps"], 1)

            x_transposes(0)
            pe.wait_ge(W["wqkv_in"], 16)
            for t in range(NT):
                n = rows(t)
                if t + 1 < NT:
                    x_transposes(t + 1)
                pe.wait_ge(W["hT_sb"], t + 1)
                for j, name in enumerate(("q", "k", "v")):
                    if t >= 1:
                        pe.wait_ge(W[f"{name}_done"], t)
                    for c in range(DC):
                        last = mm(psum[0:n, 2 + j, :], hT[:, c, P * t:P * t + n], wqkv[:, c, AW * j:AW * j + AW],
                                  start=(c == 0), stop=(c == DC - 1))
                    last.then_inc(S[f"{name}_ps"], 1)
                if t >= 1:
                    qk_transposes(t - 1)
            qk_transposes(NT - 1)

            pe.wait_ge(W["state_in"], 32)
            pe.wait_ge(W["qT_sb"], NT)
            pe.wait_ge(W["kT_sb"], NT)
            for i in range(4):
                tr(psum[:, 6, 16 * i:16 * i + 16], state_sb[:, P * i:P * i + P], ident[0:16, 0:16])
                last = tr(psum[:, 6, 64 + 4 * i:64 + 4 * i + 3], wconv_sb[:, P * i:P * i + P], ident[0:3, 0:3])
            last.then_inc(S["state_ps"], 1)
            pe.wait_ge(W["v_done"], NT)
            pe.wait_ge(W["k_done"], NT)
            for i in range(4):
                pe.wait_ge(W[f"wcv_in{i % 2}"], 48 * (i // 2 + 1))
                for tb in range(3):
                    n = 3 * i + tb
                    if n >= 2:
                        pe.wait_ge(W["cu_done"], n - 1)
                        pe.wait_ge(W["bg_sb_s"], n - 1)
                    for j in (1, 2, 0):
                        for c in range(DC):
                            last = mm(psum[:, 3 * (n % 2) + j, 0:TB], wcv[i % 2][:, c, j, :], hT[:, c, TB * tb:TB * tb + TB],
                                      start=(c == 0), stop=(c == DC - 1))
                    last.then_inc(S["cv_ps"], 1)
            pe.wait_ge(W["ncT_done"], 1)
            for i in range(4):
                last = tr(psum[0:18, 7, P * i:P * i + P], ncT[:, i, :], ident)
            last.then_inc(S["nc_ps"], 1)

            def scores(w, u):
                i, h = divmod(w, HEADS)
                if w == 0 and u == 0:
                    pe.wait_ge(W["qz_done"], 1)
                elif h == 0 and u == 0:
                    pe.wait_ge(W["qz_done"], i + 1)
                if w >= 1:
                    pe.wait_ge(W["exp_done"], 2 * w + u - 1)
                nk = P * (i + 1)
                for a in range(0, nk, 512):
                    b = min(nk, a + 512)
                    last = mm(psum[:, 2 * u + a // 512, 0:b - a], qz[i % 2][:, u, h, :], kT[:, h, a:b], start=True, stop=True)
                last.then_inc(S["s_ps"], 1)

            def weighted_values(w):
                i, h = divmod(w, HEADS)
                pe.wait_ge(W["adT_sb"], w + 1)
                if h == 0 and i >= 2:
                    pe.wait_ge(W["attT_sb"], i - 1)
                for kt in range(i + 1):
                    last = mm(psum[:, 6 + i % 2, P * h:P * h + P], adT[:, kt, :], v_sb[:, kt, P * h:P * h + P], start=(kt == 0), stop=(kt == i))
                last.then_inc(S["o_ps"], 1)

            def att_transposes(i):
                pe.wait_ge(W["att_done"], i + 1)
                for h in range(HEADS):
                    last = tr(psum[:, 6 + i % 2, P * h:P * h + P], attrow[:, P * h:P * h + P], ident)
                last.then_inc(S["attT_ps"], 1)

            pe.wait_ge(W["cu_done"], 12)
            pe.wait_ge(W["bg_sb_s"], 12)
            pe.wait_ge(W["nc_sb"], 1)
            pe.wait_ge(W["state_sb_s"], 2)
            pe.wait_ge(W["v_done"], NT)
            pe.wait_ge(W["kT_sb"], NT)
            scores(0, 0)
            scores(0, 1)
            for w in range(8 * HEADS):
                i, h = divmod(w, HEADS)
                if w + 1 < 8 * HEADS:
                    scores(w + 1, 0)
                    scores(w + 1, 1)
                if w >= 1:
                    weighted_values(w - 1)
                if h == 3 and i >= 1:
                    att_transposes(i - 1)
                pe.wait_ge(W["adiff_done"], w + 1)
                for kt in range(i + 1):
                    last = tr(psum[:, 4 + kt // 4, P * (kt % 4):P * (kt % 4) + P], adiff[:, P * kt:P * kt + P], ident)
                last.then_inc(S["adT_ps"], 1)
            weighted_values(8 * HEADS - 1)
            att_transposes(7)

            def sample_values(s):
                pe.wait_ge(W["pair_done"], s + 1)
                pe.wait_ge(W["dnew_done"], min(s + 2, NSEQ))
                for p in range(PAGES + 1):
                    m = P if p < PAGES else LNEW
                    last = mm(psum[0:m, 7, 16 * p:16 * p + 16], pdec[s % 2][:, P * p:P * p + m], pairs[s % 2][:, :], start=True, stop=True)
                last.then_inc(S["da_ps"], 1)
                pe.wait_ge(W["da_sb"], s + 1)
                pe.wait_ge(W[f"vseq_in{s % 2}"], 16 * (PAGES + 1) * (s // 2 + 1))
                for p in range(PAGES + 1):
                    if p < PAGES:
                        last = mm(psum[:, 6, :], aTs[s % 2][:, p, :], vseq[s % 2][:, p, :], start=(s == 0 and p == 0), stop=False)
                    else:
                        last = mm(psum[:, 6, :], aTs[s % 2][0:LNEW, p, :], vnew[s % 2][:, :], start=False, stop=(s == NSEQ - 1))
                last.then_inc(S["do_ps"], 1)

            pe.wait_ge(W["qbd_done"], 1)
            pe.wait_ge(W["attT_sb"], 8)
            for s in range(NSEQ):
                for p in range(PAGES):
                    n = s * PAGES + p
                    half = n // 4
                    pe.wait_ge(W[f"kseq_in{half % 3}"], 64 * (half // 3 + 1))
                    if n >= 2:
                        pe.wait_ge(W["kp_sb"], n - 1)
                    for c in range(4):
                        last = tr(psum[:, 4 + n % 2, P * c:P * c + P], kseq[half % 3][:, p % 4, P * c:P * c + P], ident)
                    last.then_inc(S["kp_ps"], 1)
                    if p >= 1:
                        page_scores(pe, s, p - 1)
                page_scores(pe, s, PAGES - 1)
                if s >= 2:
                    pe.wait_ge(W["da_sb"], s - 1)
                for c in range(4):
                    last = mm(psum[0:32, 7, 256:256 + LNEW], qbd[:, s, c, :], kTs[:, c, LNEW * s:LNEW * s + LNEW], start=(c == 0), stop=(c == 3))
                last.then_inc(S["ds_ps"], 1)
                if s >= 1:
                    sample_values(s - 1)
            sample_values(NSEQ - 1)
            pe.wait_ge(W["atts_done"], 1)
            for h in range(HEADS):
                last = tr(psum[:, 5, NSAMP * h:NSAMP * h + NSAMP], attrow[0:NSAMP, P * h:P * h + P], ident[0:NSAMP, 0:NSAMP])
            last.then_inc(S["attsT_ps"], 1)
            pe.wait_ge(W["attsT_sb"], 1)

            def router(t):
                n = rows(t)
                pe.wait_ge(W["h2_done"], t + 1)
                if t >= 1:
                    pe.wait_ge(W["h2T_sb"], t)
                for c in range(DC):
                    last = tr(psum[:, 4 + c // 4, P * (c % 4):P * (c % 4) + n], h2row[t % 2][0:n, P * c:P * c + P], ident[0:n, 0:n])
                last.then_inc(S["h2T_ps"], 1)

            def logits_of(t):
                n = rows(t)
                pe.wait_ge(W["h2T_sb"], t + 1)
                if t >= 1:
                    pe.wait_ge(W["lg_done"], t)
                for c in range(DC):
                    last = mm(psum[0:n, 6, 0:NG + NE], h2T[t % 2][:, c, 0:n], wrt[:, c, :], start=(c == 0), stop=(c == DC - 1))
                last.then_inc(S["lg_ps"], 1)

            pe.wait_ge(W["wout_in"], 16 * 5)
            for t in range(NT):
                n = rows(t)
                for j in range(2):
                    b = 2 * (t % 2) + j
                    if t >= 2:
                        pe.wait_ge(W["x1_done"], 2 * (t - 1))
                    for c in range(DC):
                        last = mm(psum[0:n, b, :], mixT(c, P * t, n), wout[:, c, 512 * j:512 * j + 512], start=(c == 0), stop=(c == DC - 1))
                    last.then_inc(S["mix_ps"], 1)
                if t >= 1:
                    router(t - 1)
                if t >= 2:
                    logits_of(t - 2)
            router(NT - 1)
            logits_of(NT - 2)
            logits_of(NT - 1)

            pe.wait_ge(W["oh_done"], 1)
            pe.wait_ge(W["x1_done"], 2 * NT)
            ohs = R["ohs"]
            mm(psum[:, 0, 0:NT * NE], C("upper"), ohs, start=True, stop=True)
            mm(psum[:, 1, 0:NT * NE], ones[:, :], ohs, start=True, stop=True).then_inc(S["cnt_ps"], 1)
            for n in range(2 * NT):
                pe.wait_ge(W["sel_done"], n + 1)
                last = mm(psum[:, 2, 0:TCOLS], lsel[n % 4][:, :], hsel[n % 4][:, :], start=(n == 0), stop=(n == 2 * NT - 1))
                last.then_inc(S["map_ps"], 1)

            pe.wait_ge(W["plan_done"], 3)
            npair = pe.value_load(plan[0:1, TCOLS:TCOLS + 1], min_val=1, max_val=MAXT // 2)

            def gather_transposes(b):
                for c in range(DC):
                    last = tr(psum[:, c // 4, P * (c % 4):P * (c % 4) + P], xg[b][:, c:D:DC], ident)
                last.then_inc(S["xgT_ps"], 1)

            pe.wait_ge(W["xg_in0"], 16)
            gather_transposes(0)
            pe.wait_ge(W["xg_in1"], 16)
            pe.wait_ge(W["xgT_sb"], 1)
            gather_transposes(1)
            with pe.Fori(0, npair) as i:
                for b in range(2):
                    j = 2 * i + b
                    pe.wait_ge(W["xgT_sb"], j + 1)
                    pe.wait_ge(W[f"wgu_in{b}"], 32 * i + 32)
                    pe.wait_ge(W["hid_done"], j + 1)
                    for c in range(DC):
                        last = mm(psum[:, 2 + b, :].rearrange("p (g n) -> p g n", g=2), xgT[b][:, c, :], wgu[b][:, :, c, :],
                                  start=(c == 0), stop=(c == DC - 1))
                    last.then_inc(S["gu_ps"], 1)
                for b in range(2):
                    j = 2 * i + b
                    pe.wait_ge(W["hid_done"], j + 3)
                    pe.wait_ge(W["hidT_sb"], j + 2)
                    for c in range(FC):
                        last = tr(psum[:, 4, P * c:P * c + P], hid[b][:, c:FE:FC], ident)
                    last.then_inc(S["hidT_ps"], 1)
                    pe.wait_ge(W["hidT_sb"], j + 3)
                    pe.wait_ge(W[f"wdn_in{b}"], 16 * i + 16)
                    pe.wait_ge(W["y_done"], j + 2)
                    for n in range(2):
                        for c in range(FC):
                            last = mm(psum[:, 5 + n, :], hidT[b][:, c, :], wdn[b][:, c, 512 * n:512 * n + 512],
                                      start=(c == 0), stop=(c == FC - 1))
                    last.then_inc(S["y_ps"], 1)
                    pe.wait_ge(W[f"xg_in{b}"], 16 * i + 32)
                    pe.wait_ge(W["xgT_sb"], j + 2)
                    gather_transposes(b)

        def bc(ap, shape, axes):
            for a in axes:
                ap = ap.unsqueeze(a)
            return ap.to_broadcast(shape)

        @block.scalar
        def _(act):
            A = nc.scalar.activation
            steps = [0]

            def link(ins):
                steps[0] += 1
                ins.then_inc(S["act_step"], 1)
                act.wait_ge(S["act_step"], steps[0])

            act.sem_inc(S["y_out0"], 16)
            act.sem_inc(S["y_out1"], 16)
            act.wait_ge(W["cond_in"], 32)
            A(cth[:, :], cond[:, :], ACT.Tanh, scale=0.5).then_inc(S["cond_th"], 1)
            act.wait_ge(W["lam_done"], 1)
            A(small[:, 85:87], small[:, 87:89], ACT.Exp).then_inc(S["lam_exp"], 1)

            def squares(t):
                n = rows(t)
                act.wait_ge(W[f"x_in{t % 2}"], 16 * (t // 2 + 1))
                if t >= 1:
                    act.wait_ge(W["ssq_done"], t)
                A(junk[0:n, :], xin[t % 2][0:n, :], ACT.Square, accum_out=ssq[0:n, t:t + 1]).then_inc(S["ssq_done"], 1)

            def copy_hT(t):
                n = rows(t)
                act.wait_ge(W["hT_ps"], t + 1)
                nc.scalar.copy(hT[:, :, P * t:P * t + n], psum[:, 0:2, :].rearrange("p b (c n) -> p (b c) n", c=4)[:, :, 0:n]).then_inc(S["hT_sb"], 1)

            act.wait_ge(W["mod_out"], 16)
            squares(0)
            copy_hT(0)
            for t in range(NT):
                n = rows(t)
                if t + 1 < NT:
                    squares(t + 1)
                    copy_hT(t + 1)
                act.wait_ge(W["v_ps"], t + 1)
                dst = v_sb[:, t, :] if t < NT - 1 else vs_row[0:n, :]
                nc.scalar.copy(dst, psum[0:n, 4, :]).then_inc(S["v_done"], 1)
                for u in ([t - 1] if t >= 1 else []) + ([t] if t == NT - 1 else []):
                    m = rows(u)
                    for name, dst, dst_s, b in (("q", qT, qTs, 5), ("k", kT, kTs, 6)):
                        act.wait_ge(W[f"{name}T_ps"], u + 1)
                        to = dst[:, :, P * u:P * u + P] if u < NT - 1 else dst_s[:, :, :]
                        nc.scalar.mul(to, psum[:, b, :].rearrange("p (h n) -> p h n", h=HEADS)[:, :, 0:m],
                                      SCALE if name == "q" else 1.0).then_inc(S[f"{name}T_sb"], 1)

            for i in range(4):
                for tb in range(3):
                    n = 3 * i + tb
                    act.wait_ge(W["cv_ps"], n + 1)
                    if n >= 1:
                        act.wait_ge(W["cu_done"], n)
                    nc.scalar.copy(cg_sb[:, :], psum[:, 3 * (n % 2) + 1, 0:TB]).then_inc(S["cg_sb_s"], 1)
                    if tb == 0 and i >= 1:
                        act.wait_ge(W["conv_done"], 2 * i)
                    nc.scalar.copy(bg_sb[:, TB * tb:TB * tb + TB], psum[:, 3 * (n % 2), 0:TB]).then_inc(S["bg_sb_s"], 1)
            act.wait_ge(W["nc_ps"], 1)
            nc.scalar.copy(nc_row[:, :], psum[0:18, 7, :]).then_inc(S["nc_sb"], 1)

            pe2 = [pexp, pexp2]

            def exps(w, u):
                nk = P * (w // HEADS + 1)
                act.wait_ge(W["nmax_done"], 2 * w + u + 1)
                if w >= 2:
                    act.wait_ge(W["adiff_done"], w - 1)
                src = psum[:, 2 * u:2 * u + 2, :].rearrange("p b n -> p (b n)")[:, 0:nk]
                k = 2 * (w % 2) + u
                A(pe2[w % 2][:, u, 0:nk], src, ACT.Exp, bias=nm[:, k:k + 1], accum_out=ls[:, k:k + 1]).then_inc(S["exp_done"], 1)

            def head_squares(i):
                act.wait_ge(W["o_ps"], 4 * i + 4)
                if i >= 1:
                    act.wait_ge(W["att_done"], i)
                for h in range(HEADS):
                    if h or i:
                        act.wait_ge(W["ssqh_done"], 4 * i + h)
                    A(ajunk[:, 0:P], psum[:, 6 + i % 2, P * h:P * h + P], ACT.Square, scale=r1s[i % 2][:, h:h + 1],
                      accum_out=hss[:, h:h + 1]).then_inc(S["ssqh_done"], 1)

            def copy_attT(i):
                act.wait_ge(W["attT_ps"], i + 1)
                nc.scalar.copy(mixA[:, :, P * i:P * i + P], psum[:, 6 + i % 2, :].rearrange("p (h n) -> p h n", h=HEADS)).then_inc(S["attT_sb"], 1)

            act.wait_ge(W["cv_ps"], 12)
            exps(0, 0)
            exps(0, 1)
            for w in range(8 * HEADS):
                i, h = divmod(w, HEADS)
                if w + 1 < 8 * HEADS:
                    exps(w + 1, 0)
                act.wait_ge(W["adT_ps"], w + 1)
                nc.scalar.copy(adT[:, 0:i + 1, :], psum[:, 4:6, :].rearrange("p b (c n) -> p (b c) n", c=4)[:, 0:i + 1, :]).then_inc(S["adT_sb"], 1)
                if w + 1 < 8 * HEADS:
                    exps(w + 1, 1)
                if h == 1 and i >= 1:
                    head_squares(i - 1)
                if h == 3 and i >= 1:
                    copy_attT(i - 1)
            head_squares(7)
            copy_attT(7)

            for s in range(NSEQ):
                for p in range(PAGES):
                    n = s * PAGES + p
                    act.wait_ge(W["kp_ps"], n + 1)
                    if n >= 2:
                        act.wait_ge(W["dscore_ps"], n - 1)
                    nc.scalar.copy(kTp[n % 2][:, :, :], psum[:, 4 + n % 2, :].rearrange("p (c n) -> p c n", c=4)).then_inc(S["kp_sb"], 1)
                act.wait_ge(W["dmax_done"], s + 1)
                if s >= 2:
                    act.wait_ge(W["da_ps"], s - 1)
                b, m = s % 2, dmx[:, 3 + s % 2:4 + s % 2]
                A(pdec[b][:, 0:PAGES * P], psum[0:32, 2 * b:2 * b + 2, :].rearrange("p b n -> p (b n)"), ACT.Exp, bias=m,
                  accum_out=dl[:, 0:1]).then_inc(S["dexp_done"], 1)
                A(pdec[b][:, PAGES * P:], snew[b][:, :], ACT.Exp, bias=m, accum_out=dl[:, 1:2]).then_inc(S["dexp_done"], 1)
            act.wait_ge(W["do_ps"], NSEQ)
            for h in range(HEADS):
                nc.scalar.copy(orow[:, h, :], psum[32 * h:32 * h + 32, 6, P * h:P * h + P]).then_inc(S["oT_sb"], 1)
            act.wait_ge(W["oT_sb"], 4)
            for h in range(HEADS):
                if h:
                    act.wait_ge(W["ssqs_done"], h)
                A(ajunk[0:NSAMP, 0:P], orow[:, h, :], ACT.Square, accum_out=hss[0:NSAMP, h:h + 1]).then_inc(S["ssqs_done"], 1)
            act.wait_ge(W["attsT_ps"], 1)
            nc.scalar.copy(mixA[:, :, SEQ:TOK], psum[:, 5, 0:HEADS * NSAMP].rearrange("p (h n) -> p h n", h=HEADS)).then_inc(S["attsT_sb"], 1)

            def copy_h2T(t):
                n = rows(t)
                act.wait_ge(W["h2T_ps"], t + 1)
                if t >= 2:
                    act.wait_ge(W["lg_ps"], t - 1)
                nc.scalar.copy(h2T[t % 2][:, :, 0:n], psum[:, 4:6, :].rearrange("p b (c n) -> p (b c) n", c=4)[:, :, 0:n]).then_inc(S["h2T_sb"], 1)

            for t in range(NT):
                n = rows(t)
                if t >= 1:
                    copy_h2T(t - 1)
                act.wait_ge(W["x1_done"], 2 * t + 2)
                if t >= 1:
                    act.wait_ge(W["ssq2_done"], t)
                A(ojunk[0:n, :], x1[0:n, t, :], ACT.Square, accum_out=ss2[0:n, t:t + 1]).then_inc(S["ssq2_done"], 1)
            copy_h2T(NT - 1)

            act.wait_ge(W["gexp_in"], 1)
            A(R["ge"], R["gs"], ACT.Exp).then_inc(S["gexp_done"], 1)
            act.wait_ge(W["wexp_in"], 1)
            A(R["ee"], R["dd"], ACT.Exp).then_inc(S["wexp_done"], 1)

            act.wait_ge(W["plan_done"], 3)
            npair = act.value_load(plan[0:1, TCOLS:TCOLS + 1], min_val=1, max_val=MAXT // 2)

            with act.Fori(npair, MAXT // 2 + 1) as i:
                act.dma_start(ys_dram[bass.ds(i * 2 * P, 2 * P), :].rearrange("(a p) d -> p a d", p=P), x1[:, 0:2, :]).then_inc(S["fill_out"], 16)

            def copy_xgT(b):
                nc.scalar.copy(xgT[b][:, :, :], psum[:, 0:2, :].rearrange("p b (c n) -> p (b c) n", c=4)).then_inc(S["xgT_sb"], 1)

            act.wait_ge(W["xgT_ps"], 3)
            copy_xgT(0)
            act.wait_ge(W["xgT_ps"], 4)
            copy_xgT(1)
            with act.Fori(0, npair) as i:
                act.sem_inc(S["fill_out"], 16)
                for b in range(2):
                    j = 2 * i + b
                    act.wait_ge(W["gu_ps"], j + 3)
                    A(th[b][:, :], psum[:, 2 + b, 0:FE], ACT.Tanh, scale=0.5).then_inc(S["th_done"], 1)
                for b in range(2):
                    j = 2 * i + b
                    act.wait_ge(W["xgT_ps"], j + 5)
                    copy_xgT(b)
                    act.wait_ge(W["y_done"], j + 3)
                    act.dma_start(ys_dram[bass.ds(j * P, P), :], yrow[b][:, :]).then_inc(S[f"y_out{b}"], 16)

            for t in range(NT):
                n = rows(t)
                act.wait_ge(W["comb_done"], t + 1)
                if t >= 1:
                    act.wait_ge(W["ssq3_done"], t)
                A(fjunk[0:n, :], x1[0:n, t, :], ACT.Square, accum_out=ss2[0:n, t:t + 1]).then_inc(S["ssq3_done"], 1)

        @block.vector
        def _(dve):
            TT, TS, STT = nc.vector.tensor_tensor, nc.vector.tensor_scalar, nc.vector.scalar_tensor_tensor
            RED = nc.vector.tensor_reduce
            steps = [0]

            def link(ins):
                steps[0] += 1
                ins.then_inc(S["dve_step"], 1)
                dve.wait_ge(S["dve_step"], steps[0])

            dve.sem_inc(S["hid_done"], 2)
            dve.sem_inc(S["hidT_sb"], 2)
            dve.sem_inc(S["y_done"], 2)
            dve.wait_ge(W["cond_th"], 1)
            STT(cond[:, :], cth[:, :], 1.0, cond[:, :], ALU.add, ALU.mult).then_inc(S["cond_act"], 1)
            dve.wait_ge(W["lam_in"], 80)
            l4 = small[:, 87:89]
            link(TT(lamv[:, 0:4:2, :], lamv[:, 0:4:2, :], lamv[:, 1:4:2, :], ALU.mult))
            RED(l4, lamv[:, 0:4:2, :], AX_X, ALU.add).then_inc(S["lam_done"], 1)
            dve.wait_ge(W["condT_ps"], 1)
            TS(condT[:, :, :], psum[:, 7, 0:DC * 9].rearrange("p (c s) -> p c s", c=DC), 0.5, None, ALU.mult).then_inc(S["condT_sb"], 1)
            dve.wait_ge(W["lam_exp"], 1)
            link(TT(neglam, small[:, 86:87], small[:, 85:86], ALU.subtract))
            link(TS(neglam, neglam, -LAM_INIT, None, ALU.add))
            link(TS(gsub, gsub, 1.0 - LAM_INIT, None, ALU.mult))
            dve.wait_ge(W["const_in"], 16)
            link(STT(sgn, C("sub1", 32), neglam[0:32, :], C("sub0", 32), ALU.mult, ALU.add))
            dve.wait_ge(W["bias_in"], 48)
            for b in range(12):
                dve.wait_ge(W["ada_ps"], b + 1)
                a = slice(512 * b, 512 * b + 512)
                TT(mod[:, a], psum[0:9, b % 2, :], bada[:, a], ALU.add).then_inc(S["ada_sb"], 1)
            dve.wait_ge(W["ada_sb"], 12)
            for name, ln in (("scale_a", lnm), ("scale_f", lnf)):
                a = slice(MOD[name] * D, MOD[name] * D + D)
                STT(mod[:, a], mod[:, a], 1.0, ln[:, :], ALU.add, ALU.mult).then_inc(S["ada_sb"], 1)

            def mod_row(t, which):
                return (which[0] if t < NT - 1 else which[1])[0:rows(t), :]

            def make_h(t):
                n = rows(t)
                dve.wait_ge(W["rstd_done"], t + 1)
                if t >= 2:
                    dve.wait_ge(W["hT_ps"], t - 1)
                h = hrow[t % 2][0:n, :]
                link(STT(h, xin[t % 2][0:n, :], rstd[0:n, t:t + 1], mod_row(t, (scale_p, scale_s)), ALU.mult, ALU.mult))
                TT(h, h, mod_row(t, (shift_p, shift_s)), ALU.add).then_inc(S["h_done"], 1)

            def rotate(t, name, b, row):
                n = rows(t)
                dve.wait_ge(W[f"{name}_ps"], t + 1)
                if t >= 2:
                    dve.wait_ge(W[f"{name}T_ps"], t - 1)
                    if name == "k":
                        dve.wait_ge(W[f"kv_out{t % 2}"], 32 * (t // 2))
                src = psum[0:n, b, :].rearrange("p (s u d) -> p s u d", s=SUBS, u=2)
                dst = row[t % 2][0:n, :].rearrange("p (s u d) -> p s u d", s=SUBS, u=2)
                tmp = ropet[0:n, :].rearrange("p (s u d) -> p s u d", s=SUBS, u=2)
                cos, nsin, sin = (rope[0:n, t, 32 * k:32 * k + 32] for k in range(3))
                TT(dst, src, bc(cos, [n, SUBS, 2, 32], (1, 1)), ALU.mult)
                TT(tmp[:, :, 0, :], src[:, :, 1, :], bc(nsin, [n, SUBS, 32], (1,)), ALU.mult)
                link(TT(tmp[:, :, 1, :], src[:, :, 0, :], bc(sin, [n, SUBS, 32], (1,)), ALU.mult))
                TT(dst, dst, tmp, ALU.add).then_inc(S[f"{name}_done"], 1)
                dve.wait_ge(W[f"{name}_done"], t + 1)

            dve.wait_ge(W["mix_rows_in"], 2 * ROWSEMS)
            make_h(0)
            for t in range(NT):
                if t + 1 < NT:
                    make_h(t + 1)
                rotate(t, "q", 2, qrow)
                rotate(t, "k", 3, krow)

            dve.wait_ge(W["state_ps"], 1)
            samples = cuT[:, :, 2 + SEQ:].rearrange("p c (s n) -> p c s n", s=NSEQ)
            nc.vector.memset(cuT[:, :, 0:2], 0.0)
            nc.vector.tensor_copy(samples[:, :, :, 0:2], psum[:, 6, 0:64].rearrange("p (c s n) -> p c s n", c=4, s=NSEQ)).then_inc(S["state_sb_s"], 1)
            nc.vector.tensor_copy(wcvT[:, :, 0:3], psum[:, 6, 64:80].rearrange("p (c k) -> p c k", c=4)[:, :, 0:3]).then_inc(S["state_sb_s"], 1)
            dve.wait_ge(W["state_sb_s"], 2)
            for i in range(4):
                for tb in range(3):
                    n = 3 * i + tb
                    dve.wait_ge(W["cg_sb_s"], n + 1)
                    src = psum[:, 3 * (n % 2) + 2, 0:TB]
                    m = TB if tb < 2 else TB - NSAMP
                    dst = cuT[:, i, 2 + TB * tb:2 + TB * tb + m]
                    last = TT(dst, src[:, 0:m], cg_sb[:, 0:m], ALU.mult)
                    if tb == 2:
                        last = TT(samples[:, i, :, 2:], src[:, m:].rearrange("p (s n) -> p s n", s=NSEQ),
                                  cg_sb[:, m:].rearrange("p (s n) -> p s n", s=NSEQ), ALU.mult)
                    last.then_inc(S["cu_done"], 1)
                dve.wait_ge(W["cu_done"], 3 * i + 3)
                dve.wait_ge(W["bg_sb_s"], 3 * i + 3)
                if i:
                    dve.wait_ge(W["conv_done"], 2 * i)
                for part in range(2):
                    if part == 0:
                        tap = [cuT[:, i, k:k + SEQ] for k in range(3)]
                        acc, gate, dst = ctmp[:, 0:SEQ], bg_sb[:, 0:SEQ], mixC[:, i, 0:SEQ]
                    else:
                        tap = [samples[:, i, :, k:k + LNEW] for k in range(3)]
                        acc, gate, dst = (v.rearrange("p (s n) -> p s n", s=NSEQ) for v in
                                          (ctmp[:, SEQ:TOK], bg_sb[:, SEQ:TOK], mixC[:, i, SEQ:TOK]))
                    link(TS(acc, tap[0], wcvT[:, i, 0:1], None, ALU.mult))
                    link(STT(acc, tap[1], wcvT[:, i, 1:2], acc, ALU.mult, ALU.add))
                    link(STT(acc, tap[2], wcvT[:, i, 2:3], acc, ALU.mult, ALU.add))
                    TT(dst, acc, gate, ALU.mult).then_inc(S["conv_done"], 1)
            nc.vector.tensor_copy(ncT[:, :, 0:2], cuT[:, :, SEQ:SEQ + 2])
            nc.vector.tensor_copy(ncT[:, :, 2:].rearrange("p c (s n) -> p c s n", s=NSEQ), samples[:, :, :, LNEW:]).then_inc(S["ncT_done"], 1)
            dve.wait_ge(W["conv_done"], 8)
            dve.wait_ge(W["qT_sb"], NT)
            link(nc.vector.memset(qbd[:, :, :, :], 0.0))
            for c in range(4):
                for u in range(2):
                    r = slice(64 * u, 64 * u + 64)
                    a = 8 * c + 4 * u
                    last = nc.vector.tensor_copy(qbd[r, :, c, a:a + LNEW], qTs[r, c, :].rearrange("p (s q) -> p s q", s=NSEQ))
            last.then_inc(S["qbd_done"], 1)

            scores = psum[:, 0:4, :].rearrange("p (s b) n -> p s (b n)", s=2)

            def maxima(w, u):
                i = w // HEADS
                dve.wait_ge(W["s_ps"], 2 * w + u + 1)
                diag = scores[:, u, P * i:P * i + P]
                TT(diag, diag, C("mask"), ALU.add).then_inc(S["mask_done"], 1)
                dve.wait_ge(W["mask_done"], 2 * w + u + 1)
                k = 2 * (w % 2) + u
                RED(nm[:, k:k + 1], scores[:, u, 0:P * (i + 1)], AX_X, ALU.max, negate=True).then_inc(S["nmax_done"], 1)

            def attention_rows(i):
                dve.wait_ge(W["rstdh_done"], i + 1)
                if i >= 1:
                    dve.wait_ge(W["attT_ps"], i)
                link(TT(hsc, r1s[i % 2], hrs, ALU.mult))
                for h in range(HEADS):
                    last = STT(attrow[:, P * h:P * h + P], psum[:, 6 + i % 2, P * h:P * h + P], hsc[:, h:h + 1], gsub, ALU.mult, ALU.mult)
                last.then_inc(S["att_done"], 1)

            maxima(0, 0)
            maxima(0, 1)
            for w in range(8 * HEADS):
                i, h = divmod(w, HEADS)
                if w + 1 < 8 * HEADS:
                    maxima(w + 1, 0)
                dve.wait_ge(W["exp_done"], 2 * w + 2)
                l0, l1 = ls[:, 2 * (w % 2):2 * (w % 2) + 1], ls[:, 2 * (w % 2) + 1:2 * (w % 2) + 2]
                nc.vector.reciprocal(r1s[i % 2][:, h:h + 1], l0)
                link(nc.vector.reciprocal(rl[:, 0:1], l1))
                link(STT(ratio, rl[:, 0:1], l0, neglam, ALU.mult, ALU.mult))
                if w >= 1:
                    dve.wait_ge(W["adT_ps"], w)
                nk = P * (i + 1)
                p2 = (pexp, pexp2)[w % 2]
                STT(adiff[:, 0:nk], p2[:, 1, 0:nk], ratio, p2[:, 0, 0:nk], ALU.mult, ALU.add).then_inc(S["adiff_done"], 1)
                if w + 1 < 8 * HEADS:
                    maxima(w + 1, 1)
                if h == 1 and i >= 1:
                    attention_rows(i - 1)
            attention_rows(7)

            def sample_maxima(s):
                b = s % 2
                dve.wait_ge(W["ds_ps"], s + 1)
                TT(snew[b][:, :], psum[0:32, 7, 256:256 + LNEW], C("dmask", 32), ALU.add).then_inc(S["dnew_done"], 1)
                dve.wait_ge(W["dnew_done"], s + 1)
                RED(dmx[:, 0:1], psum[0:32, 2 * b:2 * b + 2, :].rearrange("p b n -> p (b n)"), AX_X, ALU.max)
                link(RED(dmx[:, 1:2], snew[b][:, :], AX_X, ALU.max))
                link(TT(dmx[:, 2:3], dmx[:, 0:1], dmx[:, 1:2], ALU.max))
                TS(dmx[:, 3 + b:4 + b], dmx[:, 2:3], -1.0, None, ALU.mult).then_inc(S["dmax_done"], 1)

            def sample_weights(s):
                b = s % 2
                dve.wait_ge(W["da_ps"], s + 1)
                seq = [aTs[b][:, :, :].rearrange("p n (h x) -> p n h x", h=HEADS)[:, :, :, LNEW * r:LNEW * r + LNEW] for r in (s - 2, s)] if s >= 2 else [
                    None, aTs[b][:, :, :].rearrange("p n (h x) -> p n h x", h=HEADS)[:, :, :, LNEW * s:LNEW * s + LNEW]]
                if s >= 2:
                    dve.wait_ge(W["do_ps"], s - 1)
                    nc.vector.memset(seq[0], 0.0)
                nc.vector.tensor_copy(seq[1][:, 0:PAGES], psum[:, 7, 0:16 * PAGES].rearrange("p (n h q) -> p n h q", n=PAGES, h=HEADS))
                nc.vector.tensor_copy(seq[1][0:LNEW, PAGES], psum[0:LNEW, 7, 16 * PAGES:16 * PAGES + 16].rearrange("p (h q) -> p h q", h=HEADS)).then_inc(S["da_sb"], 1)

            def sample_pairs(s):
                dve.wait_ge(W["dexp_done"], 2 * s + 2)
                link(TT(dl[:, 2:3], dl[:, 0:1], dl[:, 1:2], ALU.add))
                link(nc.vector.reciprocal(dr[:, 0:1], dl[:, 2:3]))
                link(TT(dr[:, 1:2], dr[:, 0:1], sgn, ALU.mult))
                TS(pairs[s % 2][:, :], C("pair", 32), dr[:, 1:2], None, ALU.mult).then_inc(S["pair_done"], 1)

            dve.wait_ge(W["attT_ps"], 8)
            for b in range(2):
                link(nc.vector.memset(aTs[b][:, :, :], 0.0))
            for s in range(NSEQ):
                sample_maxima(s)
                if s >= 1:
                    sample_weights(s - 1)
                sample_pairs(s)
            sample_weights(NSEQ - 1)
            dve.wait_ge(W["rstds_done"], 1)
            for h in range(HEADS):
                last = STT(attrow[0:NSAMP, P * h:P * h + P], orow[:, h, :], hrs[0:NSAMP, h:h + 1],
                           gsub[0:NSAMP, :], ALU.mult, ALU.mult)
            last.then_inc(S["atts_done"], 1)

            def make_h2(t):
                n = rows(t)
                dve.wait_ge(W["rstd2_done"], t + 1)
                if t >= 2:
                    dve.wait_ge(W["h2T_ps"], t - 1)
                    dve.wait_ge(W[f"h2_out{t % 2}"], 16 * (t // 2))
                h = h2row[t % 2][0:n, :]
                link(STT(h, x1[0:n, t, :], rs2[0:n, t:t + 1], mod_row(t, (scale_p, scale_s)), ALU.mult, ALU.mult))
                TT(h, h, mod_row(t, (shift_p, shift_s)), ALU.add).then_inc(S["h2_done"], 1)

            def take_logits(t):
                n = rows(t)
                dve.wait_ge(W["lg_ps"], t + 1)
                TT(logit[0:n, t, :], psum[0:n, 6, 0:NG + NE], brt[0:n, :], ALU.add).then_inc(S["lg_done"], 1)

            dve.wait_ge(W["attsT_ps"], 1)
            dve.wait_ge(W["wout_in"], 80)
            link(nc.vector.memset(logit[:, NT - 1, :], 0.0))
            dve.wait_ge(W["ffn_rows_in"], 2 * ROWSEMS)
            dve.wait_ge(W["gate_rows_in"], ROWSEMS)
            dve.wait_ge(W["xres_in"], 16 * NT)
            for t in range(NT):
                n = rows(t)
                if t >= 1:
                    make_h2(t - 1)
                for j in range(2):
                    a = slice(512 * j, 512 * j + 512)
                    dve.wait_ge(W["mix_ps"], 2 * t + j + 1)
                    if t or j:
                        dve.wait_ge(W["x1_done"], 2 * t + j)
                    link(TT(otmp[0:n, :], psum[0:n, 2 * (t % 2) + j, :], mod_row(t, (gate_ap, gate_as))[:, a], ALU.mult))
                    TT(x1[0:n, t, a], x1[0:n, t, a], otmp[0:n, :], ALU.add).then_inc(S["x1_done"], 1)
                if t >= 2:
                    take_logits(t - 2)
            make_h2(NT - 1)
            take_logits(NT - 2)
            take_logits(NT - 1)

            dve.wait_ge(W["lg_done"], NT)
            dve.wait_ge(W["h2T_ps"], NT)
            dve.wait_ge(W["h2_out0"], 16 * 5)
            dve.wait_ge(W["h2_out1"], 16 * 4)
            nc.vector.memset(ones[:, :], 1.0)
            r3 = lambda n, k: R[n].rearrange("p (t e) -> p t e", e=k)
            LG, LE = logit[:, :, 0:NG], logit[:, :, NG:NG + NE]
            iota4, iota32 = C("iota")[:, 0:NG], C("iota")[:, 0:NE]

            def first_max(eq, oh, scores_, top, k, iota, mn):
                link(RED(top, scores_, AX_X, ALU.max))
                link(TT(eq, scores_, bc(top, [P, NT, k], (2,)), ALU.is_equal))
                link(STT(eq, eq, -64.0, bc(iota, [P, NT, k], (1,)), ALU.mult, ALU.add))
                link(RED(mn, eq, AX_X, ALU.min))
                link(TT(oh, eq, bc(mn, [P, NT, k], (2,)), ALU.is_equal))

            first_max(r3("eq4", NG), r3("ohg", NG), LG, R["gm"], NG, iota4, R["mn"])
            TT(r3("gs", NG), LG, bc(R["gm"], [P, NT, NG], (2,)), ALU.subtract).then_inc(S["gexp_in"], 1)
            link(TS(R["pen"], R["ohg"], -NEG, NEG, ALU.mult, ALU.add))
            el4 = R["el"].rearrange("p (t g e) -> p t g e", g=NG, e=EPG)
            link(TT(el4, LE.rearrange("p t (g e) -> p t g e", g=NG), bc(r3("pen", NG), [P, NT, NG, EPG], (3,)), ALU.add))
            first_max(r3("ta", NE), r3("oh1", NE), r3("el", NE), R["m1"], NE, iota32, R["mn"])
            link(STT(r3("el", NE), r3("oh1", NE), 2 * NEG, r3("el", NE), ALU.mult, ALU.add))
            first_max(r3("ta", NE), r3("oh2", NE), r3("el", NE), R["m2"], NE, iota32, R["mn"])
            TT(R["dd"], R["m2"], R["m1"], ALU.subtract).then_inc(S["wexp_in"], 1)
            for k in ("oh1", "oh2"):
                link(TT(r3(k, NE), r3(k, NE), bc(C("valid"), [P, NT, NE], (2,)), ALU.mult))
            TT(R["ohs"], R["oh1"], R["oh2"], ALU.add).then_inc(S["oh_done"], 1)
            dve.wait_ge(W["gexp_done"], 1)
            link(RED(R["gsum"], r3("ge", NG), AX_X, ALU.add))
            link(nc.vector.reciprocal(R["gp"], R["gsum"]))
            dve.wait_ge(W["wexp_done"], 1)
            link(TS(R["ws"], R["ee"], 1.0, None, ALU.add))
            link(nc.vector.reciprocal(R["ws"], R["ws"]))
            link(TT(cw[:, 0, :], R["ws"], R["gp"], ALU.mult))
            link(TT(cw[:, 1, :], cw[:, 0, :], R["ee"], ALU.mult))
            dve.wait_ge(W["cnt_ps"], 1)
            base, tot = r3("base", NE), psum[:, 1, 0:NT * NE].rearrange("p (t e) -> p t e", e=NE)
            link(nc.vector.memset(base[:, 0, :], 0.0))
            for t in range(1, NT):
                link(TT(base[:, t, :], tot[:, t - 1, :], base[:, t - 1, :], ALU.add))
            link(TT(R["cnt"], tot[:, NT - 1, :], base[:, NT - 1, :], ALU.add))
            link(TS(R["nt"], R["cnt"], 0.0, None, ALU.is_gt))
            for q in range(1, (TOK + P - 1) // P):
                link(STT(R["nt"], R["cnt"], float(P * q), R["nt"], ALU.is_gt, ALU.add))
            cur, nxt = "inca", "incb"
            link(nc.vector.tensor_copy(R[cur], R["nt"]))
            for d in (1, 2, 4, 8, 16):
                nc.vector.tensor_copy(R[nxt][:, 0:d], R[cur][:, 0:d])
                link(TT(R[nxt][:, d:], R[cur][:, d:], R[cur][:, 0:NE - d], ALU.add))
                cur, nxt = nxt, cur
            inc = R[cur]
            link(TT(R["first"], inc, R["nt"], ALU.subtract))
            link(TT(base, psum[:, 0, 0:NT * NE].rearrange("p (t e) -> p t e", e=NE), base, ALU.add))
            link(STT(base, bc(R["first"], [P, NT, NE], (1,)), float(P), base, ALU.mult, ALU.add))
            slot = R["slot"].rearrange("p (t k) -> p t k", k=2)
            for k, name in enumerate(("oh1", "oh2")):
                link(TT(r3("ta", NE), r3(name, NE), base, ALU.mult))
                link(RED(slot[:, :, k], r3("ta", NE), AX_X, ALU.add))
            link(nc.vector.tensor_copy(slot_i[:, :, :], slot))
            flat_i = slot_i[:, :, :].rearrange("p t k -> p (t k)")
            link(TS(slot_lo[:, :], flat_i, P - 1, None, ALU.bitwise_and))
            link(TS(slot_hi[:, :], flat_i, 7, None, ALU.logical_shift_right))
            link(nc.vector.tensor_copy(R["lo"], slot_lo[:, :]))
            link(nc.vector.tensor_copy(R["hi"], slot_hi[:, :]))
            for n in range(2 * NT):
                if n >= 4:
                    dve.wait_ge(W["map_ps"], n - 3)
                TS(lsel[n % 4][:, :], C("iota"), R["lo"][:, n:n + 1], None, ALU.is_equal)
                TS(hsel[n % 4][:, :], C("iota")[:, 0:TCOLS], R["hi"][:, n:n + 1], C("tokid")[:, n // 2:n // 2 + 1],
                   ALU.is_equal, ALU.mult).then_inc(S["sel_done"], 1)
            g3 = grid[:, :].rearrange("p (j e) -> p j e", e=NE)
            link(TT(g3, bc(inc[0:1, :], [1, TCOLS, NE], (1,)), bc(C("iota", 1)[:, 0:TCOLS], [1, TCOLS, NE], (2,)), ALU.is_le))
            tfl = R["tfl"][0:1, :]
            link(RED(tfl, g3, AX_X, ALU.add))
            link(TS(tfl, tfl, float(NE - 1), None, ALU.min))
            nc.vector.tensor_copy(plan[0:1, 0:TCOLS], tfl).then_inc(S["plan_done"], 1)
            link(TS(R["mn"][0:1, 0:1], inc[0:1, NE - 1:NE], 1.0, None, ALU.add))
            link(nc.vector.tensor_copy(plan[0:1, TCOLS + 1:TCOLS + 2], R["mn"][0:1, 0:1]))
            TS(plan[0:1, TCOLS:TCOLS + 1], plan[0:1, TCOLS + 1:TCOLS + 2], 1, None, ALU.logical_shift_right).then_inc(S["plan_done"], 1)
            dve.wait_ge(W["map_ps"], 2 * NT)
            nc.vector.tensor_copy(rowidx[:, :], psum[:, 2, 0:TCOLS]).then_inc(S["plan_done"], 1)

            dve.wait_ge(W["plan_done"], 3)
            npair = dve.value_load(plan[0:1, TCOLS:TCOLS + 1], min_val=1, max_val=MAXT // 2)
            with dve.Fori(0, npair) as i:
                for b in range(2):
                    j = 2 * i + b
                    dve.wait_ge(W["th_done"], j + 1)
                    STT(gated[b][:, :], th[b][:, :], 1.0, psum[:, 2 + b, 0:FE], ALU.add, ALU.mult).then_inc(S["m_dve_step"], 1)
                    dve.wait_ge(S["m_dve_step"], j + 1)
                    STT(hid[b][:, :], gated[b][:, :], 0.5, psum[:, 2 + b, FE:2 * FE], ALU.mult, ALU.mult).then_inc(S["hid_done"], 1)
                for b in range(2):
                    j = 2 * i + b
                    dve.wait_ge(W["hidT_ps"], j + 1)
                    nc.vector.tensor_copy(hidT[b][:, :, :], psum[:, 4, 0:FE].rearrange("p (c n) -> p c n", c=FC)).then_inc(S["hidT_sb"], 1)
                    dve.wait_ge(W["y_ps"], j + 3)
                    dve.wait_ge(W[f"y_out{b}"], 16 * i + 16)
                    nc.vector.tensor_copy(yrow[b][:, :], psum[:, 5:7, :].rearrange("p b n -> p (b n)")).then_inc(S["y_done"], 1)

            def finish(t):
                n = rows(t)
                dve.wait_ge(W["rstd3_done"], t + 1)
                if t >= 2:
                    dve.wait_ge(W[f"fin_out{t % 2}"], 16 * (t // 2))
                STT(fin[t % 2][0:n, :], x1[0:n, t, :], rs2[0:n, t:t + 1], lnfin[0:n, :], ALU.mult, ALU.mult).then_inc(S["fin_done"], 1)

            dve.wait_ge(W["fin_rows_in"], ROWSEMS + 16)
            for t in range(NT):
                n = rows(t)
                dve.wait_ge(W[f"yg_in{t % 3}"], 32 * (t // 3 + 1))
                y0, y1 = yg[t % 3][0][0:n, :], yg[t % 3][1][0:n, :]
                link(TS(y0, y0, cw[0:n, 0, t:t + 1], None, ALU.mult))
                link(STT(y0, y1, cw[0:n, 1, t:t + 1], y0, ALU.mult, ALU.add))
                link(TT(y0, y0, mod_row(t, (gate_fp, gate_fs)), ALU.mult))
                TT(x1[0:n, t, :], x1[0:n, t, :], y0, ALU.add).then_inc(S["comb_done"], 1)
                if t >= 1:
                    finish(t - 1)
            finish(NT - 1)

        @block.gpsimd
        def _(pool):
            steps = [0]

            def link(ins):
                steps[0] += 1
                ins.then_inc(S["pool_step"], 1)
                pool.wait_ge(S["pool_step"], steps[0])

            def inverse_root(dst, src, width, eps, done):
                link(nc.gpsimd.tensor_scalar(src, src, 1.0 / width, eps, ALU.mult, ALU.add))
                n, m = src.shape
                nc.gpsimd.tensor_tensor(dst, src, C("half", n).to_broadcast([n, m]), ALU.pow).then_inc(done, 1)

            pool.wait_ge(W["ada_sb"], 14)
            pool.dma_start(mod_dram, mod[:, :]).then_inc(S["mod_out"], 16)

            def root(t):
                n = rows(t)
                pool.wait_ge(W["ssq_done"], t + 1)
                inverse_root(rstd[0:n, t:t + 1], ssq[0:n, t:t + 1], D, NORM_EPS, S["rstd_done"])

            root(0)
            root(1)
            for t in range(NT):
                n = rows(t)
                pool.wait_ge(W["k_done"], t + 1)
                pool.wait_ge(W["v_done"], t + 1)
                ko, vo = (kp_out[P * t:P * t + P, :], vp_out[P * t:P * t + P, :]) if t < NT - 1 else (ks_out, vs_out)
                pool.dma_start(ko, krow[t % 2][0:n, :]).then_inc(S[f"kv_out{t % 2}"], 16)
                pool.dma_start(vo, v_sb[:, t, :] if t < NT - 1 else vs_row[0:n, :]).then_inc(S[f"kv_out{t % 2}"], 16)
                if t + 2 < NT:
                    root(t + 2)

            pool.wait_ge(W["nc_sb"], 1)
            pool.dma_start(cp_out, nc_row[0:2, :]).then_inc(S["nc_out"], 16)
            pool.dma_start(cs_out, nc_row[2:18, :]).then_inc(S["nc_out"], 16)

            def pad_queries(i):
                if i >= 2:
                    pool.wait_ge(W["s_ps"], 8 * (i - 1))
                link(nc.gpsimd.tensor_copy(qz[i % 2][0:64, 0, :, :], qT[0:64, :, P * i:P * i + P]))
                nc.gpsimd.tensor_copy(qz[i % 2][64:P, 1, :, :], qT[64:P, :, P * i:P * i + P]).then_inc(S["qz_done"], 1)
                pool.wait_ge(W["qz_done"], i + 1)

            pool.wait_ge(W["cv_ps"], 12)
            for i in range(2):
                link(nc.gpsimd.memset(qz[i][64:P, 0, :, :], 0.0))
                link(nc.gpsimd.memset(qz[i][0:64, 1, :, :], 0.0))
                pad_queries(i)
            for i in range(8):
                if i + 1 < 8 and i >= 1:
                    pool.wait_ge(W["rstdh_done"], i)
                    pad_queries(i + 1)
                pool.wait_ge(W["ssqh_done"], 4 * i + 4)
                inverse_root(hrs, hss, P, SUBLN_EPS, S["rstdh_done"])
            pool.wait_ge(W["ssqs_done"], 4)
            inverse_root(hrs[0:NSAMP, :], hss[0:NSAMP, :], P, SUBLN_EPS, S["rstds_done"])

            for t in range(NT):
                n = rows(t)
                pool.wait_ge(W["ssq2_done"], t + 1)
                inverse_root(rs2[0:n, t:t + 1], ss2[0:n, t:t + 1], D, NORM_EPS, S["rstd2_done"])
                pool.wait_ge(W["h2_done"], t + 1)
                pool.dma_start(h2_dram[P * t:P * t + n, :], h2row[t % 2][0:n, :]).then_inc(S[f"h2_out{t % 2}"], 16)

            pool.wait_ge(W["h2_out0"], 16 * 5)
            pool.wait_ge(W["h2_out1"], 16 * 4)
            pool.wait_ge(W["plan_done"], 3)
            npair = pool.value_load(plan[0:1, TCOLS:TCOLS + 1], min_val=1, max_val=MAXT // 2)

            def gather_rows(b):
                nc.gpsimd.indirect_dma_start(xg[b][:, :], None, h2_dram, bass.IndirectOffsetOnAxis(ap=idx1[b][:, 0:1], axis=0)).then_inc(S[f"xg_in{b}"], 16)

            for b in range(2):
                nc.gpsimd.tensor_copy(idx1[b][:, :], rowidx[:, b:b + 1]).then_inc(S["idx_done"], 1)
                pool.wait_ge(W["idx_done"], b + 1)
                gather_rows(b)
            with pool.Fori(0, npair) as i:
                for b in range(2):
                    j = 2 * i + b
                    pool.wait_ge(W["xgT_ps"], j + 3)
                    pool.sem_inc(S["xg_sched"], 1)
                    nc.gpsimd.tensor_copy(idx1[b][:, :], rowidx[:, bass.ds(j + 2, 1)]).then_inc(S["idx_done"], 1)
                    pool.wait_ge(W["idx_done"], j + 3)
                    pool.sem_inc(S["xg_sched"], 1)
                    gather_rows(b)

            for b in range(2):
                pool.wait_ge(W[f"y_out{b}"], 16 * npair + 16)
                pool.sem_inc(S["xg_sched"], 1)

            pool.wait_ge(W["fill_out"], 16 * (MAXT // 2 + 1))
            pool.sem_inc(S["xg_sched"], 1)

            def gather_pair(t):
                n = rows(t)
                for k in range(2):
                    nc.gpsimd.indirect_dma_start(yg[t % 3][k][0:n, :], None, ys_dram,
                                                 bass.IndirectOffsetOnAxis(ap=slot_i[0:n, t, k:k + 1], axis=0)).then_inc(S[f"yg_in{t % 3}"], 16)

            for t in range(3):
                gather_pair(t)
            for t in range(NT):
                n = rows(t)
                if t + 3 < NT:
                    pool.wait_ge(W["comb_done"], t + 1)
                    gather_pair(t + 3)
                pool.wait_ge(W["ssq3_done"], t + 1)
                inverse_root(rs2[0:n, t:t + 1], ss2[0:n, t:t + 1], D, NORM_EPS, S["rstd3_done"])


_INS = ['x_prompt', 'x_sample', 'cache_k', 'cache_v', 'state_conv', 'page_table', 'c_prompt', 'c_sample',
        'w_ada', 'b_ada', 'ln_mix', 'w_in', 'lam_q1', 'lam_k1', 'lam_q2', 'lam_k2', 'subln_g', 'w_conv', 'w_out',
        'ln_ffn', 'w_router_grp', 'b_router_grp', 'w_router_exp', 'b_router_exp', 'w_gate', 'w_up', 'w_down', 'ln_final']
_OUTS = [(1, SEQ, D), (NSEQ, LNEW, D), (1, 1, SEQ, SUBS, HD), (1, 1, SEQ, HEADS, 2 * HD), (1, 1, 2, AW),
         (1, NSEQ, LNEW, SUBS, HD), (1, NSEQ, LNEW, HEADS, 2 * HD), (1, NSEQ, 2, AW)]


def kernel(**inputs):
    import concourse.bacc as _bacc
    from concourse.bass_utils import run_bass_kernel_spmd as _run

    nc = _bacc.Bacc("TRN2", target_bir_lowering=False, num_devices=1)
    arrays, args = {"in_consts_dram": constants()}, []
    args.append(nc.dram_tensor("in_consts_dram", [P, NCONST], F32, kind="ExternalInput").ap())
    for name in _INS:
        a = np.ascontiguousarray(inputs[name])
        arrays[f"in_{name}_dram"] = a
        args.append(nc.dram_tensor(f"in_{name}_dram", a.shape, mybir.dt.from_np(a.dtype), kind="ExternalInput").ap())
    for i, shape in enumerate(_OUTS):
        args.append(nc.dram_tensor(f"out_{i}_dram", shape, F32, kind="ExternalOutput").ap())
    args.append(nc.dram_tensor("mod_scratch", [NSEQ + 1, 6 * D], F32, kind="Internal").ap())
    args.append(nc.dram_tensor("h2_scratch", [TOK, D], F32, kind="Internal").ap())
    args.append(nc.dram_tensor("ys_scratch", [(MAXT + 2) * P, D], F32, kind="Internal").ap())
    build(nc, *args)
    r = _run(nc, [arrays], core_ids=[0])
    return tuple(r.results[0][f"out_{i}_dram"] for i in range(len(_OUTS)))
```

```python
from contextlib import ExitStack

import concourse.bass as bass
import numpy as np
from concourse import mybir

F32 = mybir.dt.float32
F32R = mybir.dt.float32r
I32 = mybir.dt.int32
ALU = mybir.AluOpType
ACT = mybir.ActivationFunctionType
AX_X = mybir.AxisListType.X

P = 128
D = 1024
DC = D // P
SEQ = 1024
NSEQ, LNEW = 8, 4
NSAMP = NSEQ * LNEW
NT = SEQ // P + 1
TOK = SEQ + NSAMP
AW = 512
HEADS, SUBS, HD = 4, 8, 64
PAGES = 8
NG, EPG = 4, 8
NE = NG * EPG
FE = 256
FC = FE // P
MAXT = 2 * TOK // P + NE
MAXT += MAXT % 2
TCOLS = MAXT + 2
NOROW = 1 << 16
LAM_INIT = 0.2
NORM_EPS, SUBLN_EPS = 1e-6, 1e-5
SCALE = HD ** -0.5
NEG = -1e30
TB = TOK // 3
CUW = 2 + SEQ + NSEQ * (2 + LNEW)

_C = {}
_n = 0
for _name, _w in (("ident", P), ("mask", P), ("upper", P), ("iota", P), ("rope", NT * 96),
                  ("tokid", 2 * NT), ("valid", NT), ("dmask", LNEW), ("pair", 16), ("sub0", 1), ("sub1", 1),
                  ("half", 1)):
    _C[_name] = (_n, _n + _w)
    _n += _w
NCONST = _n


def constants():
    c = np.zeros((P, NCONST), np.float32)

    def put(name, v):
        a, b = _C[name]
        c[:v.shape[0], a:b] = v.reshape(v.shape[0], -1)

    i = np.arange(P)
    put("ident", np.eye(P, dtype=np.float32))
    put("mask", np.where(i[None, :] <= i[:, None], 0.0, NEG).astype(np.float32))
    put("upper", (i[:, None] < i[None, :]).astype(np.float32))
    put("iota", np.broadcast_to(i[None, :], (P, P)).astype(np.float32))
    pos = np.zeros((NT, P), np.float32)
    pos[:NT - 1] = np.arange(SEQ).reshape(NT - 1, P)
    pos[NT - 1, :NSAMP] = PAGES * P + np.arange(NSAMP) % LNEW
    exponent = (np.arange(0, HD, 2, dtype=np.float32) / np.float32(HD)).astype(np.float64)
    inv = (np.float32(1.0) / (10000.0 ** exponent).astype(np.float32)).astype(np.float32)
    ang = (pos[:, :, None] * inv[None, None, :]).astype(np.float32)
    table = np.concatenate([np.cos(ang), -np.sin(ang), np.sin(ang)], axis=-1).astype(np.float32)
    put("rope", np.ascontiguousarray(table.transpose(1, 0, 2)))
    tok = np.arange(NT)[None, :] * P + i[:, None]
    ok = tok < TOK
    rows_of = 1 + tok[:, :, None] + TOK * np.arange(2)
    put("tokid", np.where(ok[:, :, None], rows_of, 0).astype(np.float32))
    put("valid", ok.astype(np.float32))
    r = np.arange(SUBS * LNEW)
    put("dmask", np.where(np.arange(LNEW)[None, :] <= (r % LNEW)[:, None], 0.0, NEG).astype(np.float32))
    cols = np.arange(HEADS * LNEW)
    put("pair", ((r // (2 * LNEW))[:, None] * LNEW + (r % LNEW)[:, None] == cols[None, :]).astype(np.float32))
    put("sub0", ((r // LNEW) % 2 == 0).astype(np.float32)[:, None])
    put("sub1", ((r // LNEW) % 2 == 1).astype(np.float32)[:, None])
    put("half", np.full((P, 1), -0.5, np.float32))
    return c


def build(nc, consts, x_prompt, x_sample, cache_k, cache_v, state_conv, page_table, c_prompt, c_sample,
          w_ada, b_ada, ln_mix, w_in, lam_q1, lam_k1, lam_q2, lam_k2, subln_g, w_conv, w_out,
          ln_ffn, w_router_grp, b_router_grp, w_router_exp, b_router_exp, w_gate, w_up, w_down, ln_final,
          y_prompt, y_sample, k_prompt, v_prompt, conv_prompt, k_sample, v_sample, conv_sample,
          mod_dram, h2_dram, y_dram):
    x_p = x_prompt.rearrange("b s d -> (b s) d")
    x_s = x_sample.rearrange("b s d -> (b s) d")
    kc = cache_k.rearrange("l n p h d -> (l n) p (h d)")
    vc = cache_v.rearrange("l n p h d -> (l n) p (h d)")
    y_p = y_prompt.rearrange("b s d -> (b s) d")
    y_s = y_sample.rearrange("b s d -> (b s) d")
    kp_out = k_prompt.rearrange("l b s h d -> (l b s) (h d)")
    vp_out = v_prompt.rearrange("l b s h d -> (l b s) (h d)")
    ks_out = k_sample.rearrange("l b s h d -> (l b s) (h d)")
    vs_out = v_sample.rearrange("l b s h d -> (l b s) (h d)")
    cp_out = conv_prompt.rearrange("l b s c -> (l b s) c")
    cs_out = conv_sample.rearrange("l b s c -> (l b s) c")
    w_ada_v = w_ada[0].rearrange("(c p) n -> p c n", p=P)
    w_in_v = w_in[0].rearrange("(c p) n -> p c n", p=P)
    w_out_v = w_out[0].rearrange("(c p) n -> p c n", p=P)
    gate_v = w_gate[0].rearrange("e (p c) n -> e p c n", c=DC)
    up_v = w_up[0].rearrange("e (p c) n -> e p c n", c=DC)
    down_v = w_down[0].rearrange("e (p c) n -> e p c n", c=FC)

    with ExitStack() as ctx:
        K = 1024

        def at(name, off_bytes, shape, dt=F32):
            return nc.alloc_sbuf_tensor_at(name, shape, dt, offset=BASE + off_bytes)

        BASE = -(-nc.sbuf_base // 64) * 64
        psum = ctx.enter_context(nc.psum_tensor("psum", [P, 8, 512], F32))

        def sem(name):
            return ctx.enter_context(nc.semaphore(name))

        O_AB, O_X, O_W, O_H, O_VKQ, O_MA = 8 * K, 24 * K, 60 * K, 108 * K, 141 * K, 189 * K
        cst = at("cst", 0, [P, NCONST])
        small = at("small", NCONST * 4 + 32 - (NCONST * 4) % 32, [P, 224])
        kTs = at("kTs", 6 * K + 960, [P, HEADS, NSAMP])
        qTs = at("qTs", 7 * K + 448, [P, HEADS, NSAMP])

        def C(name, rows=P):
            a, b = _C[name]
            return cst[0:rows, a:b]

        ident = C("ident")
        rope = C("rope").rearrange("p (t c) -> p t c", t=NT)
        shift_p = at("shift_p", O_AB, [P, D]); scale_p = at("scale_p", O_AB + 4 * K, [P, D])
        shift_s = at("shift_s", O_AB + 8 * K, [P, D]); scale_s = at("scale_s", O_AB + 12 * K, [P, D])
        wada = [at(f"wada{i}", O_W + 16 * K * i, [P, DC, 512]) for i in range(3)]
        cond = at("cond", O_H, [NSEQ + 1, D]); cth = at("cth", O_H + 4 * K, [NSEQ + 1, D])
        condT = at("condT", O_H + 8 * K, [P, DC, NSEQ + 1])
        mod = at("mod", O_X, [NSEQ + 1, 6 * D])
        bada = at("bada", O_VKQ, [NSEQ + 1, 6 * D])
        lnm = at("lnm", O_VKQ + 24 * K, [NSEQ + 1, D]); lnf = at("lnf", O_VKQ + 28 * K, [NSEQ + 1, D])
        lamv = at("lamv", O_VKQ + 32 * K, [P, 4, HD]); gsub = small[:, 96:224]
        wqkv = at("wqkv", O_W, [P, DC, 3 * AW])
        hT = at("hT", O_H, [P, DC, TOK])
        xin = [at(f"xin{i}", O_X + 4 * K * i, [P, D]) for i in range(2)]
        hrow = [at(f"hrow{i}", O_X + 8 * K + 4 * K * i, [P, D]) for i in range(2)]
        qrow = [at(f"qrow{i}", O_X + 16 * K + 2 * K * i, [P, AW]) for i in range(2)]
        krow = [at(f"krow{i}", O_X + 20 * K + 2 * K * i, [P, AW]) for i in range(2)]
        ropet = at("ropet", O_X + 24 * K, [P, AW]); junk = at("junk", O_X + 26 * K, [P, D])
        vs_row = at("vs_row", O_X + 30 * K, [P, AW])
        v_sb = at("v_sb", O_VKQ, [P, NT - 1, AW])
        kT = at("kT", O_VKQ + 16 * K, [P, HEADS, SEQ]); qT = at("qT", O_VKQ + 32 * K, [P, HEADS, SEQ])
        wcv = [at(f"wcv{i}", O_W + 12 * K * i, [P, DC, 3, P]) for i in range(2)]
        cg_sb = at("cg_sb", O_W + 24 * K, [P, TB]); bg_sb = at("bg_sb", O_W + 25 * K + 512, [P, TOK])
        mixC = at("mixC", O_W + 31 * K + 512, [P, 4, TOK])
        cuT = at("cuT", O_X, [P, 4, CUW])
        ctmp = at("ctmp", O_X + 17 * K, [P, TOK])
        state_sb = at("state_sb", O_X + 22 * K, [2 * NSEQ, AW]); wcvT = at("wcvT", O_X + 24 * K, [P, 4, 4])
        wconv_sb = at("wconv_sb", O_X + 25 * K, [3, AW]); ncT = at("ncT", O_X + 27 * K, [P, 4, 18])
        nc_row = at("nc_row", O_X + 28 * K, [18, AW])
        pexp = at("pexp", O_H, [P, 2, SEQ])
        pexp2 = at("pexp2", O_H + 8 * K, [P, 2, SEQ])
        adiff = at("adiff", O_H + 16 * K, [P, SEQ])
        adT = at("adT", O_H + 20 * K, [P, SEQ // P, P])
        qz = [at(f"qz{i}", O_H + 24 * K + 4 * K * i, [P, 2, HEADS, P]) for i in range(2)]
        ajunk = at("ajunk", O_H + 32 * K, [P, P])
        attrow = at("attrow", O_X + 34 * K, [P, AW])
        mixA = at("mixA", O_MA, [P, 4, TOK])
        kseq = [at(f"kseq{i}", O_W + 8 * K * i, [P, 4, AW]) for i in range(3)]
        vseq = [at(f"vseq{i}", O_X + 16 * K * i, [P, PAGES, AW]) for i in range(2)]
        vnew = [at("vnew0", O_W + 28 * K + 512, [LNEW, AW]), at("vnew1", O_X + 32 * K, [LNEW, AW])]
        qbd = at("qbd", O_W + 24 * K, [P, NSEQ, 4, 32])
        kTp = [at(f"kTp{i}", O_H + 24 * K + 2 * K * i, [P, 4, P]) for i in range(2)]
        pdec = [at(f"pdec{i}", O_H + 4 * K * i + 512 * i, [32, PAGES * P + LNEW]) for i in range(2)]
        aTs = [at(f"aTs{i}", O_H + 9 * K + 5 * K * i, [P, PAGES + 1, P]) for i in range(2)]
        snew = [at(f"snew{i}", O_H + 19 * K + 64 * i, [32, LNEW]) for i in range(2)]
        pairs = [at(f"pairs{i}", O_H + 19 * K + 128 + 64 * i, [32, 16]) for i in range(2)]
        orow = at("orow", O_H + 20 * K, [NSAMP, HEADS, P])
        pt_sb = at("pt_sb", O_W + 28 * K, [1, NSEQ * PAGES], I32)
        wout = at("wout", O_VKQ, [P, DC, D])
        wrt = at("wrt", O_VKQ + 32 * K, [P, DC, NG + NE]); brt = at("brt", O_VKQ + 34 * K, [P, NG + NE])
        logit = at("logit", O_VKQ + 35 * K, [P, NT, NG + NE])
        gate_ap = at("gate_ap", O_W, [P, D]); gate_as = at("gate_as", O_W + 4 * K, [P, D])
        x1 = at("x1", O_X, [P, NT, D])
        h2row = [at(f"h2row{i}", O_H + 4 * K * i, [P, D]) for i in range(2)]
        h2T = [at(f"h2T{i}", O_H + 8 * K + 4 * K * i, [P, DC, P]) for i in range(2)]
        ojunk = at("ojunk", O_H + 16 * K, [P, D])
        otmp = at("otmp", O_H + 31 * K, [P, 512])
        rt = at("rt", O_H, [P, 3300])
        grid = at("grid", O_MA + 4 * K, [1, TCOLS * NE])
        lsel = [at(f"lsel{i}", O_MA + 11 * K + 512 * i, [P, P]) for i in range(4)]
        hsel = [at(f"hsel{i}", O_MA + 13 * K + 256 * i, [P, TCOLS]) for i in range(4)]
        xrow = at("xrow", O_MA, [P, TCOLS], I32)
        yidx = at("yidx", O_MA + 256, [P, TCOLS], I32)
        plan = at("plan", O_MA + 512, [1, TCOLS + 2], I32)
        cw = at("cw", O_MA + 768, [P, 2, NT])
        vmap = at("vmap", O_MA + 14 * K, [P, 3, TCOLS])
        wgu = [at(f"wgu{i}", O_W + 16 * K * i, [P, 2, DC, FE]) for i in range(2)]
        wdn = [at(f"wdn{i}", O_W + 32 * K + 8 * K * i, [P, FC, D]) for i in range(2)]
        wguL = [at(f"wguL{i}", O_W + 16 * K * i, [P, 2, DC, FE]) for i in range(2)]
        wdnL = [at(f"wdnL{i}", O_W + 32 * K + 8 * K * i, [P, FC, D]) for i in range(2)]
        wguH = [at(f"wguH{i}", O_VKQ + 16 * K * i, [P, 2, DC, FE]) for i in range(2)]
        wdnH = [at(f"wdnH{i}", O_VKQ + 32 * K + 8 * K * i, [P, FC, D]) for i in range(2)]
        gidx = [at(f"gidx{i}", O_MA + 1024 + 32 * i, [P, 1], I32) for i in range(2)]
        sidx = [at(f"sidx{i}", O_MA + 1088 + 32 * i, [P, 1], I32) for i in range(2)]
        xg = [at(f"xg{i}", O_H + 24 * K + 4 * K * i, [P, D]) for i in range(2)]
        xgH = [at(f"xgH{i}", O_H + 4 * K * i, [P, DC, P]) for i in range(2)]
        xgL = [at(f"xgL{i}", O_H + 8 * K + 4 * K * i, [P, DC, P]) for i in range(2)]
        th = [at(f"th{i}", O_H + 16 * K + K * i, [P, FE]) for i in range(2)]
        hid = [at(f"hid{i}", O_H + 18 * K + K * i, [P, FE]) for i in range(2)]
        hidH = [at(f"hidH{i}", O_H + 20 * K + K * i, [P, FC, P]) for i in range(2)]
        hidL = [at(f"hidL{i}", O_H + 22 * K + K * i, [P, FC, P]) for i in range(2)]
        gated = [at(f"gated{i}", O_MA + 2 * K + K * i, [P, FE]) for i in range(2)]
        yrow = [at(f"yrow{i}", O_MA + 4 * K + 4 * K * i, [P, D]) for i in range(2)]
        gate_fp = at("gate_fp", O_AB, [P, D]); gate_fs = at("gate_fs", O_AB + 4 * K, [P, D])
        lnfin = at("lnfin", O_AB + 8 * K, [P, D])
        yg = [[at(f"yg{i}_{k}", O_W + 8 * K * i + 4 * K * k, [P, D]) for k in range(2)] for i in range(3)]
        fin = [at(f"fin{i}", O_W + 24 * K + 4 * K * i, [P, D]) for i in range(2)]
        fjunk = at("fjunk", O_W + 32 * K, [P, D])

        ssq, rstd = small[:, 0:9], small[:, 9:18]
        neglam = small[:, 18:19]
        nm, ls, rl = small[:, 20:24], small[:, 24:28], small[:, 28:30]
        ratio = small[:, 30:31]
        r1s = [small[:, 32:36], small[:, 89:93]]
        hss, hrs, hsc = small[:, 36:40], small[:, 40:44], small[:, 44:48]
        lsum = small[:, 48:52]
        dmx, dl, dr = small[0:32, 52:57], small[0:32, 57:60], small[0:32, 60:64]
        sgn = small[0:32, 64:65]
        ss2, rs2 = small[:, 66:75], small[:, 75:84]

        R, off = {}, 0
        for name, n in (("ohs", NT * NE), ("oh1", NT * NE), ("oh2", NT * NE), ("el", NT * NE), ("ta", NT * NE), ("tb", NT * NE),
                        ("base", NT * NE), ("gm", NT), ("gs", NT * NG), ("ge", NT * NG), ("gsum", NT), ("gp", NT),
                        ("eq4", NT * NG), ("ohg", NT * NG), ("pen", NT * NG), ("mn", NT), ("m1", NT), ("m2", NT), ("dd", NT), ("ee", NT),
                        ("ws", NT), ("cnt", NE), ("nt", NE), ("inca", NE), ("incb", NE), ("first", NE), ("slot", 2 * NT),
                        ("lo", 2 * NT), ("hi", 2 * NT), ("tfl", TCOLS)):
            R[name] = rt[:, off:off + n]
            off += n
        assert off <= 3300
        ones = at("ones", O_H + 15 * K, [P, P])
        slot_i = at("slot_i", O_H + 14 * K + 256, [P, 2 * NT], I32)
        slot_lo = at("slot_lo", O_H + 14 * K, [P, 2 * NT], I32)
        slot_hi = at("slot_hi", O_H + 14 * K + 128, [P, 2 * NT], I32)

        names = """const_in cond_in bias_in wada_in0 wada_in1 wada_in2 cond_th cond_act condT_ps condT_sb ada_ps ada_sb
        mod_out mix_rows_in lam_in lam_exp lam_done wqkv_in x_in0 x_in1 ssq_done rstd_done h_done hT_ps hT_sb q_ps k_ps v_ps
        q_done k_done v_done qT_ps kT_ps qT_sb kT_sb kv_out0 kv_out1 wcv_in0 wcv_in1 state_in state_ps state_sb_s
        cv_ps cg_sb_s bg_sb_s cu_done conv_done nc_ps nc_sb nc_out ncT_done
        qz_done s_ps mask_done nmax_done exp_done adiff_done adT_ps adT_sb o_ps ssqh_done rstdh_done att_done attT_ps attT_sb
        dscore_ps page_in kseq_in0 kseq_in1 kseq_in2 vseq_in0 vseq_in1 kp_ps kp_sb qbd_done ds_ps dnew_done dmax_done dexp_done pair_done
        da_ps da_sb do_ps oT_sb ssqs_done rstds_done atts_done attsT_ps attsT_sb
        wout_in ffn_rows_in gate_rows_in xres_in mix_ps x1_done ssq2_done rstd2_done h2_done h2_out0 h2_out1 h2T_ps h2T_sb lg_ps lg_done
        gexp_in gexp_done wexp_in wexp_done oh_done cnt_ps sel_done map_ps plan_done
        wgate_in0 wgate_in1 wup_in0 wup_in1 wdn_in0 wdn_in1 wguH_done wguL_done wdnH_done wdnL_done gidx_done sidx_done xg_in0 xg_in1 go_on
        xgT_ps xgH_done xgL_done gu_ps th_done hid_done hidT_ps hidH_done hidL_done y_ps y_done y_out0 y_out1
        fin_rows_in yg_in0 yg_in1 yg_in2 comb_done scaled_done ssq3_done rstd3_done fin_done fin_out0 fin_out1
        dve_step act_step pool_step m_dve_step""".split()
        S = {n: sem(n) for n in names}

        block = ctx.enter_context(nc.Block())

        def rows(t):
            return P if t < NT - 1 else NSAMP

        def mixT(c, lo, n):
            return (mixA if c < 4 else mixC)[:, c % 4, lo:lo + n]

        MOD = {"shift_a": 0, "scale_a": 1, "gate_a": 2, "shift_f": 3, "scale_f": 4, "gate_f": 5}

        def load_mod(eng, name, dst_p, dst_s, s):
            a = MOD[name] * D
            eng.dma_start(dst_p[:, :], mod_dram[0, a:a + D].partition_broadcast(P)).then_inc(s, 16)
            for i in range(NSEQ):
                eng.dma_start(dst_s[LNEW * i:LNEW * i + LNEW, :],
                              mod_dram[1 + i, a:a + D].partition_broadcast(LNEW)).then_inc(s, 16)

        ROWSEMS = 16 * (1 + NSEQ)

        def expert_steps(eng, step, mid):
            for b in range(2):
                step(b, b, 0, True, 2)
            with eng.Fori(0, mid) as m:
                for b in range(2):
                    step(2 * m + (2 + b), b, m + 1, False, 2)
            for b in range(2):
                step(2 * mid + (2 + b), b, mid + 1, False, 1 - b)

        def r32(ap):
            return ap.bitcast(F32R)
        W = S

        @block.sync
        def _(sp):
            sp.dma_start(cst[:, :], consts).then_inc(S["const_in"], 16)
            sp.dma_start(cond[0:1, :], c_prompt).then_inc(S["cond_in"], 16)
            sp.dma_start(cond[1:NSEQ + 1, :], c_sample).then_inc(S["cond_in"], 16)
            for b in range(12):
                if b >= 3:
                    sp.wait_ge(W["ada_ps"], b - 2)
                sp.dma_start(wada[b % 3][:, :, :], w_ada_v[:, :, 512 * b:512 * b + 512]).then_inc(S[f"wada_in{b % 3}"], 16)
                if b == 0:
                    sp.dma_start(bada[:, :], b_ada[0].partition_broadcast(NSEQ + 1)).then_inc(S["bias_in"], 16)
                    sp.dma_start(lnm[:, :], ln_mix[0].partition_broadcast(NSEQ + 1)).then_inc(S["bias_in"], 16)
                    sp.dma_start(lnf[:, :], ln_ffn[0].partition_broadcast(NSEQ + 1)).then_inc(S["bias_in"], 16)
                    for i, v in enumerate((lam_q1, lam_k1, lam_q2, lam_k2)):
                        sp.dma_start(lamv[:, i, :], v[0].partition_broadcast(P)).then_inc(S["lam_in"], 16)
                    sp.dma_start(gsub, subln_g[0].partition_broadcast(P)).then_inc(S["lam_in"], 16)
            sp.wait_ge(W["ada_ps"], 12)
            sp.dma_start(wqkv[:, :, :], w_in_v[:, :, 0:3 * AW]).then_inc(S["wqkv_in"], 16)
            sp.wait_ge(W["mod_out"], 16)
            load_mod(sp, "shift_a", shift_p, shift_s, S["mix_rows_in"])
            load_mod(sp, "scale_a", scale_p, scale_s, S["mix_rows_in"])
            for t in range(NT):
                if t >= 2:
                    sp.wait_ge(W["h_done"], t - 1)
                src = x_p[P * t:P * t + P, :] if t < NT - 1 else x_s
                sp.dma_start(xin[t % 2][0:rows(t), :], src).then_inc(S[f"x_in{t % 2}"], 16)
            sp.wait_ge(W["v_ps"], NT)
            for i in range(4):
                if i >= 2:
                    sp.wait_ge(W["cv_ps"], 3 * (i - 1))
                for j in range(3):
                    a = 3 * AW + j * AW + P * i
                    sp.dma_start(wcv[i % 2][:, :, j, :], w_in_v[:, :, a:a + P]).then_inc(S[f"wcv_in{i % 2}"], 16)
                if i == 0:
                    sp.wait_ge(W["kT_ps"], NT)
                    sp.wait_ge(W["kv_out0"], 32 * 5)
                    sp.wait_ge(W["kv_out1"], 32 * 4)
                    sp.wait_ge(W["rstd_done"], NT)
                    sp.dma_start(state_sb[:, :], state_conv.rearrange("l b s c -> (l b s) c")).then_inc(S["state_in"], 16)
                    sp.dma_start(wconv_sb[:, :], w_conv[0]).then_inc(S["state_in"], 16)
            sp.wait_ge(W["cv_ps"], 12)
            sp.wait_ge(W["conv_done"], 8)
            sp.dma_start(pt_sb[:, :], page_table.rearrange("b n -> (b n)").rearrange("(a n) -> a n", a=1)).then_inc(S["page_in"], 16)
            sp.wait_ge(W["page_in"], 16)
            sp.wait_ge(W["nc_out"], 32)
            for s in range(NSEQ):
                if s >= 2:
                    sp.wait_ge(W["do_ps"], s - 1)
                for g in range(2):
                    n = 2 * s + g
                    if n >= 3:
                        sp.wait_ge(W["kp_ps"], 4 * (n - 2))
                    for j in range(4):
                        p = 4 * g + j
                        page = sp.value_load(pt_sb[0:1, s * PAGES + p:s * PAGES + p + 1], min_val=0, max_val=kc.shape[0] - 1)
                        sp.dma_start(kseq[n % 3][:, j, :], kc[bass.ds(page, 1)].rearrange("o p c -> p (o c)")).then_inc(S[f"kseq_in{n % 3}"], 16)
                        sp.dma_start(vseq[s % 2][:, p, :], vc[bass.ds(page, 1)].rearrange("o p c -> p (o c)")).then_inc(S[f"vseq_in{s % 2}"], 16)
                sp.dma_start(vnew[s % 2][:, :], vs_out[LNEW * s:LNEW * s + LNEW, :]).then_inc(S[f"vseq_in{s % 2}"], 16)
            sp.wait_ge(W["o_ps"], 32)
            sp.dma_start(wout[:, :, :], w_out_v).then_inc(S["wout_in"], 16)
            sp.dma_start(wrt[:, :, 0:NG], w_router_grp[0].rearrange("(c p) n -> p c n", p=P)).then_inc(S["wout_in"], 16)
            sp.dma_start(wrt[:, :, NG:NG + NE], w_router_exp[0].rearrange("(c p) n -> p c n", p=P)).then_inc(S["wout_in"], 16)
            sp.dma_start(brt[:, 0:NG], b_router_grp[0].partition_broadcast(P)).then_inc(S["wout_in"], 16)
            sp.dma_start(brt[:, NG:NG + NE], b_router_exp[0].partition_broadcast(P)).then_inc(S["wout_in"], 16)
            load_mod(sp, "shift_f", shift_p, shift_s, S["ffn_rows_in"])
            load_mod(sp, "scale_f", scale_p, scale_s, S["ffn_rows_in"])
            sp.wait_ge(W["kp_ps"], 64)
            load_mod(sp, "gate_a", gate_ap, gate_as, S["gate_rows_in"])
            sp.wait_ge(W["do_ps"], NSEQ)
            for t in range(NT):
                if t == NT - 1:
                    sp.wait_ge(W["attsT_ps"], 1)
                src = x_p[P * t:P * t + P, :] if t < NT - 1 else x_s
                sp.dma_start(x1[0:rows(t), t, :], src).then_inc(S["xres_in"], 16)
            sp.wait_ge(W["h2_done"], NT)
            load_mod(sp, "gate_f", gate_fp, gate_fs, S["fin_rows_in"])
            sp.dma_start(lnfin[:, :], ln_final.partition_broadcast(P)).then_inc(S["fin_rows_in"], 16)
            sp.wait_ge(W["plan_done"], 2)
            mid = sp.value_load(plan[0:1, TCOLS:TCOLS + 1], min_val=NE // 2 - 2, max_val=MAXT // 2 - 2)

            def load_gate_up(j, b):
                e = sp.value_load(plan[0:1, bass.ds(j, 1)], min_val=0, max_val=NE - 1)
                sp.dma_start(wgu[b][:, 0, :, :], gate_v[bass.ds(e, 1)].rearrange("o p c n -> p (o c) n")).then_inc(S[f"wgate_in{b}"], 16)
                sp.dma_start(wgu[b][:, 1, :, :], up_v[bass.ds(e, 1)].rearrange("o p c n -> p (o c) n")).then_inc(S[f"wup_in{b}"], 16)

            def load_weights(j, b, i, first, left):
                if left:
                    if not (first and b == 0):
                        sp.wait_ge(W["gu_ps"], j)
                    load_gate_up(j + 1, 1 - b)
                e = sp.value_load(plan[0:1, bass.ds(j, 1)], min_val=0, max_val=NE - 1)
                if not first:
                    sp.wait_ge(W["y_ps"], j - 1)
                sp.dma_start(wdn[b][:, :, :], down_v[bass.ds(e, 1)].rearrange("o p c n -> p (o c) n")).then_inc(S[f"wdn_in{b}"], 16)

            load_gate_up(0, 0)
            expert_steps(sp, load_weights, mid)
            for b in range(2):
                sp.wait_ge(W[f"y_out{b}"], 16 * mid + 32)
                sp.sem_inc(S["go_on"], 1)

            def load_pair(t):
                n = rows(t)
                for k in range(2):
                    a = TOK * k + P * t
                    sp.dma_start(yg[t % 3][k][0:n, :], y_dram[a:a + n, :]).then_inc(S[f"yg_in{t % 3}"], 16)

            for t in range(3):
                load_pair(t)
            for t in range(NT):
                if t + 3 < NT:
                    sp.wait_ge(W["comb_done"], t + 1)
                    load_pair(t + 3)
                sp.wait_ge(W["fin_done"], t + 1)
                dst = y_p[P * t:P * t + P, :] if t < NT - 1 else y_s
                sp.dma_start(dst, fin[t % 2][0:rows(t), :]).then_inc(S[f"fin_out{t % 2}"], 16)
            sp.wait_ge(W["fin_out0"], 16 * 5)
            sp.wait_ge(W["fin_out1"], 16 * 4)
            sp.wait_ge(W["kv_out0"], 32 * 5)
            sp.wait_ge(W["kv_out1"], 32 * 4)
            sp.wait_ge(W["nc_out"], 32)

        def bank(b, n=512, rows_=P):
            return psum[0:rows_, b, 0:n]

        def page_scores(pe, s, p):
            n = s * PAGES + p
            pe.wait_ge(W["kp_sb"], n + 1)
            if p == 0 and s >= 2:
                pe.wait_ge(W["dexp_done"], 2 * s - 2)
            for c in range(4):
                last = nc.tensor.matmul(psum[0:32, 2 * (s % 2) + p // 4, P * (p % 4):P * (p % 4) + P], qbd[:, s, c, :], kTp[n % 2][:, c, :],
                                        start=(c == 0), stop=(c == 3))
            last.then_inc(S["dscore_ps"], 1)

        @block.tensor
        def _(pe):
            mm, tr = nc.tensor.matmul, nc.tensor.transpose

            pe.wait_ge(W["const_in"], 16)
            pe.wait_ge(W["cond_act"], 1)
            cT = bank(7, DC * 9).rearrange("p (c s) -> p c s", c=DC)
            for c in range(DC):
                last = tr(cT[:, c, :], cond[:, P * c:P * c + P], ident[0:9, 0:9])
            last.then_inc(S["condT_ps"], 1)
            pe.wait_ge(W["condT_sb"], 1)
            for b in range(12):
                pe.wait_ge(W[f"wada_in{b % 3}"], 16 * (b // 3 + 1))
                if b >= 2:
                    pe.wait_ge(W["ada_sb"], b - 1)
                for c in range(DC):
                    last = mm(psum[0:9, b % 2, :], condT[:, c, :], wada[b % 3][:, c, :], start=(c == 0), stop=(c == DC - 1))
                last.then_inc(S["ada_ps"], 1)

            def x_transposes(t):
                pe.wait_ge(W["h_done"], t + 1)
                if t >= 1:
                    pe.wait_ge(W["hT_sb"], t)
                n = rows(t)
                for c in range(DC):
                    last = tr(psum[:, c // 4, P * (c % 4):P * (c % 4) + n], hrow[t % 2][0:n, P * c:P * c + P], ident[0:n, 0:n])
                last.then_inc(S["hT_ps"], 1)

            def qk_transposes(t):
                n = rows(t)
                for name, src, b in (("q", qrow, 5), ("k", krow, 6)):
                    pe.wait_ge(W[f"{name}_done"], t + 1)
                    if t >= 1:
                        pe.wait_ge(W[f"{name}T_sb"], t)
                    for h in range(HEADS):
                        last = tr(psum[:, b, P * h:P * h + n], src[t % 2][0:n, P * h:P * h + P], ident[0:n, 0:n])
                    last.then_inc(S[f"{name}T_ps"], 1)

            x_transposes(0)
            pe.wait_ge(W["wqkv_in"], 16)
            for t in range(NT):
                n = rows(t)
                if t + 1 < NT:
                    x_transposes(t + 1)
                pe.wait_ge(W["hT_sb"], t + 1)
                for j, name in enumerate(("q", "k", "v")):
                    if t >= 1:
                        pe.wait_ge(W[f"{name}_done"], t)
                    for c in range(DC):
                        last = mm(psum[0:n, 2 + j, :], hT[:, c, P * t:P * t + n], wqkv[:, c, AW * j:AW * j + AW],
                                  start=(c == 0), stop=(c == DC - 1))
                    last.then_inc(S[f"{name}_ps"], 1)
                if t >= 1:
                    qk_transposes(t - 1)
            qk_transposes(NT - 1)

            pe.wait_ge(W["state_in"], 32)
            pe.wait_ge(W["qT_sb"], NT)
            pe.wait_ge(W["kT_sb"], NT)
            for i in range(4):
                tr(psum[:, 6, 16 * i:16 * i + 16], state_sb[:, P * i:P * i + P], ident[0:16, 0:16])
                last = tr(psum[:, 6, 64 + 4 * i:64 + 4 * i + 3], wconv_sb[:, P * i:P * i + P], ident[0:3, 0:3])
            last.then_inc(S["state_ps"], 1)
            pe.wait_ge(W["v_done"], NT)
            pe.wait_ge(W["k_done"], NT)
            for i in range(4):
                pe.wait_ge(W[f"wcv_in{i % 2}"], 48 * (i // 2 + 1))
                for tb in range(3):
                    n = 3 * i + tb
                    if n >= 2:
                        pe.wait_ge(W["cu_done"], n - 1)
                        pe.wait_ge(W["bg_sb_s"], n - 1)
                    for j in (1, 2, 0):
                        for c in range(DC):
                            last = mm(psum[:, 3 * (n % 2) + j, 0:TB], wcv[i % 2][:, c, j, :], hT[:, c, TB * tb:TB * tb + TB],
                                      start=(c == 0), stop=(c == DC - 1))
                    last.then_inc(S["cv_ps"], 1)
            pe.wait_ge(W["ncT_done"], 1)
            for i in range(4):
                last = tr(psum[0:18, 7, P * i:P * i + P], ncT[:, i, :], ident)
            last.then_inc(S["nc_ps"], 1)

            def scores(w, u):
                i, h = divmod(w, HEADS)
                if w == 0 and u == 0:
                    pe.wait_ge(W["qz_done"], 1)
                elif h == 0 and u == 0:
                    pe.wait_ge(W["qz_done"], i + 1)
                if w >= 1:
                    pe.wait_ge(W["exp_done"], 2 * w + u - 1)
                nk = P * (i + 1)
                for a in range(0, nk, 512):
                    b = min(nk, a + 512)
                    last = mm(psum[:, 2 * u + a // 512, 0:b - a], qz[i % 2][:, u, h, :], kT[:, h, a:b], start=True, stop=True)
                last.then_inc(S["s_ps"], 1)

            def weighted_values(w):
                i, h = divmod(w, HEADS)
                pe.wait_ge(W["adT_sb"], w + 1)
                if h == 0 and i >= 2:
                    pe.wait_ge(W["attT_sb"], i - 1)
                for kt in range(i + 1):
                    last = mm(psum[:, 6 + i % 2, P * h:P * h + P], adT[:, kt, :], v_sb[:, kt, P * h:P * h + P], start=(kt == 0), stop=(kt == i))
                last.then_inc(S["o_ps"], 1)

            def att_transposes(i):
                pe.wait_ge(W["att_done"], i + 1)
                for h in range(HEADS):
                    last = tr(psum[:, 6 + i % 2, P * h:P * h + P], attrow[:, P * h:P * h + P], ident)
                last.then_inc(S["attT_ps"], 1)

            pe.wait_ge(W["cu_done"], 12)
            pe.wait_ge(W["bg_sb_s"], 12)
            pe.wait_ge(W["nc_sb"], 1)
            pe.wait_ge(W["state_sb_s"], 2)
            pe.wait_ge(W["v_done"], NT)
            pe.wait_ge(W["kT_sb"], NT)
            scores(0, 0)
            scores(0, 1)
            for w in range(8 * HEADS):
                i, h = divmod(w, HEADS)
                if w + 1 < 8 * HEADS:
                    scores(w + 1, 0)
                    scores(w + 1, 1)
                if w >= 1:
                    weighted_values(w - 1)
                if h == 3 and i >= 1:
                    att_transposes(i - 1)
                pe.wait_ge(W["adiff_done"], w + 1)
                for kt in range(i + 1):
                    last = tr(psum[:, 4 + kt // 4, P * (kt % 4):P * (kt % 4) + P], adiff[:, P * kt:P * kt + P], ident)
                last.then_inc(S["adT_ps"], 1)
            weighted_values(8 * HEADS - 1)
            att_transposes(7)

            def sample_values(s):
                pe.wait_ge(W["pair_done"], s + 1)
                pe.wait_ge(W["dnew_done"], min(s + 2, NSEQ))
                for p in range(PAGES + 1):
                    m = P if p < PAGES else LNEW
                    last = mm(psum[0:m, 7, 16 * p:16 * p + 16], pdec[s % 2][:, P * p:P * p + m], pairs[s % 2][:, :], start=True, stop=True)
                last.then_inc(S["da_ps"], 1)
                pe.wait_ge(W["da_sb"], s + 1)
                pe.wait_ge(W[f"vseq_in{s % 2}"], 16 * (PAGES + 1) * (s // 2 + 1))
                for p in range(PAGES + 1):
                    if p < PAGES:
                        last = mm(psum[:, 6, :], aTs[s % 2][:, p, :], vseq[s % 2][:, p, :], start=(s == 0 and p == 0), stop=False)
                    else:
                        last = mm(psum[:, 6, :], aTs[s % 2][0:LNEW, p, :], vnew[s % 2][:, :], start=False, stop=(s == NSEQ - 1))
                last.then_inc(S["do_ps"], 1)

            pe.wait_ge(W["qbd_done"], 1)
            pe.wait_ge(W["attT_sb"], 8)
            for s in range(NSEQ):
                for p in range(PAGES):
                    n = s * PAGES + p
                    half = n // 4
                    pe.wait_ge(W[f"kseq_in{half % 3}"], 64 * (half // 3 + 1))
                    if n >= 2:
                        pe.wait_ge(W["kp_sb"], n - 1)
                    for c in range(4):
                        last = tr(psum[:, 4 + n % 2, P * c:P * c + P], kseq[half % 3][:, p % 4, P * c:P * c + P], ident)
                    last.then_inc(S["kp_ps"], 1)
                    if p >= 1:
                        page_scores(pe, s, p - 1)
                page_scores(pe, s, PAGES - 1)
                if s >= 2:
                    pe.wait_ge(W["da_sb"], s - 1)
                for c in range(4):
                    last = mm(psum[0:32, 7, 256:256 + LNEW], qbd[:, s, c, :], kTs[:, c, LNEW * s:LNEW * s + LNEW], start=(c == 0), stop=(c == 3))
                last.then_inc(S["ds_ps"], 1)
                if s >= 1:
                    sample_values(s - 1)
            sample_values(NSEQ - 1)
            pe.wait_ge(W["atts_done"], 1)
            for h in range(HEADS):
                last = tr(psum[:, 5, NSAMP * h:NSAMP * h + NSAMP], attrow[0:NSAMP, P * h:P * h + P], ident[0:NSAMP, 0:NSAMP])
            last.then_inc(S["attsT_ps"], 1)
            pe.wait_ge(W["attsT_sb"], 1)

            def router(t):
                n = rows(t)
                pe.wait_ge(W["h2_done"], t + 1)
                if t >= 1:
                    pe.wait_ge(W["h2T_sb"], t)
                for c in range(DC):
                    last = tr(psum[:, 4 + c // 4, P * (c % 4):P * (c % 4) + n], h2row[t % 2][0:n, P * c:P * c + P], ident[0:n, 0:n])
                last.then_inc(S["h2T_ps"], 1)

            def logits_of(t):
                n = rows(t)
                pe.wait_ge(W["h2T_sb"], t + 1)
                if t >= 1:
                    pe.wait_ge(W["lg_done"], t)
                for c in range(DC):
                    last = mm(psum[0:n, 6, 0:NG + NE], h2T[t % 2][:, c, 0:n], wrt[:, c, :], start=(c == 0), stop=(c == DC - 1))
                last.then_inc(S["lg_ps"], 1)

            pe.wait_ge(W["wout_in"], 16 * 5)
            for t in range(NT):
                n = rows(t)
                for j in range(2):
                    b = 2 * (t % 2) + j
                    if t >= 2:
                        pe.wait_ge(W["x1_done"], 2 * (t - 1))
                    for c in range(DC):
                        last = mm(psum[0:n, b, :], mixT(c, P * t, n), wout[:, c, 512 * j:512 * j + 512], start=(c == 0), stop=(c == DC - 1))
                    last.then_inc(S["mix_ps"], 1)
                if t >= 1:
                    router(t - 1)
                if t >= 2:
                    logits_of(t - 2)
            router(NT - 1)
            logits_of(NT - 2)
            logits_of(NT - 1)

            pe.wait_ge(W["oh_done"], 1)
            pe.wait_ge(W["x1_done"], 2 * NT)
            ohs = R["ohs"]
            mm(psum[:, 0, 0:NT * NE], C("upper"), ohs, start=True, stop=True)
            mm(psum[:, 1, 0:NT * NE], ones[:, :], ohs, start=True, stop=True).then_inc(S["cnt_ps"], 1)
            for n in range(2 * NT):
                pe.wait_ge(W["sel_done"], n + 1)
                last = mm(psum[:, 2, 0:TCOLS], lsel[n % 4][:, :], hsel[n % 4][:, :], start=(n == 0), stop=(n == 2 * NT - 1))
                last.then_inc(S["map_ps"], 1)

            pe.wait_ge(W["plan_done"], 2)
            mid = pe.value_load(plan[0:1, TCOLS:TCOLS + 1], min_val=NE // 2 - 2, max_val=MAXT // 2 - 2)

            def three_passes(out, xH, xL, wH, wL, chunks):
                parts = ((xH, wH), (xH, wL), (xL, wH))
                for c in range(chunks):
                    for k, (x, w) in enumerate(parts):
                        ins = mm(out, r32(x(c)), r32(w(c)), start=(c == 0 and k == 0), stop=(c == chunks - 1 and k == 2))
                return ins

            def gather_transposes(b):
                for c in range(DC):
                    last = tr(psum[:, c // 4, P * (c % 4):P * (c % 4) + P], xg[b][:, c:D:DC], ident)
                last.then_inc(S["xgT_ps"], 1)

            def down_products(j, b, i):
                pe.wait_ge(W["hidL_done"], j + 1)
                pe.wait_ge(W["wdnL_done"], j + 1)
                for n in range(2):
                    a = slice(512 * n, 512 * n + 512)
                    last = three_passes(psum[:, 5 + n, :], lambda c: hidH[b][:, c, :], lambda c: hidL[b][:, c, :],
                                        lambda c: wdnH[b][:, c, a], lambda c: wdnL[b][:, c, a], FC)
                last.then_inc(S["y_ps"], 1)

            def expert_products(j, b, i, first, left):
                pe.wait_ge(W["xgL_done"], j + 1)
                pe.wait_ge(W["wguL_done"], 2 * j + 2)
                three_passes(psum[:, 2 + b, :].rearrange("p (g n) -> p g n", g=2), lambda c: xgH[b][:, c, :], lambda c: xgL[b][:, c, :],
                             lambda c: wguH[b][:, :, c, :], lambda c: wguL[b][:, :, c, :], DC).then_inc(S["gu_ps"], 1)
                if left:
                    pe.wait_ge(W[f"xg_in{1 - b}"], 16 * (i + 1 + b))
                    gather_transposes(1 - b)
                if not (first and b == 0):
                    if not (first and b == 1):
                        pe.wait_ge(W["y_done"], j - 1)
                    down_products(j - 1, 1 - b, i)
                pe.wait_ge(W["hid_done"], j + 1)
                for c in range(FC):
                    last = tr(psum[:, 4, P * c:P * c + P], hid[b][:, c:FE:FC], ident)
                last.then_inc(S["hidT_ps"], 1)

            pe.wait_ge(W["xg_in0"], 16)
            gather_transposes(0)
            expert_steps(pe, expert_products, mid)
            pe.wait_ge(W["y_done"], 2 * mid + 3)
            down_products(2 * mid + 3, 1, mid + 1)

        def bc(ap, shape, axes):
            for a in axes:
                ap = ap.unsqueeze(a)
            return ap.to_broadcast(shape)

        @block.scalar
        def _(act):
            A = nc.scalar.activation
            steps = [0]

            def link(ins):
                steps[0] += 1
                ins.then_inc(S["act_step"], 1)
                act.wait_ge(S["act_step"], steps[0])

            act.wait_ge(W["cond_in"], 32)
            A(cth[:, :], cond[:, :], ACT.Tanh, scale=0.5).then_inc(S["cond_th"], 1)
            act.wait_ge(W["lam_done"], 1)
            A(small[:, 85:87], small[:, 87:89], ACT.Exp).then_inc(S["lam_exp"], 1)

            def squares(t):
                n = rows(t)
                act.wait_ge(W[f"x_in{t % 2}"], 16 * (t // 2 + 1))
                if t >= 1:
                    act.wait_ge(W["ssq_done"], t)
                A(junk[0:n, :], xin[t % 2][0:n, :], ACT.Square, accum_out=ssq[0:n, t:t + 1]).then_inc(S["ssq_done"], 1)

            def copy_hT(t):
                n = rows(t)
                act.wait_ge(W["hT_ps"], t + 1)
                nc.scalar.copy(hT[:, :, P * t:P * t + n], psum[:, 0:2, :].rearrange("p b (c n) -> p (b c) n", c=4)[:, :, 0:n]).then_inc(S["hT_sb"], 1)

            act.wait_ge(W["mod_out"], 16)
            squares(0)
            copy_hT(0)
            for t in range(NT):
                n = rows(t)
                if t + 1 < NT:
                    squares(t + 1)
                    copy_hT(t + 1)
                act.wait_ge(W["v_ps"], t + 1)
                dst = v_sb[:, t, :] if t < NT - 1 else vs_row[0:n, :]
                nc.scalar.copy(dst, psum[0:n, 4, :]).then_inc(S["v_done"], 1)
                for u in ([t - 1] if t >= 1 else []) + ([t] if t == NT - 1 else []):
                    m = rows(u)
                    for name, dst, dst_s, b in (("q", qT, qTs, 5), ("k", kT, kTs, 6)):
                        act.wait_ge(W[f"{name}T_ps"], u + 1)
                        to = dst[:, :, P * u:P * u + P] if u < NT - 1 else dst_s[:, :, :]
                        nc.scalar.mul(to, psum[:, b, :].rearrange("p (h n) -> p h n", h=HEADS)[:, :, 0:m],
                                      SCALE if name == "q" else 1.0).then_inc(S[f"{name}T_sb"], 1)

            for i in range(4):
                for tb in range(3):
                    n = 3 * i + tb
                    act.wait_ge(W["cv_ps"], n + 1)
                    if n >= 1:
                        act.wait_ge(W["cu_done"], n)
                    nc.scalar.copy(cg_sb[:, :], psum[:, 3 * (n % 2) + 1, 0:TB]).then_inc(S["cg_sb_s"], 1)
                    if tb == 0 and i >= 1:
                        act.wait_ge(W["conv_done"], 2 * i)
                    nc.scalar.copy(bg_sb[:, TB * tb:TB * tb + TB], psum[:, 3 * (n % 2), 0:TB]).then_inc(S["bg_sb_s"], 1)
            act.wait_ge(W["nc_ps"], 1)
            nc.scalar.copy(nc_row[:, :], psum[0:18, 7, :]).then_inc(S["nc_sb"], 1)

            pe2 = [pexp, pexp2]

            def exps(w, u):
                nk = P * (w // HEADS + 1)
                act.wait_ge(W["nmax_done"], 2 * w + u + 1)
                if w >= 2:
                    act.wait_ge(W["adiff_done"], w - 1)
                src = psum[:, 2 * u:2 * u + 2, :].rearrange("p b n -> p (b n)")[:, 0:nk]
                k = 2 * (w % 2) + u
                A(pe2[w % 2][:, u, 0:nk], src, ACT.Exp, bias=nm[:, k:k + 1], accum_out=ls[:, k:k + 1]).then_inc(S["exp_done"], 1)

            def head_squares(i):
                act.wait_ge(W["o_ps"], 4 * i + 4)
                if i >= 1:
                    act.wait_ge(W["att_done"], i)
                for h in range(HEADS):
                    if h or i:
                        act.wait_ge(W["ssqh_done"], 4 * i + h)
                    A(ajunk[:, 0:P], psum[:, 6 + i % 2, P * h:P * h + P], ACT.Square, scale=r1s[i % 2][:, h:h + 1],
                      accum_out=hss[:, h:h + 1]).then_inc(S["ssqh_done"], 1)

            def copy_attT(i):
                act.wait_ge(W["attT_ps"], i + 1)
                nc.scalar.copy(mixA[:, :, P * i:P * i + P], psum[:, 6 + i % 2, :].rearrange("p (h n) -> p h n", h=HEADS)).then_inc(S["attT_sb"], 1)

            act.wait_ge(W["cv_ps"], 12)
            exps(0, 0)
            exps(0, 1)
            for w in range(8 * HEADS):
                i, h = divmod(w, HEADS)
                if w + 1 < 8 * HEADS:
                    exps(w + 1, 0)
                act.wait_ge(W["adT_ps"], w + 1)
                nc.scalar.copy(adT[:, 0:i + 1, :], psum[:, 4:6, :].rearrange("p b (c n) -> p (b c) n", c=4)[:, 0:i + 1, :]).then_inc(S["adT_sb"], 1)
                if w + 1 < 8 * HEADS:
                    exps(w + 1, 1)
                if h == 1 and i >= 1:
                    head_squares(i - 1)
                if h == 3 and i >= 1:
                    copy_attT(i - 1)
            head_squares(7)
            copy_attT(7)

            for s in range(NSEQ):
                for p in range(PAGES):
                    n = s * PAGES + p
                    act.wait_ge(W["kp_ps"], n + 1)
                    if n >= 2:
                        act.wait_ge(W["dscore_ps"], n - 1)
                    nc.scalar.copy(kTp[n % 2][:, :, :], psum[:, 4 + n % 2, :].rearrange("p (c n) -> p c n", c=4)).then_inc(S["kp_sb"], 1)
                act.wait_ge(W["dmax_done"], s + 1)
                if s >= 2:
                    act.wait_ge(W["da_ps"], s - 1)
                b, m = s % 2, dmx[:, 3 + s % 2:4 + s % 2]
                A(pdec[b][:, 0:PAGES * P], psum[0:32, 2 * b:2 * b + 2, :].rearrange("p b n -> p (b n)"), ACT.Exp, bias=m,
                  accum_out=dl[:, 0:1]).then_inc(S["dexp_done"], 1)
                A(pdec[b][:, PAGES * P:], snew[b][:, :], ACT.Exp, bias=m, accum_out=dl[:, 1:2]).then_inc(S["dexp_done"], 1)
            act.wait_ge(W["do_ps"], NSEQ)
            for h in range(HEADS):
                nc.scalar.copy(orow[:, h, :], psum[32 * h:32 * h + 32, 6, P * h:P * h + P]).then_inc(S["oT_sb"], 1)
            act.wait_ge(W["oT_sb"], 4)
            for h in range(HEADS):
                if h:
                    act.wait_ge(W["ssqs_done"], h)
                A(ajunk[0:NSAMP, 0:P], orow[:, h, :], ACT.Square, accum_out=hss[0:NSAMP, h:h + 1]).then_inc(S["ssqs_done"], 1)
            act.wait_ge(W["attsT_ps"], 1)
            nc.scalar.copy(mixA[:, :, SEQ:TOK], psum[:, 5, 0:HEADS * NSAMP].rearrange("p (h n) -> p h n", h=HEADS)).then_inc(S["attsT_sb"], 1)

            def copy_h2T(t):
                n = rows(t)
                act.wait_ge(W["h2T_ps"], t + 1)
                if t >= 2:
                    act.wait_ge(W["lg_ps"], t - 1)
                nc.scalar.copy(h2T[t % 2][:, :, 0:n], psum[:, 4:6, :].rearrange("p b (c n) -> p (b c) n", c=4)[:, :, 0:n]).then_inc(S["h2T_sb"], 1)

            for t in range(NT):
                n = rows(t)
                if t >= 1:
                    copy_h2T(t - 1)
                act.wait_ge(W["x1_done"], 2 * t + 2)
                if t >= 1:
                    act.wait_ge(W["ssq2_done"], t)
                A(ojunk[0:n, :], x1[0:n, t, :], ACT.Square, accum_out=ss2[0:n, t:t + 1]).then_inc(S["ssq2_done"], 1)
            copy_h2T(NT - 1)

            act.wait_ge(W["gexp_in"], 1)
            A(R["ge"], R["gs"], ACT.Exp).then_inc(S["gexp_done"], 1)
            act.wait_ge(W["wexp_in"], 1)
            A(R["ee"], R["dd"], ACT.Exp).then_inc(S["wexp_done"], 1)

            act.wait_ge(W["plan_done"], 2)
            mid = act.value_load(plan[0:1, TCOLS:TCOLS + 1], min_val=NE // 2 - 2, max_val=MAXT // 2 - 2)

            def lead_gate_up(j, b, i):
                for g in range(2):
                    act.wait_ge(W[f"{('wgate', 'wup')[g]}_in{b}"], 16 * i + 16)
                    nc.scalar.copy(r32(wguH[b][:, g, :, :]), wgu[b][:, g, :, :]).then_inc(S["wguH_done"], 1)

            def lead_rows(b):
                nc.scalar.copy(r32(xgH[b][:, :, :]), psum[:, 0:2, :].rearrange("p b (c n) -> p (b c) n", c=4)).then_inc(S["xgH_done"], 1)

            def copy_y(j, b, i, stored):
                act.wait_ge(W["y_ps"], j + 1)
                if stored:
                    act.wait_ge(W[f"y_out{b}"], 16 * i)
                nc.scalar.copy(yrow[b][:, :], psum[:, 5:7, :].rearrange("p b n -> p (b n)")).then_inc(S["y_done"], 1)

            def expert_copies(j, b, i, first, left):
                if left:
                    lead_gate_up(j + 1, 1 - b, i + b)
                act.wait_ge(W["gu_ps"], j + 1)
                A(th[b][:, :], psum[:, 2 + b, 0:FE], ACT.Tanh, scale=0.5).then_inc(S["th_done"], 1)
                if left:
                    act.wait_ge(W["xgT_ps"], j + 2)
                    lead_rows(1 - b)
                act.wait_ge(W[f"wdn_in{b}"], 16 * i + 16)
                nc.scalar.copy(r32(wdnH[b][:, :, :]), wdn[b][:, :, :]).then_inc(S["wdnH_done"], 1)
                if not (first and b == 0):
                    copy_y(j - 1, 1 - b, i - 1 + b, not first)
                act.wait_ge(W["hidT_ps"], j + 1)
                nc.scalar.copy(r32(hidH[b][:, :, :]), psum[:, 4, 0:FE].rearrange("p (c n) -> p c n", c=FC)).then_inc(S["hidH_done"], 1)

            lead_gate_up(0, 0, 0)
            act.wait_ge(W["xgT_ps"], 1)
            lead_rows(0)
            expert_steps(act, expert_copies, mid)
            copy_y(2 * mid + 3, 1, mid + 1, True)

            def scaled(t):
                n = rows(t)
                act.wait_ge(W[f"yg_in{t % 3}"], 32 * (t // 3 + 1))
                y0 = yg[t % 3][0][0:n, :]
                nc.scalar.mul(y0, y0, cw[0:n, 0, t:t + 1]).then_inc(S["scaled_done"], 1)

            scaled(0)
            for t in range(NT):
                n = rows(t)
                if t + 1 < NT:
                    scaled(t + 1)
                act.wait_ge(W["comb_done"], t + 1)
                if t >= 1:
                    act.wait_ge(W["ssq3_done"], t)
                A(fjunk[0:n, :], x1[0:n, t, :], ACT.Square, accum_out=ss2[0:n, t:t + 1]).then_inc(S["ssq3_done"], 1)

        @block.vector
        def _(dve):
            TT, TS, STT = nc.vector.tensor_tensor, nc.vector.tensor_scalar, nc.vector.scalar_tensor_tensor
            RED = nc.vector.tensor_reduce
            steps = [0]

            def link(ins):
                steps[0] += 1
                ins.then_inc(S["dve_step"], 1)
                dve.wait_ge(S["dve_step"], steps[0])

            dve.wait_ge(W["cond_th"], 1)
            STT(cond[:, :], cth[:, :], 1.0, cond[:, :], ALU.add, ALU.mult).then_inc(S["cond_act"], 1)
            dve.wait_ge(W["lam_in"], 80)
            l4 = small[:, 87:89]
            link(TT(lamv[:, 0:4:2, :], lamv[:, 0:4:2, :], lamv[:, 1:4:2, :], ALU.mult))
            RED(l4, lamv[:, 0:4:2, :], AX_X, ALU.add).then_inc(S["lam_done"], 1)
            dve.wait_ge(W["condT_ps"], 1)
            TS(condT[:, :, :], psum[:, 7, 0:DC * 9].rearrange("p (c s) -> p c s", c=DC), 0.5, None, ALU.mult).then_inc(S["condT_sb"], 1)
            dve.wait_ge(W["lam_exp"], 1)
            link(TT(neglam, small[:, 86:87], small[:, 85:86], ALU.subtract))
            link(TS(neglam, neglam, -LAM_INIT, None, ALU.add))
            link(TS(gsub, gsub, 1.0 - LAM_INIT, None, ALU.mult))
            dve.wait_ge(W["const_in"], 16)
            link(STT(sgn, C("sub1", 32), neglam[0:32, :], C("sub0", 32), ALU.mult, ALU.add))
            dve.wait_ge(W["bias_in"], 48)
            for b in range(12):
                dve.wait_ge(W["ada_ps"], b + 1)
                a = slice(512 * b, 512 * b + 512)
                TT(mod[:, a], psum[0:9, b % 2, :], bada[:, a], ALU.add).then_inc(S["ada_sb"], 1)
            dve.wait_ge(W["ada_sb"], 12)
            for name, ln in (("scale_a", lnm), ("scale_f", lnf)):
                a = slice(MOD[name] * D, MOD[name] * D + D)
                STT(mod[:, a], mod[:, a], 1.0, ln[:, :], ALU.add, ALU.mult).then_inc(S["ada_sb"], 1)

            def mod_row(t, which):
                return (which[0] if t < NT - 1 else which[1])[0:rows(t), :]

            def make_h(t):
                n = rows(t)
                dve.wait_ge(W["rstd_done"], t + 1)
                if t >= 2:
                    dve.wait_ge(W["hT_ps"], t - 1)
                h = hrow[t % 2][0:n, :]
                link(STT(h, xin[t % 2][0:n, :], rstd[0:n, t:t + 1], mod_row(t, (scale_p, scale_s)), ALU.mult, ALU.mult))
                TT(h, h, mod_row(t, (shift_p, shift_s)), ALU.add).then_inc(S["h_done"], 1)

            def rotate(t, name, b, row):
                n = rows(t)
                dve.wait_ge(W[f"{name}_ps"], t + 1)
                if t >= 2:
                    dve.wait_ge(W[f"{name}T_ps"], t - 1)
                    if name == "k":
                        dve.wait_ge(W[f"kv_out{t % 2}"], 32 * (t // 2))
                src = psum[0:n, b, :].rearrange("p (s u d) -> p s u d", s=SUBS, u=2)
                dst = row[t % 2][0:n, :].rearrange("p (s u d) -> p s u d", s=SUBS, u=2)
                tmp = ropet[0:n, :].rearrange("p (s u d) -> p s u d", s=SUBS, u=2)
                cos, nsin, sin = (rope[0:n, t, 32 * k:32 * k + 32] for k in range(3))
                TT(dst, src, bc(cos, [n, SUBS, 2, 32], (1, 1)), ALU.mult)
                TT(tmp[:, :, 0, :], src[:, :, 1, :], bc(nsin, [n, SUBS, 32], (1,)), ALU.mult)
                link(TT(tmp[:, :, 1, :], src[:, :, 0, :], bc(sin, [n, SUBS, 32], (1,)), ALU.mult))
                TT(dst, dst, tmp, ALU.add).then_inc(S[f"{name}_done"], 1)
                dve.wait_ge(W[f"{name}_done"], t + 1)

            dve.wait_ge(W["mix_rows_in"], 2 * ROWSEMS)
            make_h(0)
            for t in range(NT):
                if t + 1 < NT:
                    make_h(t + 1)
                rotate(t, "q", 2, qrow)
                rotate(t, "k", 3, krow)

            dve.wait_ge(W["state_ps"], 1)
            samples = cuT[:, :, 2 + SEQ:].rearrange("p c (s n) -> p c s n", s=NSEQ)
            nc.vector.memset(cuT[:, :, 0:2], 0.0)
            nc.vector.tensor_copy(samples[:, :, :, 0:2], psum[:, 6, 0:64].rearrange("p (c s n) -> p c s n", c=4, s=NSEQ)).then_inc(S["state_sb_s"], 1)
            nc.vector.tensor_copy(wcvT[:, :, 0:3], psum[:, 6, 64:80].rearrange("p (c k) -> p c k", c=4)[:, :, 0:3]).then_inc(S["state_sb_s"], 1)
            dve.wait_ge(W["state_sb_s"], 2)
            for i in range(4):
                for tb in range(3):
                    n = 3 * i + tb
                    dve.wait_ge(W["cg_sb_s"], n + 1)
                    src = psum[:, 3 * (n % 2) + 2, 0:TB]
                    m = TB if tb < 2 else TB - NSAMP
                    dst = cuT[:, i, 2 + TB * tb:2 + TB * tb + m]
                    last = TT(dst, src[:, 0:m], cg_sb[:, 0:m], ALU.mult)
                    if tb == 2:
                        last = TT(samples[:, i, :, 2:], src[:, m:].rearrange("p (s n) -> p s n", s=NSEQ),
                                  cg_sb[:, m:].rearrange("p (s n) -> p s n", s=NSEQ), ALU.mult)
                    last.then_inc(S["cu_done"], 1)
                dve.wait_ge(W["cu_done"], 3 * i + 3)
                dve.wait_ge(W["bg_sb_s"], 3 * i + 3)
                if i:
                    dve.wait_ge(W["conv_done"], 2 * i)
                for part in range(2):
                    if part == 0:
                        tap = [cuT[:, i, k:k + SEQ] for k in range(3)]
                        acc, gate, dst = ctmp[:, 0:SEQ], bg_sb[:, 0:SEQ], mixC[:, i, 0:SEQ]
                    else:
                        tap = [samples[:, i, :, k:k + LNEW] for k in range(3)]
                        acc, gate, dst = (v.rearrange("p (s n) -> p s n", s=NSEQ) for v in
                                          (ctmp[:, SEQ:TOK], bg_sb[:, SEQ:TOK], mixC[:, i, SEQ:TOK]))
                    link(TS(acc, tap[0], wcvT[:, i, 0:1], None, ALU.mult))
                    link(STT(acc, tap[1], wcvT[:, i, 1:2], acc, ALU.mult, ALU.add))
                    link(STT(acc, tap[2], wcvT[:, i, 2:3], acc, ALU.mult, ALU.add))
                    TT(dst, acc, gate, ALU.mult).then_inc(S["conv_done"], 1)
            nc.vector.tensor_copy(ncT[:, :, 0:2], cuT[:, :, SEQ:SEQ + 2])
            nc.vector.tensor_copy(ncT[:, :, 2:].rearrange("p c (s n) -> p c s n", s=NSEQ), samples[:, :, :, LNEW:]).then_inc(S["ncT_done"], 1)
            dve.wait_ge(W["conv_done"], 8)
            dve.wait_ge(W["qT_sb"], NT)
            link(nc.vector.memset(qbd[:, :, :, :], 0.0))
            for c in range(4):
                for u in range(2):
                    r = slice(64 * u, 64 * u + 64)
                    a = 8 * c + 4 * u
                    last = nc.vector.tensor_copy(qbd[r, :, c, a:a + LNEW], qTs[r, c, :].rearrange("p (s q) -> p s q", s=NSEQ))
            last.then_inc(S["qbd_done"], 1)

            scores = psum[:, 0:4, :].rearrange("p (s b) n -> p s (b n)", s=2)

            def maxima(w, u):
                i = w // HEADS
                dve.wait_ge(W["s_ps"], 2 * w + u + 1)
                diag = scores[:, u, P * i:P * i + P]
                TT(diag, diag, C("mask"), ALU.add).then_inc(S["mask_done"], 1)
                dve.wait_ge(W["mask_done"], 2 * w + u + 1)
                k = 2 * (w % 2) + u
                RED(nm[:, k:k + 1], scores[:, u, 0:P * (i + 1)], AX_X, ALU.max, negate=True).then_inc(S["nmax_done"], 1)

            def attention_rows(i):
                dve.wait_ge(W["rstdh_done"], i + 1)
                if i >= 1:
                    dve.wait_ge(W["attT_ps"], i)
                link(TT(hsc, r1s[i % 2], hrs, ALU.mult))
                for h in range(HEADS):
                    last = STT(attrow[:, P * h:P * h + P], psum[:, 6 + i % 2, P * h:P * h + P], hsc[:, h:h + 1], gsub, ALU.mult, ALU.mult)
                last.then_inc(S["att_done"], 1)

            maxima(0, 0)
            maxima(0, 1)
            for w in range(8 * HEADS):
                i, h = divmod(w, HEADS)
                if w + 1 < 8 * HEADS:
                    maxima(w + 1, 0)
                dve.wait_ge(W["exp_done"], 2 * w + 2)
                l0, l1 = ls[:, 2 * (w % 2):2 * (w % 2) + 1], ls[:, 2 * (w % 2) + 1:2 * (w % 2) + 2]
                nc.vector.reciprocal(r1s[i % 2][:, h:h + 1], l0)
                link(nc.vector.reciprocal(rl[:, 0:1], l1))
                link(STT(ratio, rl[:, 0:1], l0, neglam, ALU.mult, ALU.mult))
                if w >= 1:
                    dve.wait_ge(W["adT_ps"], w)
                nk = P * (i + 1)
                p2 = (pexp, pexp2)[w % 2]
                STT(adiff[:, 0:nk], p2[:, 1, 0:nk], ratio, p2[:, 0, 0:nk], ALU.mult, ALU.add).then_inc(S["adiff_done"], 1)
                if w + 1 < 8 * HEADS:
                    maxima(w + 1, 1)
                if h == 1 and i >= 1:
                    attention_rows(i - 1)
            attention_rows(7)

            def sample_maxima(s):
                b = s % 2
                dve.wait_ge(W["ds_ps"], s + 1)
                TT(snew[b][:, :], psum[0:32, 7, 256:256 + LNEW], C("dmask", 32), ALU.add).then_inc(S["dnew_done"], 1)
                dve.wait_ge(W["dnew_done"], s + 1)
                RED(dmx[:, 0:1], psum[0:32, 2 * b:2 * b + 2, :].rearrange("p b n -> p (b n)"), AX_X, ALU.max)
                link(RED(dmx[:, 1:2], snew[b][:, :], AX_X, ALU.max))
                link(TT(dmx[:, 2:3], dmx[:, 0:1], dmx[:, 1:2], ALU.max))
                TS(dmx[:, 3 + b:4 + b], dmx[:, 2:3], -1.0, None, ALU.mult).then_inc(S["dmax_done"], 1)

            def sample_weights(s):
                b = s % 2
                dve.wait_ge(W["da_ps"], s + 1)
                seq = [aTs[b][:, :, :].rearrange("p n (h x) -> p n h x", h=HEADS)[:, :, :, LNEW * r:LNEW * r + LNEW] for r in (s - 2, s)] if s >= 2 else [
                    None, aTs[b][:, :, :].rearrange("p n (h x) -> p n h x", h=HEADS)[:, :, :, LNEW * s:LNEW * s + LNEW]]
                if s >= 2:
                    dve.wait_ge(W["do_ps"], s - 1)
                    nc.vector.memset(seq[0], 0.0)
                nc.vector.tensor_copy(seq[1][:, 0:PAGES], psum[:, 7, 0:16 * PAGES].rearrange("p (n h q) -> p n h q", n=PAGES, h=HEADS))
                nc.vector.tensor_copy(seq[1][0:LNEW, PAGES], psum[0:LNEW, 7, 16 * PAGES:16 * PAGES + 16].rearrange("p (h q) -> p h q", h=HEADS)).then_inc(S["da_sb"], 1)

            def sample_pairs(s):
                dve.wait_ge(W["dexp_done"], 2 * s + 2)
                link(TT(dl[:, 2:3], dl[:, 0:1], dl[:, 1:2], ALU.add))
                link(nc.vector.reciprocal(dr[:, 0:1], dl[:, 2:3]))
                link(TT(dr[:, 1:2], dr[:, 0:1], sgn, ALU.mult))
                TS(pairs[s % 2][:, :], C("pair", 32), dr[:, 1:2], None, ALU.mult).then_inc(S["pair_done"], 1)

            dve.wait_ge(W["attT_ps"], 8)
            for b in range(2):
                link(nc.vector.memset(aTs[b][:, :, :], 0.0))
            for s in range(NSEQ):
                sample_maxima(s)
                if s >= 1:
                    sample_weights(s - 1)
                sample_pairs(s)
            sample_weights(NSEQ - 1)
            dve.wait_ge(W["rstds_done"], 1)
            for h in range(HEADS):
                last = STT(attrow[0:NSAMP, P * h:P * h + P], orow[:, h, :], hrs[0:NSAMP, h:h + 1],
                           gsub[0:NSAMP, :], ALU.mult, ALU.mult)
            last.then_inc(S["atts_done"], 1)

            def make_h2(t):
                n = rows(t)
                dve.wait_ge(W["rstd2_done"], t + 1)
                if t >= 2:
                    dve.wait_ge(W["h2T_ps"], t - 1)
                    dve.wait_ge(W[f"h2_out{t % 2}"], 16 * (t // 2))
                h = h2row[t % 2][0:n, :]
                link(STT(h, x1[0:n, t, :], rs2[0:n, t:t + 1], mod_row(t, (scale_p, scale_s)), ALU.mult, ALU.mult))
                TT(h, h, mod_row(t, (shift_p, shift_s)), ALU.add).then_inc(S["h2_done"], 1)

            def take_logits(t):
                n = rows(t)
                dve.wait_ge(W["lg_ps"], t + 1)
                TT(logit[0:n, t, :], psum[0:n, 6, 0:NG + NE], brt[0:n, :], ALU.add).then_inc(S["lg_done"], 1)

            dve.wait_ge(W["attsT_ps"], 1)
            dve.wait_ge(W["wout_in"], 80)
            link(nc.vector.memset(logit[:, NT - 1, :], 0.0))
            dve.wait_ge(W["ffn_rows_in"], 2 * ROWSEMS)
            dve.wait_ge(W["gate_rows_in"], ROWSEMS)
            dve.wait_ge(W["xres_in"], 16 * NT)
            for t in range(NT):
                n = rows(t)
                if t >= 1:
                    make_h2(t - 1)
                for j in range(2):
                    a = slice(512 * j, 512 * j + 512)
                    dve.wait_ge(W["mix_ps"], 2 * t + j + 1)
                    if t or j:
                        dve.wait_ge(W["x1_done"], 2 * t + j)
                    link(TT(otmp[0:n, :], psum[0:n, 2 * (t % 2) + j, :], mod_row(t, (gate_ap, gate_as))[:, a], ALU.mult))
                    TT(x1[0:n, t, a], x1[0:n, t, a], otmp[0:n, :], ALU.add).then_inc(S["x1_done"], 1)
                if t >= 2:
                    take_logits(t - 2)
            make_h2(NT - 1)
            take_logits(NT - 2)
            take_logits(NT - 1)

            dve.wait_ge(W["lg_done"], NT)
            dve.wait_ge(W["h2T_ps"], NT)
            dve.wait_ge(W["h2_out0"], 16 * 5)
            dve.wait_ge(W["h2_out1"], 16 * 4)
            nc.vector.memset(ones[:, :], 1.0)
            r3 = lambda n, k: R[n].rearrange("p (t e) -> p t e", e=k)
            LG, LE = logit[:, :, 0:NG], logit[:, :, NG:NG + NE]
            iota4, iota32 = C("iota")[:, 0:NG], C("iota")[:, 0:NE]

            def first_max(eq, oh, scores_, top, k, iota, mn):
                link(RED(top, scores_, AX_X, ALU.max))
                link(TT(eq, scores_, bc(top, [P, NT, k], (2,)), ALU.is_equal))
                link(STT(eq, eq, -64.0, bc(iota, [P, NT, k], (1,)), ALU.mult, ALU.add))
                link(RED(mn, eq, AX_X, ALU.min))
                link(TT(oh, eq, bc(mn, [P, NT, k], (2,)), ALU.is_equal))

            first_max(r3("eq4", NG), r3("ohg", NG), LG, R["gm"], NG, iota4, R["mn"])
            TT(r3("gs", NG), LG, bc(R["gm"], [P, NT, NG], (2,)), ALU.subtract).then_inc(S["gexp_in"], 1)
            link(TS(R["pen"], R["ohg"], -NEG, NEG, ALU.mult, ALU.add))
            el4 = R["el"].rearrange("p (t g e) -> p t g e", g=NG, e=EPG)
            link(TT(el4, LE.rearrange("p t (g e) -> p t g e", g=NG), bc(r3("pen", NG), [P, NT, NG, EPG], (3,)), ALU.add))
            first_max(r3("ta", NE), r3("oh1", NE), r3("el", NE), R["m1"], NE, iota32, R["mn"])
            link(STT(r3("el", NE), r3("oh1", NE), 2 * NEG, r3("el", NE), ALU.mult, ALU.add))
            first_max(r3("ta", NE), r3("oh2", NE), r3("el", NE), R["m2"], NE, iota32, R["mn"])
            TT(R["dd"], R["m2"], R["m1"], ALU.subtract).then_inc(S["wexp_in"], 1)
            for k in ("oh1", "oh2"):
                link(TT(r3(k, NE), r3(k, NE), bc(C("valid"), [P, NT, NE], (2,)), ALU.mult))
            TT(R["ohs"], R["oh1"], R["oh2"], ALU.add).then_inc(S["oh_done"], 1)
            dve.wait_ge(W["gexp_done"], 1)
            link(RED(R["gsum"], r3("ge", NG), AX_X, ALU.add))
            link(nc.vector.reciprocal(R["gp"], R["gsum"]))
            dve.wait_ge(W["wexp_done"], 1)
            link(TS(R["ws"], R["ee"], 1.0, None, ALU.add))
            link(nc.vector.reciprocal(R["ws"], R["ws"]))
            link(TT(cw[:, 0, :], R["ws"], R["gp"], ALU.mult))
            link(TT(cw[:, 1, :], cw[:, 0, :], R["ee"], ALU.mult))
            dve.wait_ge(W["cnt_ps"], 1)
            base, tot = r3("base", NE), psum[:, 1, 0:NT * NE].rearrange("p (t e) -> p t e", e=NE)
            link(nc.vector.memset(base[:, 0, :], 0.0))
            for t in range(1, NT):
                link(TT(base[:, t, :], tot[:, t - 1, :], base[:, t - 1, :], ALU.add))
            link(TT(R["cnt"], tot[:, NT - 1, :], base[:, NT - 1, :], ALU.add))
            link(nc.vector.memset(R["nt"], 1.0))
            for q in range(1, (TOK + P - 1) // P):
                link(STT(R["nt"], R["cnt"], float(P * q), R["nt"], ALU.is_gt, ALU.add))
            cur, nxt = "inca", "incb"
            link(nc.vector.tensor_copy(R[cur], R["nt"]))
            for d in (1, 2, 4, 8, 16):
                nc.vector.tensor_copy(R[nxt][:, 0:d], R[cur][:, 0:d])
                link(TT(R[nxt][:, d:], R[cur][:, d:], R[cur][:, 0:NE - d], ALU.add))
                cur, nxt = nxt, cur
            inc = R[cur]
            link(TT(R["first"], inc, R["nt"], ALU.subtract))
            link(TT(base, psum[:, 0, 0:NT * NE].rearrange("p (t e) -> p t e", e=NE), base, ALU.add))
            link(STT(base, bc(R["first"], [P, NT, NE], (1,)), float(P), base, ALU.mult, ALU.add))
            slot = R["slot"].rearrange("p (t k) -> p t k", k=2)
            for k, name in enumerate(("oh1", "oh2")):
                link(TT(r3("ta", NE), r3(name, NE), base, ALU.mult))
                link(RED(slot[:, :, k], r3("ta", NE), AX_X, ALU.add))
            link(nc.vector.tensor_copy(slot_i[:, :], R["slot"]))
            flat_i = slot_i[:, :]
            link(TS(slot_lo[:, :], flat_i, P - 1, None, ALU.bitwise_and))
            link(TS(slot_hi[:, :], flat_i, 7, None, ALU.logical_shift_right))
            link(nc.vector.tensor_copy(R["lo"], slot_lo[:, :]))
            link(nc.vector.tensor_copy(R["hi"], slot_hi[:, :]))
            for n in range(2 * NT):
                if n >= 4:
                    dve.wait_ge(W["map_ps"], n - 3)
                TS(lsel[n % 4][:, :], C("iota"), R["lo"][:, n:n + 1], None, ALU.is_equal)
                TS(hsel[n % 4][:, :], C("iota")[:, 0:TCOLS], R["hi"][:, n:n + 1], C("tokid")[:, n:n + 1],
                   ALU.is_equal, ALU.mult).then_inc(S["sel_done"], 1)
            g3 = grid[:, :].rearrange("p (j e) -> p j e", e=NE)
            link(TT(g3, bc(inc[0:1, :], [1, TCOLS, NE], (1,)), bc(C("iota", 1)[:, 0:TCOLS], [1, TCOLS, NE], (2,)), ALU.is_le))
            tfl = R["tfl"][0:1, :]
            link(RED(tfl, g3, AX_X, ALU.add))
            link(TS(tfl, tfl, float(NE - 1), None, ALU.min))
            nc.vector.tensor_copy(plan[0:1, 0:TCOLS], tfl).then_inc(S["plan_done"], 1)
            link(TS(R["mn"][0:1, 0:1], inc[0:1, NE - 1:NE], -3.0, None, ALU.add))
            link(nc.vector.tensor_copy(plan[0:1, TCOLS + 1:TCOLS + 2], R["mn"][0:1, 0:1]))
            TS(plan[0:1, TCOLS:TCOLS + 1], plan[0:1, TCOLS + 1:TCOLS + 2], 1, None, ALU.logical_shift_right).then_inc(S["plan_done"], 1)
            dve.wait_ge(W["map_ps"], 2 * NT)
            link(TS(vmap[:, 0, :], psum[:, 2, 0:TCOLS], 0.0, float(NOROW), ALU.is_equal, ALU.mult))
            link(TS(vmap[:, 1, :], psum[:, 2, 0:TCOLS], TOK + 0.5, float(-TOK), ALU.is_gt, ALU.mult))
            link(STT(vmap[:, 0, :], psum[:, 2, 0:TCOLS], -1.0, vmap[:, 0, :], ALU.add, ALU.add))
            link(TT(vmap[:, 1, :], vmap[:, 1, :], vmap[:, 0, :], ALU.add))
            link(nc.vector.tensor_copy(xrow[:, :], vmap[:, 1, :]))
            nc.vector.tensor_copy(yidx[:, :], vmap[:, 0, :]).then_inc(S["plan_done"], 1)

            mid = dve.value_load(plan[0:1, TCOLS:TCOLS + 1], min_val=NE // 2 - 2, max_val=MAXT // 2 - 2)

            def rest_gate_up(j, b, g):
                dve.wait_ge(W["wguH_done"], 2 * j + g + 1)
                TT(r32(wguL[b][:, g, :, :]), wgu[b][:, g, :, :], wguH[b][:, g, :, :], ALU.subtract).then_inc(S["wguL_done"], 1)

            def rest_rows(j, b):
                dve.wait_ge(W["xgH_done"], j + 1)
                TT(r32(xgL[b][:, :, :]), psum[:, 0:2, :].rearrange("p b (c n) -> p (b c) n", c=4), xgH[b][:, :, :],
                   ALU.subtract).then_inc(S["xgL_done"], 1)

            def expert_rests(j, b, i, first, left):
                if left:
                    rest_gate_up(j + 1, 1 - b, 0)
                dve.wait_ge(W["th_done"], j + 1)
                STT(gated[b][:, :], th[b][:, :], 1.0, psum[:, 2 + b, 0:FE], ALU.add, ALU.mult).then_inc(S["m_dve_step"], 1)
                dve.wait_ge(S["m_dve_step"], j + 1)
                STT(hid[b][:, :], gated[b][:, :], 0.5, psum[:, 2 + b, FE:2 * FE], ALU.mult, ALU.mult).then_inc(S["hid_done"], 1)
                if left:
                    rest_gate_up(j + 1, 1 - b, 1)
                    rest_rows(j + 1, 1 - b)
                dve.wait_ge(W["wdnH_done"], j + 1)
                TT(r32(wdnL[b][:, :, :]), wdn[b][:, :, :], wdnH[b][:, :, :], ALU.subtract).then_inc(S["wdnL_done"], 1)
                dve.wait_ge(W["hidH_done"], j + 1)
                TT(r32(hidL[b][:, :, :]), psum[:, 4, 0:FE].rearrange("p (c n) -> p c n", c=FC), hidH[b][:, :, :],
                   ALU.subtract).then_inc(S["hidL_done"], 1)

            for g in range(2):
                rest_gate_up(0, 0, g)
            rest_rows(0, 0)
            expert_steps(dve, expert_rests, mid)

            def finish(t):
                n = rows(t)
                dve.wait_ge(W["rstd3_done"], t + 1)
                if t >= 2:
                    dve.wait_ge(W[f"fin_out{t % 2}"], 16 * (t // 2))
                STT(fin[t % 2][0:n, :], x1[0:n, t, :], rs2[0:n, t:t + 1], lnfin[0:n, :], ALU.mult, ALU.mult).then_inc(S["fin_done"], 1)

            dve.wait_ge(W["fin_rows_in"], ROWSEMS + 16)
            for t in range(NT):
                n = rows(t)
                dve.wait_ge(W["scaled_done"], t + 1)
                y0, y1 = yg[t % 3][0][0:n, :], yg[t % 3][1][0:n, :]
                link(STT(y0, y1, cw[0:n, 1, t:t + 1], y0, ALU.mult, ALU.add))
                link(TT(y0, y0, mod_row(t, (gate_fp, gate_fs)), ALU.mult))
                TT(x1[0:n, t, :], x1[0:n, t, :], y0, ALU.add).then_inc(S["comb_done"], 1)
                if t >= 1:
                    finish(t - 1)
            finish(NT - 1)

        @block.gpsimd
        def _(pool):
            steps = [0]

            def link(ins):
                steps[0] += 1
                ins.then_inc(S["pool_step"], 1)
                pool.wait_ge(S["pool_step"], steps[0])

            def inverse_root(dst, src, width, eps, done):
                link(nc.gpsimd.tensor_scalar(src, src, 1.0 / width, eps, ALU.mult, ALU.add))
                n, m = src.shape
                nc.gpsimd.tensor_tensor(dst, src, C("half", n).to_broadcast([n, m]), ALU.pow).then_inc(done, 1)

            pool.wait_ge(W["ada_sb"], 14)
            pool.dma_start(mod_dram, mod[:, :]).then_inc(S["mod_out"], 16)

            def root(t):
                n = rows(t)
                pool.wait_ge(W["ssq_done"], t + 1)
                inverse_root(rstd[0:n, t:t + 1], ssq[0:n, t:t + 1], D, NORM_EPS, S["rstd_done"])

            root(0)
            root(1)
            for t in range(NT):
                n = rows(t)
                pool.wait_ge(W["k_done"], t + 1)
                pool.wait_ge(W["v_done"], t + 1)
                ko, vo = (kp_out[P * t:P * t + P, :], vp_out[P * t:P * t + P, :]) if t < NT - 1 else (ks_out, vs_out)
                pool.dma_start(ko, krow[t % 2][0:n, :]).then_inc(S[f"kv_out{t % 2}"], 16)
                pool.dma_start(vo, v_sb[:, t, :] if t < NT - 1 else vs_row[0:n, :]).then_inc(S[f"kv_out{t % 2}"], 16)
                if t + 2 < NT:
                    root(t + 2)

            pool.wait_ge(W["nc_sb"], 1)
            pool.dma_start(cp_out, nc_row[0:2, :]).then_inc(S["nc_out"], 16)
            pool.dma_start(cs_out, nc_row[2:18, :]).then_inc(S["nc_out"], 16)

            def pad_queries(i):
                if i >= 2:
                    pool.wait_ge(W["s_ps"], 8 * (i - 1))
                link(nc.gpsimd.tensor_copy(qz[i % 2][0:64, 0, :, :], qT[0:64, :, P * i:P * i + P]))
                nc.gpsimd.tensor_copy(qz[i % 2][64:P, 1, :, :], qT[64:P, :, P * i:P * i + P]).then_inc(S["qz_done"], 1)
                pool.wait_ge(W["qz_done"], i + 1)

            pool.wait_ge(W["cv_ps"], 12)
            for i in range(2):
                link(nc.gpsimd.memset(qz[i][64:P, 0, :, :], 0.0))
                link(nc.gpsimd.memset(qz[i][0:64, 1, :, :], 0.0))
                pad_queries(i)
            for i in range(8):
                if i + 1 < 8 and i >= 1:
                    pool.wait_ge(W["rstdh_done"], i)
                    pad_queries(i + 1)
                pool.wait_ge(W["ssqh_done"], 4 * i + 4)
                inverse_root(hrs, hss, P, SUBLN_EPS, S["rstdh_done"])
            pool.wait_ge(W["ssqs_done"], 4)
            inverse_root(hrs[0:NSAMP, :], hss[0:NSAMP, :], P, SUBLN_EPS, S["rstds_done"])

            for t in range(NT):
                n = rows(t)
                pool.wait_ge(W["ssq2_done"], t + 1)
                inverse_root(rs2[0:n, t:t + 1], ss2[0:n, t:t + 1], D, NORM_EPS, S["rstd2_done"])
                pool.wait_ge(W["h2_done"], t + 1)
                pool.dma_start(h2_dram[P * t:P * t + n, :], h2row[t % 2][0:n, :]).then_inc(S[f"h2_out{t % 2}"], 16)

            pool.wait_ge(W["x1_done"], 2 * NT)
            for b in range(2):
                link(nc.gpsimd.memset(xg[b][:, :], 0.0))
            pool.wait_ge(W["h2_out0"], 16 * 5)
            pool.wait_ge(W["h2_out1"], 16 * 4)
            pool.wait_ge(W["plan_done"], 3)
            mid = pool.value_load(plan[0:1, TCOLS:TCOLS + 1], min_val=NE // 2 - 2, max_val=MAXT // 2 - 2)

            def gather_rows(j, b):
                nc.gpsimd.tensor_copy(gidx[b][:, :], xrow[:, bass.ds(j, 1)]).then_inc(S["gidx_done"], 1)
                pool.wait_ge(W["gidx_done"], j + 1)
                pool.sem_inc(S["go_on"], 1)
                nc.gpsimd.indirect_dma_start(xg[b][:, :], None, h2_dram, bass.IndirectOffsetOnAxis(ap=gidx[b][:, 0:1], axis=0),
                                             bounds_check=TOK - 1, oob_is_err=False).then_inc(S[f"xg_in{b}"], 16)

            def scatter_rows(j, b):
                pool.wait_ge(W["y_done"], j + 1)
                pool.sem_inc(S["go_on"], 1)
                nc.gpsimd.tensor_copy(sidx[b][:, :], yidx[:, bass.ds(j, 1)]).then_inc(S["sidx_done"], 1)
                pool.wait_ge(W["sidx_done"], j + 1)
                pool.sem_inc(S["go_on"], 1)
                nc.gpsimd.indirect_dma_start(y_dram, bass.IndirectOffsetOnAxis(ap=sidx[b][:, 0:1], axis=0), yrow[b][:, :], None,
                                             bounds_check=2 * TOK - 1, oob_is_err=False).then_inc(S[f"y_out{b}"], 16)

            def move_rows(j, b, i, first, left):
                if left == 2:
                    pool.wait_ge(W["xgT_ps"], j + 1)
                    pool.sem_inc(S["go_on"], 1)
                    gather_rows(j + 2, b)
                if not (first and b == 0):
                    scatter_rows(j - 1, 1 - b)

            gather_rows(0, 0)
            gather_rows(1, 1)
            expert_steps(pool, move_rows, mid)
            scatter_rows(2 * mid + 3, 1)

            for t in range(NT):
                n = rows(t)
                pool.wait_ge(W["ssq3_done"], t + 1)
                inverse_root(rs2[0:n, t:t + 1], ss2[0:n, t:t + 1], D, NORM_EPS, S["rstd3_done"])


_INS = ['x_prompt', 'x_sample', 'cache_k', 'cache_v', 'state_conv', 'page_table', 'c_prompt', 'c_sample',
        'w_ada', 'b_ada', 'ln_mix', 'w_in', 'lam_q1', 'lam_k1', 'lam_q2', 'lam_k2', 'subln_g', 'w_conv', 'w_out',
        'ln_ffn', 'w_router_grp', 'b_router_grp', 'w_router_exp', 'b_router_exp', 'w_gate', 'w_up', 'w_down', 'ln_final']
_OUTS = [(1, SEQ, D), (NSEQ, LNEW, D), (1, 1, SEQ, SUBS, HD), (1, 1, SEQ, HEADS, 2 * HD), (1, 1, 2, AW),
         (1, NSEQ, LNEW, SUBS, HD), (1, NSEQ, LNEW, HEADS, 2 * HD), (1, NSEQ, 2, AW)]


def kernel(**inputs):
    import concourse.bacc as _bacc
    from concourse.bass_utils import run_bass_kernel_spmd as _run

    nc = _bacc.Bacc("TRN2", target_bir_lowering=False, num_devices=1)
    arrays, args = {"in_consts_dram": constants()}, []
    args.append(nc.dram_tensor("in_consts_dram", [P, NCONST], F32, kind="ExternalInput").ap())
    for name in _INS:
        a = np.ascontiguousarray(inputs[name])
        arrays[f"in_{name}_dram"] = a
        args.append(nc.dram_tensor(f"in_{name}_dram", a.shape, mybir.dt.from_np(a.dtype), kind="ExternalInput").ap())
    for i, shape in enumerate(_OUTS):
        args.append(nc.dram_tensor(f"out_{i}_dram", shape, F32, kind="ExternalOutput").ap())
    args.append(nc.dram_tensor("mod_scratch", [NSEQ + 1, 6 * D], F32, kind="Internal").ap())
    args.append(nc.dram_tensor("h2_scratch", [TOK, D], F32, kind="Internal").ap())
    args.append(nc.dram_tensor("y_scratch", [2 * TOK, D], F32, kind="Internal").ap())
    build(nc, *args)
    r = _run(nc, [arrays], core_ids=[0])
    return tuple(r.results[0][f"out_{i}_dram"] for i in range(len(_OUTS)))
```

```python
from contextlib import ExitStack

import concourse.bass as bass
import numpy as np
from concourse import mybir

F32 = mybir.dt.float32
F32R = mybir.dt.float32r
I32 = mybir.dt.int32
ALU = mybir.AluOpType
ACT = mybir.ActivationFunctionType
AX_X = mybir.AxisListType.X

P = 128
D = 1024
DC = D // P
SEQ = 1024
NSEQ, LNEW = 8, 4
NSAMP = NSEQ * LNEW
NT = SEQ // P + 1
TOK = SEQ + NSAMP
AW = 512
HEADS, SUBS, HD = 4, 8, 64
PAGES = 8
NG, EPG = 4, 8
NE = NG * EPG
FE = 256
FC = FE // P
MAXT = 2 * TOK // P + NE
MAXT += MAXT % 2
TCOLS = MAXT + 2
NOROW = 1 << 16
LAM_INIT = 0.2
NORM_EPS, SUBLN_EPS = 1e-6, 1e-5
SCALE = HD ** -0.5
NEG = -1e30
TB = TOK // 3
CUW = 2 + SEQ + NSEQ * (2 + LNEW)

_C = {}
_n = 0
for _name, _w in (("ident", P), ("mask", P), ("upper", P), ("iota", P), ("rope", NT * 96),
                  ("tokid", 2 * NT), ("valid", NT), ("dmask", LNEW), ("pair", 16), ("sub0", 1), ("sub1", 1),
                  ("half", 1), ("tilecol", 1)):
    _C[_name] = (_n, _n + _w)
    _n += _w
NCONST = _n


def constants():
    c = np.zeros((P, NCONST), np.float32)

    def put(name, v):
        a, b = _C[name]
        c[:v.shape[0], a:b] = v.reshape(v.shape[0], -1)

    i = np.arange(P)
    put("ident", np.eye(P, dtype=np.float32))
    put("mask", np.where(i[None, :] <= i[:, None], 0.0, NEG).astype(np.float32))
    put("upper", (i[:, None] < i[None, :]).astype(np.float32))
    put("iota", np.broadcast_to(i[None, :], (P, P)).astype(np.float32))
    pos = np.zeros((NT, P), np.float32)
    pos[:NT - 1] = np.arange(SEQ).reshape(NT - 1, P)
    pos[NT - 1, :NSAMP] = PAGES * P + np.arange(NSAMP) % LNEW
    exponent = (np.arange(0, HD, 2, dtype=np.float32) / np.float32(HD)).astype(np.float64)
    inv = (np.float32(1.0) / (10000.0 ** exponent).astype(np.float32)).astype(np.float32)
    ang = (pos[:, :, None] * inv[None, None, :]).astype(np.float32)
    table = np.concatenate([np.cos(ang), -np.sin(ang), np.sin(ang)], axis=-1).astype(np.float32)
    put("rope", np.ascontiguousarray(table.transpose(1, 0, 2)))
    tok = np.arange(NT)[None, :] * P + i[:, None]
    ok = tok < TOK
    rows_of = 1 + tok[:, :, None] + TOK * np.arange(2)
    put("tokid", np.where(ok[:, :, None], rows_of, 0).astype(np.float32))
    put("valid", ok.astype(np.float32))
    r = np.arange(SUBS * LNEW)
    put("dmask", np.where(np.arange(LNEW)[None, :] <= (r % LNEW)[:, None], 0.0, NEG).astype(np.float32))
    cols = np.arange(HEADS * LNEW)
    put("pair", ((r // (2 * LNEW))[:, None] * LNEW + (r % LNEW)[:, None] == cols[None, :]).astype(np.float32))
    put("sub0", ((r // LNEW) % 2 == 0).astype(np.float32)[:, None])
    put("sub1", ((r // LNEW) % 2 == 1).astype(np.float32)[:, None])
    put("tilecol", i[:, None].astype(np.float32))
    put("half", np.full((P, 1), -0.5, np.float32))
    return c


def build(nc, consts, x_prompt, x_sample, cache_k, cache_v, state_conv, page_table, c_prompt, c_sample,
          w_ada, b_ada, ln_mix, w_in, lam_q1, lam_k1, lam_q2, lam_k2, subln_g, w_conv, w_out,
          ln_ffn, w_router_grp, b_router_grp, w_router_exp, b_router_exp, w_gate, w_up, w_down, ln_final,
          y_prompt, y_sample, k_prompt, v_prompt, conv_prompt, k_sample, v_sample, conv_sample,
          mod_dram, h2_dram, y_dram):
    x_p = x_prompt.rearrange("b s d -> (b s) d")
    x_s = x_sample.rearrange("b s d -> (b s) d")
    kc = cache_k.rearrange("l n p h d -> (l n) p (h d)")
    vc = cache_v.rearrange("l n p h d -> (l n) p (h d)")
    y_p = y_prompt.rearrange("b s d -> (b s) d")
    y_s = y_sample.rearrange("b s d -> (b s) d")
    kp_out = k_prompt.rearrange("l b s h d -> (l b s) (h d)")
    vp_out = v_prompt.rearrange("l b s h d -> (l b s) (h d)")
    ks_out = k_sample.rearrange("l b s h d -> (l b s) (h d)")
    vs_out = v_sample.rearrange("l b s h d -> (l b s) (h d)")
    cp_out = conv_prompt.rearrange("l b s c -> (l b s) c")
    cs_out = conv_sample.rearrange("l b s c -> (l b s) c")
    w_ada_v = w_ada[0].rearrange("(c p) n -> p c n", p=P)
    w_in_v = w_in[0].rearrange("(c p) n -> p c n", p=P)
    w_out_v = w_out[0].rearrange("(c p) n -> p c n", p=P)
    gate_v = w_gate[0].rearrange("e (p c) n -> e p c n", c=DC)
    up_v = w_up[0].rearrange("e (p c) n -> e p c n", c=DC)
    down_v = w_down[0].rearrange("e (p c) n -> e p c n", c=FC)

    with ExitStack() as ctx:
        K = 1024

        def at(name, off_bytes, shape, dt=F32):
            return nc.alloc_sbuf_tensor_at(name, shape, dt, offset=BASE + off_bytes)

        BASE = -(-nc.sbuf_base // 64) * 64
        psum = ctx.enter_context(nc.psum_tensor("psum", [P, 8, 512], F32))

        def sem(name):
            return ctx.enter_context(nc.semaphore(name))

        O_AB, O_X, O_W, O_H, O_VKQ, O_MA = 8 * K, 24 * K, 60 * K, 108 * K, 141 * K, 189 * K
        cst = at("cst", 0, [P, NCONST])
        small = at("small", NCONST * 4 + 32 - (NCONST * 4) % 32, [P, 224])
        kTs = at("kTs", 6 * K + 960, [P, HEADS, NSAMP])
        qTs = at("qTs", 7 * K + 448, [P, HEADS, NSAMP])

        def C(name, rows=P):
            a, b = _C[name]
            return cst[0:rows, a:b]

        ident = C("ident")
        rope = C("rope").rearrange("p (t c) -> p t c", t=NT)
        shift_p = at("shift_p", O_AB, [P, D]); scale_p = at("scale_p", O_AB + 4 * K, [P, D])
        shift_s = at("shift_s", O_AB + 8 * K, [P, D]); scale_s = at("scale_s", O_AB + 12 * K, [P, D])
        WADA = (O_MA, O_MA + 8 * K, O_H + 9 * K, O_H + 17 * K, O_H + 25 * K, O_VKQ + 34 * K)
        wada = [at(f"wada{i}", o, [P, DC // 2, 512]) for i, o in enumerate(WADA)]
        wadaL = [at(f"wadaL{i}", o, [P, DC // 2, 512]) for i, o in enumerate(WADA)]
        wadaH = [at(f"wadaH{i}", o, [P, DC // 2, 512]) for i, o in enumerate((O_X + 12 * K, O_X + 20 * K, O_H))]
        condTH = at("condTH", O_H + 8 * K + 320, [P, DC, NSEQ + 1]); condTL = at("condTL", O_H + 8 * K + 640, [P, DC, NSEQ + 1])
        cond = at("cond", O_H, [NSEQ + 1, D]); cth = at("cth", O_H + 4 * K, [NSEQ + 1, D])
        condT = at("condT", O_H + 8 * K, [P, DC, NSEQ + 1])
        mod = at("mod", O_VKQ, [NSEQ + 1, 6 * D])
        lnm = at("lnm", O_VKQ + 24 * K, [NSEQ + 1, D]); lnf = at("lnf", O_VKQ + 28 * K, [NSEQ + 1, D])
        lamv = at("lamv", O_VKQ + 32 * K, [P, 4, HD]); gsub = small[:, 96:224]
        wqkv = at("wqkv", O_W, [P, DC, 3 * AW])
        hT = at("hT", O_H, [P, DC, TOK])
        xin = [at(f"xin{i}", O_X + 4 * K * i, [P, D]) for i in range(3)]
        hrow = [at(f"hrow{i}", O_X + 12 * K + 4 * K * i, [P, D]) for i in range(2)]
        qrow = [at(f"qrow{i}", O_X + 20 * K + 2 * K * i, [P, AW]) for i in range(2)]
        krow = [at(f"krow{i}", O_X + 24 * K + 2 * K * i, [P, AW]) for i in range(2)]
        ropet = at("ropet", O_X + 28 * K, [P, AW]); junk = at("junk", O_X + 30 * K, [P, D])
        vs_row = at("vs_row", O_X + 34 * K, [P, AW])
        v_sb = at("v_sb", O_VKQ, [P, NT - 1, AW])
        kT = at("kT", O_VKQ + 16 * K, [P, HEADS, SEQ]); qT = at("qT", O_VKQ + 32 * K, [P, HEADS, SEQ])
        wcv = [at("wcv0", O_MA, [P, DC, 3, P]), at("wcv1", O_W + 12 * K, [P, DC, 3, P])]
        cg_sb = at("cg_sb", O_W + 24 * K, [P, TB]); bg_sb = at("bg_sb", O_W + 25 * K + 512, [P, TOK])
        mixC = at("mixC", O_W + 31 * K + 512, [P, 4, TOK])
        cuT = at("cuT", O_X, [P, 4, CUW])
        ctmp = at("ctmp", O_X + 17 * K, [P, TOK])
        state_sb = at("state_sb", O_X + 22 * K, [2 * NSEQ, AW]); wcvT = at("wcvT", O_X + 24 * K, [P, 4, 4])
        wconv_sb = at("wconv_sb", O_X + 25 * K, [3, AW]); ncT = at("ncT", O_X + 27 * K, [P, 4, 18])
        nc_row = at("nc_row", O_X + 28 * K, [18, AW])
        pexp = at("pexp", O_H, [P, 2, SEQ])
        pexp2 = at("pexp2", O_H + 8 * K, [P, 2, SEQ])
        adiff = at("adiff", O_H + 16 * K, [P, SEQ])
        adT = at("adT", O_H + 20 * K, [P, SEQ // P, P])
        qz = [at(f"qz{i}", O_AB + 4 * K * i, [P, 2, HEADS, P]) for i in range(2)]
        ajunk = at("ajunk", O_H + 32 * K, [P, P])
        attrow = at("attrow", O_X + 34 * K, [P, AW])
        mixA = at("mixA", O_MA, [P, 4, TOK])
        kseq = [at(f"kseq{i}", O_W + 8 * K * i, [P, 4, AW]) for i in range(3)]
        vseq = [at(f"vseq{i}", O_X + 16 * K * i, [P, PAGES, AW]) for i in range(2)]
        vnew = [at("vnew0", O_W + 28 * K + 512, [LNEW, AW]), at("vnew1", O_X + 32 * K, [LNEW, AW])]
        qbd = at("qbd", O_W + 24 * K, [P, NSEQ, 4, 32])
        kTp = [at(f"kTp{i}", O_H + 24 * K + 2 * K * i, [P, 4, P]) for i in range(2)]
        pdec = [at(f"pdec{i}", O_H + 4 * K * i + 512 * i, [32, PAGES * P + LNEW]) for i in range(2)]
        aTs = [at(f"aTs{i}", O_H + 9 * K + 5 * K * i, [P, PAGES + 1, P]) for i in range(2)]
        snew = [at(f"snew{i}", O_H + 19 * K + 64 * i, [32, LNEW]) for i in range(2)]
        pairs = [at(f"pairs{i}", O_H + 19 * K + 128 + 64 * i, [32, 16]) for i in range(2)]
        orow = at("orow", O_X + 32 * K, [NSAMP, HEADS, P])
        pt_sb = at("pt_sb", O_W + 28 * K, [1, NSEQ * PAGES], I32)
        wout = at("wout", O_VKQ, [P, DC, D])
        woutL = at("woutL", O_VKQ, [P, DC, D])
        woutH = [at("woutH0", O_VKQ + 36 * K, [P, 3, D]), at("woutH1", O_W + 8 * K, [P, DC - 3, D])]
        mixH = [at(f"mixH{i}", O_H + (20 + 4 * i) * K, [P, DC // 2, P]) for i in range(3)]
        mixL = [at(f"mixL{i}", o, [P, DC // 2, P]) for i, o in enumerate((O_H + 22 * K, O_H + 26 * K, O_W + 28 * K))]
        wrt = at("wrt", O_VKQ + 32 * K, [P, DC, NG + NE]); brt = at("brt", O_VKQ + 33 * K + 256, [P, NG + NE])
        logit = at("logit", O_VKQ + 33 * K + 512, [P, NT, NG + NE])
        gate_ap = at("gate_ap", O_W, [P, D]); gate_as = at("gate_as", O_W + 4 * K, [P, D])
        x1 = at("x1", O_X, [P, NT, D])
        h2row = [at(f"h2row{i}", O_H + 4 * K * i, [P, D]) for i in range(2)]
        h2T = [at(f"h2T{i}", O_H + 8 * K + 4 * K * i, [P, DC, P]) for i in range(2)]
        ojunk = at("ojunk", O_H + 16 * K, [P, D])
        otmp = at("otmp", O_H + 31 * K, [P, 512])
        rt = at("rt", O_H, [P, 3300])
        lsel = [at(f"lsel{i}", O_MA + 4 * K + 512 * i, [P, P]) for i in range(4)]
        hsel = [at(f"hsel{i}", O_MA + 6 * K + 256 * i, [P, TCOLS]) for i in range(4)]
        xrow = at("xrow", O_MA, [P, TCOLS], I32)
        yidx = at("yidx", O_MA + 256, [P, TCOLS], I32)
        plan = at("plan", O_MA + 10 * K, [1, TCOLS + NE + 2], I32)
        cw = at("cw", O_MA + 768, [P, 2, NT])
        vmap = at("vmap", O_MA + 8 * K, [P, 3, TCOLS])
        wgu = [at(f"wgu{i}", O_W + 16 * K * i, [P, 2, DC, FE]) for i in range(2)]
        wdn = [at(f"wdn{i}", O_W + 32 * K + 8 * K * i, [P, FC, D]) for i in range(2)]
        wguL = [at(f"wguL{i}", O_W + 16 * K * i, [P, 2, DC, FE]) for i in range(2)]
        wdnL = [at(f"wdnL{i}", O_W + 32 * K + 8 * K * i, [P, FC, D]) for i in range(2)]
        wguH = [at(f"wguH{i}", O_VKQ + 16 * K * i, [P, 2, DC, FE]) for i in range(2)]
        wdnH = [at(f"wdnH{i}", O_VKQ + 32 * K + 8 * K * i, [P, FC, D]) for i in range(2)]
        gidx = [at(f"gidx{i}", O_MA + 1024 + 32 * i, [P, 1], I32) for i in range(2)]
        sidx = [at(f"sidx{i}", O_MA + 1088 + 32 * i, [P, 1], I32) for i in range(2)]
        xg = [at(f"xg{i}", O_H + 24 * K + 4 * K * i, [P, D]) for i in range(2)]
        xgH = [at(f"xgH{i}", O_H + 4 * K * i, [P, DC, P]) for i in range(2)]
        xgL = [at(f"xgL{i}", O_H + 8 * K + 4 * K * i, [P, DC, P]) for i in range(2)]
        th = [at(f"th{i}", O_H + 16 * K + K * i, [P, FE]) for i in range(2)]
        hid = [at(f"hid{i}", O_H + 18 * K + K * i, [P, FE]) for i in range(2)]
        hidH = [at(f"hidH{i}", O_H + 20 * K + K * i, [P, FC, P]) for i in range(2)]
        hidL = [at(f"hidL{i}", O_H + 22 * K + K * i, [P, FC, P]) for i in range(2)]
        gated = [at(f"gated{i}", O_MA + 2 * K + K * i, [P, FE]) for i in range(2)]
        yrow = [at("yrow0", O_MA + 4 * K, [P, D]), at("yrow1", O_MA + 12 * K, [P, D])]
        gate_fp = at("gate_fp", O_AB, [P, D]); gate_fs = at("gate_fs", O_AB + 4 * K, [P, D])
        lnfin = at("lnfin", O_AB + 8 * K, [P, D])
        yg = [[at(f"yg{i}_{k}", O_W + 8 * K * i + 4 * K * k, [P, D]) for k in range(2)] for i in range(3)]
        fin = [at(f"fin{i}", O_W + 24 * K + 4 * K * i, [P, D]) for i in range(2)]
        fjunk = at("fjunk", O_W + 32 * K, [P, D])

        ssq, rstd = small[:, 0:9], small[:, 9:18]
        neglam = small[:, 18:19]
        nm, ls, rl = small[:, 20:24], small[:, 24:28], small[:, 28:30]
        ratio = small[:, 30:31]
        r1s = [small[:, 32:36], small[:, 89:93]]
        hss, hrs, hsc = small[:, 36:40], small[:, 40:44], small[:, 44:48]
        lsum = small[:, 48:52]
        dmx, dl, dr = small[0:32, 52:57], small[0:32, 57:60], small[0:32, 60:64]
        sgn = small[0:32, 64:65]
        ss2, rs2 = small[:, 66:75], small[:, 75:84]

        R, off = {}, 0
        for name, n in (("ohs", NT * NE), ("oh1", NT * NE), ("oh2", NT * NE), ("el", NT * NE), ("ta", NT * NE), ("tb", NT * NE),
                        ("base", NT * NE), ("gm", NT), ("gs", NT * NG), ("ge", NT * NG), ("gsum", NT), ("gp", NT),
                        ("eq4", NT * NG), ("ohg", NT * NG), ("pen", NT * NG), ("mn", NT), ("m1", NT), ("m2", NT), ("dd", NT), ("ee", NT),
                        ("ws", NT), ("cnt", NE), ("nt", NE), ("inca", NE), ("incb", NE), ("first", NE), ("slot", 2 * NT),
                        ("lo", 2 * NT), ("hi", 2 * NT), ("pcol", 1)):
            R[name] = rt[:, off:off + n]
            off += n
        assert off <= 3300
        INC, MID = TCOLS, TCOLS + NE
        ones = at("ones", O_H + 15 * K, [P, P])
        slot_i = at("slot_i", O_H + 14 * K + 256, [P, 2 * NT], I32)
        slot_lo = at("slot_lo", O_H + 14 * K, [P, 2 * NT], I32)
        slot_hi = at("slot_hi", O_H + 14 * K + 128, [P, 2 * NT], I32)

        names = """const_in cond_in bias_in wada_in0 wada_in1 wada_in2 cond_th cond_act condT_ps condT_sb ada_ps ada_sb gain_done
        mod_out mix_rows_in lam_in lam_exp lam_done wqkv_in x_in0 x_in1 x_in2 ssq_done rstd_done h_done hT_ps hT_sb qkv_ps
        q_done k_done v_done qT_ps kT_ps qT_sb kT_sb kv_out0 kv_out1 wcv_in0 wcv_in1 state_in state_ps state_sb_s
        cv_ps gates_sb cu_done conv_done nc_ps nc_sb nc_out ncT_done
        qz_done s_ps mask_done nmax_done exp_done adiff_done adT_ps adT_sb o_ps ssqh_done rstdh_done att_done attT_ps attT_sb
        dscore_ps page_in kseq_in0 kseq_in1 kseq_in2 vseq_in0 vseq_in1 kp_ps kp_sb qbd_done ds_ps dnew_done dmax_done dexp_done pair_done
        da_ps da_sb do_ps oT_sb ssqs_done rstds_done atts_done attsT_ps attsT_sb
        wout_in lead_done rest_done half_used sub2_rows_in mix_ps x1_done ssq2_done rstd2_done h2_done h2_out0 h2_out1 h2T_ps h2T_sb lg_ps lg_done
        rexp_in rexp_done tcols_done plan_ps oh_done cnt_ps sel_done map_ps plan_done
        wgate_in0 wgate_in1 wup_in0 wup_in1 wdn_in0 wdn_in1 wguH_done wguL_done wdnH_done wdnL_done gidx_done sidx_done xg_in0 xg_in1 go_on
        xgT_ps xgH_done xgL_done gu_ps th_done hid_done hidT_ps hidH_done hidL_done y_ps y_done y_out0 y_out1
        fin_rows_in yg_in0 yg_in1 yg_in2 comb_done scaled_done ssq3_done rstd3_done fin_done fin_out0 fin_out1
        dve_step act_step pool_step m_dve_step""".split()
        S = {n: sem(n) for n in names}

        block = ctx.enter_context(nc.Block())

        def rows(t):
            return P if t < NT - 1 else NSAMP

        def mixT(c, lo, n):
            return (mixA if c < 4 else mixC)[:, c % 4, lo:lo + n]

        MOD = {"shift_a": 0, "scale_a": 1, "gate_a": 2, "shift_f": 3, "scale_f": 4, "gate_f": 5}

        def load_mod(eng, name, dst_p, dst_s, s):
            a = MOD[name] * D
            eng.dma_start(dst_p[:, :], mod_dram[0, a:a + D].partition_broadcast(P)).then_inc(s, 16)
            for i in range(NSEQ):
                eng.dma_start(dst_s[LNEW * i:LNEW * i + LNEW, :],
                              mod_dram[1 + i, a:a + D].partition_broadcast(LNEW)).then_inc(s, 16)

        ROWSEMS = 16 * (1 + NSEQ)
        ADAB = 12

        def expert_steps(eng, step, mid):
            for b in range(2):
                step(b, b, 0, True, 2)
            with eng.Fori(0, mid) as m:
                for b in range(2):
                    step(2 * m + (2 + b), b, m + 1, False, 2)
            for b in range(2):
                step(2 * mid + (2 + b), b, mid + 1, False, 1 - b)

        def expert_of(eng, j):
            return eng.value_load(plan[0:1, bass.ds(j, 1)], min_val=0, max_val=NE - 1)

        def step_of(e, before):
            return (e - before + NE) & 1

        def in_slot(eng, e, body, new=1):
            for slot in range(2):
                bit = (e + (1 - slot)) & 1
                with eng.If(((bit + new) >> 1) > 0):
                    body(slot)

        def r32(ap):
            return ap.bitcast(F32R)

        def lead_of_wout(c):
            return woutH[0][:, c, :] if c < 3 else woutH[1][:, c - 3, :]
        W = S

        @block.sync
        def _(sp):
            sp.dma_start(cst[:, :], consts).then_inc(S["const_in"], 16)
            sp.dma_start(cond[0:1, :], c_prompt).then_inc(S["cond_in"], 16)
            sp.dma_start(cond[1:NSEQ + 1, :], c_sample).then_inc(S["cond_in"], 16)
            for b in range(ADAB):
                if b >= 3:
                    sp.wait_ge(W["ada_ps"], b - 2)
                for u in range(2):
                    sp.dma_start(wada[2 * (b % 3) + u][:, :, :], w_ada_v[:, 4 * u:4 * u + 4, 512 * b:512 * b + 512]).then_inc(S[f"wada_in{b % 3}"], 16)
                if b == 9:
                    sp.wait_ge(W["mod_out"], 16)
                    load_mod(sp, "shift_a", shift_p, shift_s, S["mix_rows_in"])
                    load_mod(sp, "scale_a", scale_p, scale_s, S["mix_rows_in"])
                if b == 6:
                    for t in range(3):
                        sp.dma_start(xin[t][:, :], x_p[P * t:P * t + P, :]).then_inc(S[f"x_in{t}"], 16)
                if b == 0:
                    sp.dma_start(mod[:, :], b_ada[0].partition_broadcast(NSEQ + 1)).then_inc(S["bias_in"], 16)
                    sp.dma_start(lnm[:, :], ln_mix[0].partition_broadcast(NSEQ + 1)).then_inc(S["bias_in"], 16)
                    sp.dma_start(lnf[:, :], ln_ffn[0].partition_broadcast(NSEQ + 1)).then_inc(S["bias_in"], 16)
                    for i, v in enumerate((lam_q1, lam_k1, lam_q2, lam_k2)):
                        sp.dma_start(lamv[:, i, :], v[0].partition_broadcast(P)).then_inc(S["lam_in"], 16)
                    sp.dma_start(gsub, subln_g[0].partition_broadcast(P)).then_inc(S["lam_in"], 16)
            sp.dma_start(wqkv[:, :, :], w_in_v[:, :, 0:3 * AW]).then_inc(S["wqkv_in"], 16)
            for t in range(3, NT):
                sp.wait_ge(W["h_done"], t - 2)
                src = x_p[P * t:P * t + P, :] if t < NT - 1 else x_s
                sp.dma_start(xin[t % 3][0:rows(t), :], src).then_inc(S[f"x_in{t % 3}"], 16)
            for i in range(4):
                if i == 1:
                    sp.wait_ge(W["qkv_ps"], 3 * NT)
                if i >= 2:
                    sp.wait_ge(W["cv_ps"], 3 * (i - 1))
                for j in range(3):
                    a = 3 * AW + j * AW + P * i
                    sp.dma_start(wcv[i % 2][:, :, j, :], w_in_v[:, :, a:a + P]).then_inc(S[f"wcv_in{i % 2}"], 16)
                if i == 0:
                    sp.wait_ge(W["kT_ps"], NT)
                    sp.wait_ge(W["kv_out0"], 32 * 5)
                    sp.wait_ge(W["kv_out1"], 32 * 4)
                    sp.wait_ge(W["rstd_done"], NT)
                    sp.dma_start(state_sb[:, :], state_conv.rearrange("l b s c -> (l b s) c")).then_inc(S["state_in"], 16)
                    sp.dma_start(wconv_sb[:, :], w_conv[0]).then_inc(S["state_in"], 16)
            sp.wait_ge(W["cv_ps"], 12)
            sp.wait_ge(W["conv_done"], 8)
            sp.dma_start(pt_sb[:, :], page_table.rearrange("b n -> (b n)").rearrange("(a n) -> a n", a=1)).then_inc(S["page_in"], 16)
            sp.wait_ge(W["page_in"], 16)
            sp.wait_ge(W["nc_out"], 32)
            def page_of(s, p):
                return sp.value_load(pt_sb[0:1, s * PAGES + p:s * PAGES + p + 1], min_val=0, max_val=kc.shape[0] - 1)

            def load_keys(s):
                for g in range(2):
                    n = 2 * s + g
                    if n >= 3:
                        sp.wait_ge(W["kp_ps"], 4 * (n - 2))
                    for j in range(4):
                        page = page_of(s, 4 * g + j)
                        sp.dma_start(kseq[n % 3][:, j, :], kc[bass.ds(page, 1)].rearrange("o p c -> p (o c)")).then_inc(S[f"kseq_in{n % 3}"], 16)

            def load_values(s):
                if s >= 2:
                    sp.wait_ge(W["do_ps"], s - 1)
                for p in range(PAGES):
                    page = page_of(s, p)
                    sp.dma_start(vseq[s % 2][:, p, :], vc[bass.ds(page, 1)].rearrange("o p c -> p (o c)")).then_inc(S[f"vseq_in{s % 2}"], 16)
                sp.dma_start(vnew[s % 2][:, :], vs_out[LNEW * s:LNEW * s + LNEW, :]).then_inc(S[f"vseq_in{s % 2}"], 16)

            load_keys(0)
            for s in range(NSEQ):
                if s + 1 < NSEQ:
                    load_keys(s + 1)
                load_values(s)
                if s == 1:
                    sp.wait_ge(W["o_ps"], 32)
                    sp.dma_start(wout[:, :, :], w_out_v).then_inc(S["wout_in"], 16)
                    sp.dma_start(wrt[:, :, 0:NG], w_router_grp[0].rearrange("(c p) n -> p c n", p=P)).then_inc(S["wout_in"], 16)
                    sp.dma_start(wrt[:, :, NG:NG + NE], w_router_exp[0].rearrange("(c p) n -> p c n", p=P)).then_inc(S["wout_in"], 16)
                    sp.dma_start(brt[:, 0:NG], b_router_grp[0].partition_broadcast(P)).then_inc(S["wout_in"], 16)
                    sp.dma_start(brt[:, NG:NG + NE], b_router_exp[0].partition_broadcast(P)).then_inc(S["wout_in"], 16)
            load_mod(sp, "shift_f", shift_p, shift_s, S["sub2_rows_in"])
            load_mod(sp, "scale_f", scale_p, scale_s, S["sub2_rows_in"])
            sp.wait_ge(W["kp_ps"], 64)
            load_mod(sp, "gate_a", gate_ap, gate_as, S["sub2_rows_in"])
            sp.wait_ge(W["do_ps"], NSEQ)
            for t in range(NT):
                if t == NT - 1:
                    sp.wait_ge(W["attsT_ps"], 1)
                src = x_p[P * t:P * t + P, :] if t < NT - 1 else x_s
                sp.dma_start(x1[0:rows(t), t, :], src).then_inc(S["sub2_rows_in"], 16)

            def load_gate_up(e, b):
                sp.dma_start(wgu[b][:, 0, :, :], gate_v[bass.ds(e, 1)].rearrange("o p c n -> p (o c) n")).then_inc(S[f"wgate_in{b}"], 16)
                sp.dma_start(wgu[b][:, 1, :, :], up_v[bass.ds(e, 1)].rearrange("o p c n -> p (o c) n")).then_inc(S[f"wup_in{b}"], 16)

            sp.wait_ge(W["x1_done"], 2 * NT)
            load_gate_up(0, 0)
            sp.wait_ge(W["h2_done"], NT)
            load_mod(sp, "gate_f", gate_fp, gate_fs, S["fin_rows_in"])
            sp.dma_start(lnfin[:, :], ln_final.partition_broadcast(P)).then_inc(S["fin_rows_in"], 16)

            def load_expert(e, b, i, first, last):
                if not (first and b == 0) and not last:
                    sp.wait_ge(W["gu_ps"], sp.value_load(plan[0:1, bass.ds(e + (INC - 1), 1)], min_val=1, max_val=MAXT))
                if not last:
                    load_gate_up(e + 1, 1 - b)
                if not first:
                    sp.wait_ge(W["y_ps"], sp.value_load(plan[0:1, bass.ds(e + (INC - 2), 1)], min_val=1, max_val=MAXT))
                sp.dma_start(wdn[b][:, :, :], down_v[bass.ds(e, 1)].rearrange("o p c n -> p (o c) n")).then_inc(S[f"wdn_in{b}"], 16)

            load_expert(0, 0, 0, True, False)
            sp.wait_ge(W["plan_done"], 1)
            mid = sp.value_load(plan[0:1, MID:MID + 1], min_val=NE // 2 - 2, max_val=MAXT // 2 - 2)
            load_expert(1, 1, 0, True, False)
            with sp.Fori(0, NE // 2 - 2) as m:
                for b in range(2):
                    load_expert(2 * m + (2 + b), b, m + 1, False, False)
            for b in range(2):
                load_expert(NE - 2 + b, b, NE // 2 - 1, False, b == 1)
            for b in range(2):
                sp.wait_ge(W[f"y_out{b}"], 16 * mid + 32)
                sp.sem_inc(S["go_on"], 1)

            def load_pair(t):
                n = rows(t)
                for k in range(2):
                    a = TOK * k + P * t
                    sp.dma_start(yg[t % 3][k][0:n, :], y_dram[a:a + n, :]).then_inc(S[f"yg_in{t % 3}"], 16)

            for t in range(3):
                load_pair(t)
            for t in range(NT):
                if t + 3 < NT:
                    sp.wait_ge(W["comb_done"], t + 1)
                    load_pair(t + 3)
                sp.wait_ge(W["fin_done"], t + 1)
                dst = y_p[P * t:P * t + P, :] if t < NT - 1 else y_s
                sp.dma_start(dst, fin[t % 2][0:rows(t), :]).then_inc(S[f"fin_out{t % 2}"], 16)
            sp.wait_ge(W["fin_out0"], 16 * 5)
            sp.wait_ge(W["fin_out1"], 16 * 4)
            sp.wait_ge(W["kv_out0"], 32 * 5)
            sp.wait_ge(W["kv_out1"], 32 * 4)
            sp.wait_ge(W["nc_out"], 32)

        def bank(b, n=512, rows_=P):
            return psum[0:rows_, b, 0:n]

        def page_scores(pe, s, p):
            n = s * PAGES + p
            pe.wait_ge(W["kp_sb"], n + 1)
            if p == 0 and s >= 2:
                pe.wait_ge(W["dexp_done"], 2 * s - 2)
            for c in range(4):
                last = nc.tensor.matmul(psum[0:32, 2 * (s % 2) + p // 4, P * (p % 4):P * (p % 4) + P], qbd[:, s, c, :], kTp[n % 2][:, c, :],
                                        start=(c == 0), stop=(c == 3))
            last.then_inc(S["dscore_ps"], 1)

        @block.tensor
        def _(pe):
            mm, tr = nc.tensor.matmul, nc.tensor.transpose

            def three_passes(out, xH, xL, wH, wL, chunks, begin=True, end=True):
                parts = ((xH, wH), (xH, wL), (xL, wH))
                for c in range(chunks):
                    for k, (x, w) in enumerate(parts):
                        ins = mm(out, r32(x(c)), r32(w(c)), start=(begin and c == 0 and k == 0), stop=(end and c == chunks - 1 and k == 2))
                return ins

            pe.wait_ge(W["const_in"], 16)
            pe.wait_ge(W["cond_act"], 1)
            cT = bank(7, DC * 9).rearrange("p (c s) -> p c s", c=DC)
            for c in range(DC):
                last = tr(cT[:, c, :], cond[:, P * c:P * c + P], ident[0:9, 0:9])
            last.then_inc(S["condT_ps"], 1)
            pe.wait_ge(W["condT_sb"], 1)
            for b in range(ADAB):
                if b >= 2:
                    pe.wait_ge(W["ada_sb"], b - 1)
                for u in range(2):
                    n = 2 * b + u
                    pe.wait_ge(W["rest_done"], n + 1)
                    last = three_passes(psum[0:9, b % 2, :], lambda c: condTH[:, 4 * u + c, :], lambda c: condTL[:, 4 * u + c, :],
                                        lambda c: wadaH[n % 3][:, c, :], lambda c: wadaL[n % 6][:, c, :],
                                        DC // 2, begin=(u == 0), end=(u == 1))
                    last.then_inc(S["ada_ps" if u else "half_used"], 1)

            def x_transposes(t):
                pe.wait_ge(W["h_done"], t + 1)
                if t >= 1:
                    pe.wait_ge(W["hT_sb"], t)
                n = rows(t)
                for c in range(DC):
                    last = tr(psum[:, c // 4, P * (c % 4):P * (c % 4) + n], hrow[t % 2][0:n, P * c:P * c + P], ident[0:n, 0:n])
                last.then_inc(S["hT_ps"], 1)

            def qk_transposes(t):
                n = rows(t)
                for name, src, b in (("q", qrow, 5), ("k", krow, 6)):
                    pe.wait_ge(W[f"{name}_done"], t + 1)
                    if t >= 1:
                        pe.wait_ge(W[f"{name}T_sb"], t)
                    for h in range(HEADS):
                        last = tr(psum[:, b, P * h:P * h + n], src[t % 2][0:n, P * h:P * h + P], ident[0:n, 0:n])
                    last.then_inc(S[f"{name}T_ps"], 1)

            x_transposes(0)
            pe.wait_ge(W["wqkv_in"], 16)
            for t in range(NT):
                n = rows(t)
                if t + 1 < NT:
                    x_transposes(t + 1)
                pe.wait_ge(W["hT_sb"], t + 1)
                for j, name in enumerate(("q", "k", "v")):
                    if t >= 1:
                        pe.wait_ge(W[f"{name}_done"], t)
                    for c in range(DC):
                        last = mm(psum[0:n, 2 + j, :], hT[:, c, P * t:P * t + n], wqkv[:, c, AW * j:AW * j + AW],
                                  start=(c == 0), stop=(c == DC - 1))
                    last.then_inc(S["qkv_ps"], 1)
                if t >= 1:
                    qk_transposes(t - 1)
            qk_transposes(NT - 1)

            def state_transposes():
                pe.wait_ge(W["state_in"], 32)
                pe.wait_ge(W["qT_sb"], NT)
                pe.wait_ge(W["kT_sb"], NT)
                for i in range(4):
                    tr(psum[:, 6, 16 * i:16 * i + 16], state_sb[:, P * i:P * i + P], ident[0:16, 0:16])
                    last = tr(psum[:, 6, 64 + 4 * i:64 + 4 * i + 3], wconv_sb[:, P * i:P * i + P], ident[0:3, 0:3])
                last.then_inc(S["state_ps"], 1)
                pe.wait_ge(W["v_done"], NT)
                pe.wait_ge(W["k_done"], NT)

            for i in range(4):
                pe.wait_ge(W[f"wcv_in{i % 2}"], 48 * (i // 2 + 1))
                for tb in range(3):
                    n = 3 * i + tb
                    if n >= 2:
                        pe.wait_ge(W["cu_done"], n - 1)
                        pe.wait_ge(W["gates_sb"], 2 * (n - 1))
                    for j in (1, 2, 0):
                        for c in range(DC):
                            last = mm(psum[:, 3 * (n % 2) + j, 0:TB], wcv[i % 2][:, c, j, :], hT[:, c, TB * tb:TB * tb + TB],
                                      start=(c == 0), stop=(c == DC - 1))
                    last.then_inc(S["cv_ps"], 1)
                    if n == 0:
                        state_transposes()
            def scores(w, u):
                i, h = divmod(w, HEADS)
                if w == 0 and u == 0:
                    pe.wait_ge(W["qz_done"], 1)
                elif h == 0 and u == 0:
                    pe.wait_ge(W["qz_done"], i + 1)
                if w >= 1:
                    pe.wait_ge(W["exp_done"], 2 * w + u - 1)
                nk = P * (i + 1)
                for a in range(0, nk, 512):
                    b = min(nk, a + 512)
                    last = mm(psum[:, 2 * u + a // 512, 0:b - a], qz[i % 2][:, u, h, :], kT[:, h, a:b], start=True, stop=True)
                last.then_inc(S["s_ps"], 1)

            def weighted_values(w):
                i, h = divmod(w, HEADS)
                pe.wait_ge(W["adT_sb"], w + 1)
                if h == 0 and i >= 2:
                    pe.wait_ge(W["attT_sb"], i - 1)
                for kt in range(i + 1):
                    last = mm(psum[:, 6 + i % 2, P * h:P * h + P], adT[:, kt, :], v_sb[:, kt, P * h:P * h + P], start=(kt == 0), stop=(kt == i))
                last.then_inc(S["o_ps"], 1)

            def att_transposes(i):
                pe.wait_ge(W["att_done"], i + 1)
                for h in range(HEADS):
                    last = tr(psum[:, 6 + i % 2, P * h:P * h + P], attrow[:, P * h:P * h + P], ident)
                last.then_inc(S["attT_ps"], 1)

            pe.wait_ge(W["cu_done"], 12)
            pe.wait_ge(W["gates_sb"], 24)
            pe.wait_ge(W["state_sb_s"], 2)
            pe.wait_ge(W["v_done"], NT)
            pe.wait_ge(W["kT_sb"], NT)
            scores(0, 0)
            scores(0, 1)
            for w in range(8 * HEADS):
                i, h = divmod(w, HEADS)
                if w + 1 < 8 * HEADS:
                    scores(w + 1, 0)
                    scores(w + 1, 1)
                if w >= 1:
                    weighted_values(w - 1)
                if w == 2:
                    pe.wait_ge(W["ncT_done"], 1)
                    for c in range(4):
                        last = tr(psum[0:18, 7, P * c:P * c + P], ncT[:, c, :], ident)
                    last.then_inc(S["nc_ps"], 1)
                if w == 5:
                    pe.wait_ge(W["nc_sb"], 1)
                if h == 3 and i >= 1:
                    att_transposes(i - 1)
                pe.wait_ge(W["adiff_done"], w + 1)
                for kt in range(i + 1):
                    last = tr(psum[:, 4 + kt // 4, P * (kt % 4):P * (kt % 4) + P], adiff[:, P * kt:P * kt + P], ident)
                last.then_inc(S["adT_ps"], 1)
            weighted_values(8 * HEADS - 1)
            att_transposes(7)

            def sample_values(s):
                pe.wait_ge(W["pair_done"], s + 1)
                pe.wait_ge(W["dnew_done"], min(s + 2, NSEQ))
                for p in range(PAGES + 1):
                    m = P if p < PAGES else LNEW
                    last = mm(psum[0:m, 7, 16 * p:16 * p + 16], pdec[s % 2][:, P * p:P * p + m], pairs[s % 2][:, :], start=True, stop=True)
                last.then_inc(S["da_ps"], 1)
                pe.wait_ge(W["da_sb"], s + 1)
                pe.wait_ge(W[f"vseq_in{s % 2}"], 16 * (PAGES + 1) * (s // 2 + 1))
                for p in range(PAGES + 1):
                    if p < PAGES:
                        last = mm(psum[:, 6, :], aTs[s % 2][:, p, :], vseq[s % 2][:, p, :], start=(s == 0 and p == 0), stop=False)
                    else:
                        last = mm(psum[:, 6, :], aTs[s % 2][0:LNEW, p, :], vnew[s % 2][:, :], start=False, stop=(s == NSEQ - 1))
                last.then_inc(S["do_ps"], 1)

            pe.wait_ge(W["qbd_done"], 1)
            pe.wait_ge(W["attT_sb"], 8)
            for s in range(NSEQ):
                for p in range(PAGES):
                    n = s * PAGES + p
                    half = n // 4
                    pe.wait_ge(W[f"kseq_in{half % 3}"], 64 * (half // 3 + 1))
                    if n >= 2:
                        pe.wait_ge(W["kp_sb"], n - 1)
                    for c in range(4):
                        last = tr(psum[:, 4 + n % 2, P * c:P * c + P], kseq[half % 3][:, p % 4, P * c:P * c + P], ident)
                    last.then_inc(S["kp_ps"], 1)
                    if p >= 1:
                        page_scores(pe, s, p - 1)
                page_scores(pe, s, PAGES - 1)
                if s >= 2:
                    pe.wait_ge(W["da_sb"], s - 1)
                for c in range(4):
                    last = mm(psum[0:32, 7, 256:256 + LNEW], qbd[:, s, c, :], kTs[:, c, LNEW * s:LNEW * s + LNEW], start=(c == 0), stop=(c == 3))
                last.then_inc(S["ds_ps"], 1)
                if s >= 1:
                    sample_values(s - 1)
            sample_values(NSEQ - 1)

            def router(t):
                n = rows(t)
                pe.wait_ge(W["h2_done"], t + 1)
                if t >= 1:
                    pe.wait_ge(W["h2T_sb"], t)
                for c in range(DC):
                    last = tr(psum[:, 4 + c // 4, P * (c % 4):P * (c % 4) + n], h2row[t % 2][0:n, P * c:P * c + P], ident[0:n, 0:n])
                last.then_inc(S["h2T_ps"], 1)

            def logits_of(t):
                n = rows(t)
                pe.wait_ge(W["h2T_sb"], t + 1)
                if t >= 1:
                    pe.wait_ge(W["lg_done"], t)
                for c in range(DC):
                    last = mm(psum[0:n, 6, 0:NG + NE], h2T[t % 2][:, c, 0:n], wrt[:, c, :], start=(c == 0), stop=(c == DC - 1))
                last.then_inc(S["lg_ps"], 1)

            pe.wait_ge(W["wout_in"], 16 * 5)
            for t in range(NT):
                n = rows(t)
                if t >= 2:
                    pe.wait_ge(W["x1_done"], 2 * (t - 1))
                for half in range(2):
                    m = 2 * t + half
                    pe.wait_ge(W["rest_done"], 2 * ADAB + DC + m + 1)
                    for j in range(2):
                        a = slice(512 * j, 512 * j + 512)
                        last = three_passes(psum[0:n, 2 * (t % 2) + j, :],
                                            lambda c: mixH[m % 3][:, c, 0:n], lambda c: mixL[m % 3][:, c, 0:n],
                                            lambda c: lead_of_wout(4 * half + c)[:, a], lambda c: woutL[:, 4 * half + c, a],
                                            DC // 2, begin=(half == 0), end=(half == 1))
                        if half == 1:
                            last.then_inc(S["mix_ps"], 1)
                    if half == 0:
                        last.then_inc(S["half_used"], 1)
                if t == 0:
                    pe.wait_ge(W["atts_done"], 1)
                    for h in range(HEADS):
                        last = tr(psum[:, 7, NSAMP * h:NSAMP * h + NSAMP], attrow[0:NSAMP, P * h:P * h + P], ident[0:NSAMP, 0:NSAMP])
                    last.then_inc(S["attsT_ps"], 1)
                if t >= 1:
                    router(t - 1)
                if t >= 2:
                    logits_of(t - 2)
            router(NT - 1)
            logits_of(NT - 2)
            logits_of(NT - 1)

            pe.wait_ge(W["oh_done"], 1)
            pe.wait_ge(W["attsT_sb"], 1)
            pe.wait_ge(W["x1_done"], 2 * NT)
            ohs = R["ohs"]
            mm(psum[:, 0, 0:NT * NE], C("upper"), ohs, start=True, stop=True)
            mm(psum[:, 1, 0:NT * NE], ones[:, :], ohs, start=True, stop=True).then_inc(S["cnt_ps"], 1)
            pe.wait_ge(W["tcols_done"], 1)
            tr(psum[0:1, 7, 0:P], R["pcol"], ident).then_inc(S["plan_ps"], 1)
            for n in range(2 * NT):
                pe.wait_ge(W["sel_done"], n + 1)
                last = mm(psum[:, 2, 0:TCOLS], lsel[n % 4][:, :], hsel[n % 4][:, :], start=(n == 0), stop=(n == 2 * NT - 1))
                last.then_inc(S["map_ps"], 1)

            pe.wait_ge(W["plan_done"], 1)
            mid = pe.value_load(plan[0:1, MID:MID + 1], min_val=NE // 2 - 2, max_val=MAXT // 2 - 2)

            def gather_transposes(b):
                for c in range(DC):
                    last = tr(psum[:, c // 4, P * (c % 4):P * (c % 4) + P], xg[b][:, c:D:DC], ident)
                last.then_inc(S["xgT_ps"], 1)

            def down_products(j, b, first):
                e = expert_of(pe, j)
                def products(slot):
                    if not first:
                        pe.wait_ge(W["y_done"], j)
                    pe.wait_ge(W["hidL_done"], j + 1)
                    pe.wait_ge(W["wdnL_done"], e + 1)
                    for n in range(2):
                        a = slice(512 * n, 512 * n + 512)
                        last = three_passes(psum[:, 5 + n, :], lambda c: hidH[b][:, c, :], lambda c: hidL[b][:, c, :],
                                            lambda c: wdnH[slot][:, c, a], lambda c: wdnL[slot][:, c, a], FC)
                    last.then_inc(S["y_ps"], 1)

                in_slot(pe, e, products)

            def expert_products(j, b, i, first, left):
                e = expert_of(pe, j)
                def products(slot):
                    pe.wait_ge(W["xgL_done"], j + 1)
                    pe.wait_ge(W["wguL_done"], 2 * e + 2)
                    three_passes(psum[:, 2 + b, :].rearrange("p (g n) -> p g n", g=2), lambda c: xgH[b][:, c, :], lambda c: xgL[b][:, c, :],
                                 lambda c: wguH[slot][:, :, c, :], lambda c: wguL[slot][:, :, c, :], DC).then_inc(S["gu_ps"], 1)

                in_slot(pe, e, products)
                if left:
                    pe.wait_ge(W[f"xg_in{1 - b}"], 16 * (i + 1 + b))
                    gather_transposes(1 - b)
                if not (first and b == 0):
                    down_products(j - 1, 1 - b, first)
                pe.wait_ge(W["hid_done"], j + 1)
                for c in range(FC):
                    last = tr(psum[:, 4, P * c:P * c + P], hid[b][:, c:FE:FC], ident)
                last.then_inc(S["hidT_ps"], 1)

            pe.wait_ge(W["xg_in0"], 16)
            gather_transposes(0)
            expert_steps(pe, expert_products, mid)
            down_products(2 * mid + 3, 1, False)

        def bc(ap, shape, axes):
            for a in axes:
                ap = ap.unsqueeze(a)
            return ap.to_broadcast(shape)

        @block.scalar
        def _(act):
            A = nc.scalar.activation
            steps = [0]

            def link(ins):
                steps[0] += 1
                ins.then_inc(S["act_step"], 1)
                act.wait_ge(S["act_step"], steps[0])

            act.wait_ge(W["cond_in"], 32)
            A(cth[:, :], cond[:, :], ACT.Tanh, scale=0.5).then_inc(S["cond_th"], 1)

            def squares(t):
                n = rows(t)
                act.wait_ge(W[f"x_in{t % 3}"], 16 * (t // 3 + 1))
                if t >= 1:
                    act.wait_ge(W["ssq_done"], t)
                A(junk[0:n, :], xin[t % 3][0:n, :], ACT.Square, accum_out=ssq[0:n, t:t + 1]).then_inc(S["ssq_done"], 1)

            def copy_hT(t):
                n = rows(t)
                act.wait_ge(W["hT_ps"], t + 1)
                nc.scalar.copy(hT[:, :, P * t:P * t + n], psum[:, 0:2, :].rearrange("p b (c n) -> p (b c) n", c=4)[:, :, 0:n]).then_inc(S["hT_sb"], 1)

            act.wait_ge(W["condT_ps"], 1)
            for n in range(2 * ADAB):
                b, u = divmod(n, 2)
                act.wait_ge(W[f"wada_in{b % 3}"], 32 * (b // 3 + 1))
                if n >= 3:
                    if u:
                        act.wait_ge(W["half_used"], b)
                    else:
                        act.wait_ge(W["ada_ps"], b - 1)
                nc.scalar.copy(r32(wadaH[n % 3][:, :, :]), wada[n % 6][:, :, :]).then_inc(S["lead_done"], 1)
                if n == 1:
                    act.wait_ge(W["lam_done"], 1)
                    A(small[:, 85:87], small[:, 87:89], ACT.Exp).then_inc(S["lam_exp"], 1)
                if n in (18, 20, 22):
                    squares((n - 18) // 2)
            copy_hT(0)
            for t in range(NT):
                n = rows(t)
                if t + 1 < NT:
                    copy_hT(t + 1)
                if t + 3 < NT:
                    squares(t + 3)
                act.wait_ge(W["qkv_ps"], 3 * t + 3)
                if t == 0:
                    act.wait_ge(W["mod_out"], 32)
                dst = v_sb[:, t, :] if t < NT - 1 else vs_row[0:n, :]
                nc.scalar.copy(dst, psum[0:n, 4, :]).then_inc(S["v_done"], 1)
                for u in ([t - 1] if t >= 1 else []) + ([t] if t == NT - 1 else []):
                    m = rows(u)
                    for name, dst, dst_s, b in (("q", qT, qTs, 5), ("k", kT, kTs, 6)):
                        act.wait_ge(W[f"{name}T_ps"], u + 1)
                        to = dst[:, :, P * u:P * u + P] if u < NT - 1 else dst_s[:, :, :]
                        nc.scalar.mul(to, psum[:, b, :].rearrange("p (h n) -> p h n", h=HEADS)[:, :, 0:m],
                                      SCALE if name == "q" else 1.0).then_inc(S[f"{name}T_sb"], 1)

            for i in range(4):
                for tb in range(3):
                    n = 3 * i + tb
                    act.wait_ge(W["cv_ps"], n + 1)
                    if n >= 1:
                        act.wait_ge(W["cu_done"], n)
                    nc.scalar.copy(cg_sb[:, :], psum[:, 3 * (n % 2) + 1, 0:TB]).then_inc(S["gates_sb"], 1)
                    if tb == 0 and i >= 1:
                        act.wait_ge(W["conv_done"], 2 * i)
                    nc.scalar.copy(bg_sb[:, TB * tb:TB * tb + TB], psum[:, 3 * (n % 2), 0:TB]).then_inc(S["gates_sb"], 1)
            pe2 = [pexp, pexp2]

            def exps(w, u):
                nk = P * (w // HEADS + 1)
                act.wait_ge(W["nmax_done"], 2 * w + u + 1)
                if w >= 2:
                    act.wait_ge(W["adiff_done"], w - 1)
                src = psum[:, 2 * u:2 * u + 2, :].rearrange("p b n -> p (b n)")[:, 0:nk]
                k = 2 * (w % 2) + u
                A(pe2[w % 2][:, u, 0:nk], src, ACT.Exp, bias=nm[:, k:k + 1], accum_out=ls[:, k:k + 1]).then_inc(S["exp_done"], 1)

            def head_squares(i):
                act.wait_ge(W["o_ps"], 4 * i + 4)
                if i >= 1:
                    act.wait_ge(W["att_done"], i)
                for h in range(HEADS):
                    if h or i:
                        act.wait_ge(W["ssqh_done"], 4 * i + h)
                    A(ajunk[:, 0:P], psum[:, 6 + i % 2, P * h:P * h + P], ACT.Square, scale=r1s[i % 2][:, h:h + 1],
                      accum_out=hss[:, h:h + 1]).then_inc(S["ssqh_done"], 1)

            def copy_attT(i):
                act.wait_ge(W["attT_ps"], i + 1)
                nc.scalar.copy(mixA[:, :, P * i:P * i + P], psum[:, 6 + i % 2, :].rearrange("p (h n) -> p h n", h=HEADS)).then_inc(S["attT_sb"], 1)

            act.wait_ge(W["cv_ps"], 12)
            exps(0, 0)
            exps(0, 1)
            for w in range(8 * HEADS):
                i, h = divmod(w, HEADS)
                if w + 1 < 8 * HEADS:
                    exps(w + 1, 0)
                act.wait_ge(W["adT_ps"], w + 1)
                nc.scalar.copy(adT[:, 0:i + 1, :], psum[:, 4:6, :].rearrange("p b (c n) -> p (b c) n", c=4)[:, 0:i + 1, :]).then_inc(S["adT_sb"], 1)
                if w + 1 < 8 * HEADS:
                    exps(w + 1, 1)
                if w == 2:
                    act.wait_ge(W["nc_ps"], 1)
                    nc.scalar.copy(nc_row[:, :], psum[0:18, 7, :]).then_inc(S["nc_sb"], 1)
                if h == 1 and i >= 1:
                    head_squares(i - 1)
                if h == 3 and i >= 1:
                    copy_attT(i - 1)
            head_squares(7)
            copy_attT(7)

            for s in range(NSEQ):
                for p in range(PAGES):
                    n = s * PAGES + p
                    act.wait_ge(W["kp_ps"], n + 1)
                    if n >= 2:
                        act.wait_ge(W["dscore_ps"], n - 1)
                    nc.scalar.copy(kTp[n % 2][:, :, :], psum[:, 4 + n % 2, :].rearrange("p (c n) -> p c n", c=4)).then_inc(S["kp_sb"], 1)
                act.wait_ge(W["dmax_done"], s + 1)
                if s >= 2:
                    act.wait_ge(W["da_ps"], s - 1)
                b, m = s % 2, dmx[:, 3 + s % 2:4 + s % 2]
                A(pdec[b][:, 0:PAGES * P], psum[0:32, 2 * b:2 * b + 2, :].rearrange("p b n -> p (b n)"), ACT.Exp, bias=m,
                  accum_out=dl[:, 0:1]).then_inc(S["dexp_done"], 1)
                A(pdec[b][:, PAGES * P:], snew[b][:, :], ACT.Exp, bias=m, accum_out=dl[:, 1:2]).then_inc(S["dexp_done"], 1)
                if s in (4, 5, 6):
                    act.wait_ge(W["wout_in"], 80)
                    nc.scalar.copy(r32(lead_of_wout(s - 4)), wout[:, s - 4, :]).then_inc(S["lead_done"], 1)
            act.wait_ge(W["kp_ps"], 64)
            act.wait_ge(W["ds_ps"], NSEQ)
            for c in range(3, DC):
                nc.scalar.copy(r32(lead_of_wout(c)), wout[:, c, :]).then_inc(S["lead_done"], 1)
            def copy_h2T(t):
                n = rows(t)
                act.wait_ge(W["h2T_ps"], t + 1)
                if t >= 2:
                    act.wait_ge(W["lg_ps"], t - 1)
                nc.scalar.copy(h2T[t % 2][:, :, 0:n], psum[:, 4:6, :].rearrange("p b (c n) -> p (b c) n", c=4)[:, :, 0:n]).then_inc(S["h2T_sb"], 1)

            def lead_of_mix(m):
                t, half = divmod(m, 2)
                n = rows(t)
                if m >= 3:
                    if half:
                        act.wait_ge(W["half_used"], ADAB + t)
                    else:
                        act.wait_ge(W["mix_ps"], 2 * (t - 1))
                src = (mixA, mixC)[half][:, :, P * t:P * t + n]
                nc.scalar.copy(r32(mixH[m % 3][:, :, 0:n]), src).then_inc(S["lead_done"], 1)

            act.wait_ge(W["do_ps"], NSEQ)
            lead_of_mix(0)
            lead_of_mix(1)
            for h in range(HEADS):
                nc.scalar.copy(orow[:, h, :], psum[32 * h:32 * h + 32, 6, P * h:P * h + P]).then_inc(S["oT_sb"], 1)
            act.wait_ge(W["oT_sb"], 4)
            for h in range(HEADS):
                if h:
                    act.wait_ge(W["ssqs_done"], h)
                A(ajunk[0:NSAMP, 0:P], orow[:, h, :], ACT.Square, accum_out=hss[0:NSAMP, h:h + 1]).then_inc(S["ssqs_done"], 1)
            for t in range(NT):
                n = rows(t)
                if t == 1:
                    act.wait_ge(W["attsT_ps"], 1)
                    nc.scalar.copy(mixA[:, :, SEQ:TOK], psum[:, 7, 0:HEADS * NSAMP].rearrange("p (h n) -> p h n", h=HEADS)).then_inc(S["attsT_sb"], 1)
                    act.wait_ge(W["attsT_sb"], 1)
                if t + 1 < NT:
                    lead_of_mix(2 * t + 2)
                    lead_of_mix(2 * t + 3)
                if t >= 1:
                    copy_h2T(t - 1)
                act.wait_ge(W["x1_done"], 2 * t + 2)
                if t >= 1:
                    act.wait_ge(W["ssq2_done"], t)
                A(ojunk[0:n, :], x1[0:n, t, :], ACT.Square, accum_out=ss2[0:n, t:t + 1]).then_inc(S["ssq2_done"], 1)
            copy_h2T(NT - 1)

            def lead_gate_up(slot, i):
                for g in range(2):
                    act.wait_ge(W[f"{('wgate', 'wup')[g]}_in{slot}"], 16 * i + 16)
                    nc.scalar.copy(r32(wguH[slot][:, g, :, :]), wgu[slot][:, g, :, :]).then_inc(S["wguH_done"], 1)

            def lead_down(slot, i):
                act.wait_ge(W[f"wdn_in{slot}"], 16 * i + 16)
                nc.scalar.copy(r32(wdnH[slot][:, :, :]), wdn[slot][:, :, :]).then_inc(S["wdnH_done"], 1)

            lead_gate_up(0, 0)

            act.wait_ge(W["rexp_in"], 1)
            A(R["ge"], R["gs"], ACT.Exp).then_inc(S["rexp_done"], 1)
            act.wait_ge(W["rexp_in"], 2)
            A(R["ee"], R["dd"], ACT.Exp).then_inc(S["rexp_done"], 1)

            act.wait_ge(W["plan_done"], 1)
            mid = act.value_load(plan[0:1, MID:MID + 1], min_val=NE // 2 - 2, max_val=MAXT // 2 - 2)

            def lead_rows(b):
                nc.scalar.copy(r32(xgH[b][:, :, :]), psum[:, 0:2, :].rearrange("p b (c n) -> p (b c) n", c=4)).then_inc(S["xgH_done"], 1)

            def copy_y(j, b, i, stored):
                act.wait_ge(W["y_ps"], j + 1)
                if stored:
                    act.wait_ge(W[f"y_out{b}"], 16 * i)
                nc.scalar.copy(yrow[b][:, :], psum[:, 5:7, :].rearrange("p b n -> p (b n)")).then_inc(S["y_done"], 1)

            def expert_copies(j, b, i, first, left):
                if left:
                    e = expert_of(act, j + 1)
                    in_slot(act, e, lambda slot: lead_gate_up(slot, e >> 1), step_of(e, expert_of(act, j)))
                act.wait_ge(W["gu_ps"], j + 1)
                A(th[b][:, :], psum[:, 2 + b, 0:FE], ACT.Tanh, scale=0.5).then_inc(S["th_done"], 1)
                if left:
                    act.wait_ge(W["xgT_ps"], j + 2)
                    lead_rows(1 - b)
                if first and b == 0:
                    lead_down(0, 0)
                else:
                    e = expert_of(act, j)
                    in_slot(act, e, lambda slot: lead_down(slot, e >> 1), step_of(e, expert_of(act, j - 1)))
                if not (first and b == 0):
                    copy_y(j - 1, 1 - b, i - 1 + b, not first)
                act.wait_ge(W["hidT_ps"], j + 1)
                nc.scalar.copy(r32(hidH[b][:, :, :]), psum[:, 4, 0:FE].rearrange("p (c n) -> p c n", c=FC)).then_inc(S["hidH_done"], 1)

            act.wait_ge(W["xgT_ps"], 1)
            lead_rows(0)
            expert_steps(act, expert_copies, mid)
            copy_y(2 * mid + 3, 1, mid + 1, True)

            def scaled(t):
                n = rows(t)
                act.wait_ge(W[f"yg_in{t % 3}"], 32 * (t // 3 + 1))
                y0 = yg[t % 3][0][0:n, :]
                nc.scalar.mul(y0, y0, cw[0:n, 0, t:t + 1]).then_inc(S["scaled_done"], 1)

            scaled(0)
            for t in range(NT):
                n = rows(t)
                if t + 1 < NT:
                    scaled(t + 1)
                act.wait_ge(W["comb_done"], t + 1)
                if t >= 1:
                    act.wait_ge(W["ssq3_done"], t)
                A(fjunk[0:n, :], x1[0:n, t, :], ACT.Square, accum_out=ss2[0:n, t:t + 1]).then_inc(S["ssq3_done"], 1)

        @block.vector
        def _(dve):
            TT, TS, STT = nc.vector.tensor_tensor, nc.vector.tensor_scalar, nc.vector.scalar_tensor_tensor
            RED = nc.vector.tensor_reduce
            steps = [0]

            def link(ins):
                steps[0] += 1
                ins.then_inc(S["dve_step"], 1)
                dve.wait_ge(S["dve_step"], steps[0])

            dve.wait_ge(W["cond_th"], 1)
            STT(cond[:, :], cth[:, :], 1.0, cond[:, :], ALU.add, ALU.mult).then_inc(S["cond_act"], 1)
            dve.wait_ge(W["condT_ps"], 1)
            link(TS(condT[:, :, :], psum[:, 7, 0:DC * 9].rearrange("p (c s) -> p c s", c=DC), 0.5, None, ALU.mult))
            link(nc.vector.tensor_copy(r32(condTH[:, :, :]), condT[:, :, :]))
            TT(r32(condTL[:, :, :]), condT[:, :, :], condTH[:, :, :], ALU.subtract).then_inc(S["condT_sb"], 1)
            dve.wait_ge(W["lam_in"], 80)
            l4 = small[:, 87:89]
            link(TT(lamv[:, 0:4:2, :], lamv[:, 0:4:2, :], lamv[:, 1:4:2, :], ALU.mult))
            RED(l4, lamv[:, 0:4:2, :], AX_X, ALU.add).then_inc(S["lam_done"], 1)
            dve.wait_ge(W["bias_in"], 48)

            def rest_of_ada(n):
                dve.wait_ge(W["lead_done"], n + 1)
                TT(r32(wadaL[n % 6][:, :, :]), wada[n % 6][:, :, :], wadaH[n % 3][:, :, :], ALU.subtract).then_inc(S["rest_done"], 1)

            rest_of_ada(0)
            rest_of_ada(1)
            dve.wait_ge(W["lam_exp"], 1)
            link(TT(neglam, small[:, 86:87], small[:, 85:86], ALU.subtract))
            link(TS(neglam, neglam, -LAM_INIT, None, ALU.add))
            link(TS(gsub, gsub, 1.0 - LAM_INIT, None, ALU.mult))
            dve.wait_ge(W["const_in"], 16)
            link(STT(sgn, C("sub1", 32), neglam[0:32, :], C("sub0", 32), ALU.mult, ALU.add))
            for b in range(ADAB):
                if b + 1 < ADAB:
                    rest_of_ada(2 * b + 2)
                    rest_of_ada(2 * b + 3)
                dve.wait_ge(W["ada_ps"], b + 1)
                a = slice(512 * b, 512 * b + 512)
                TT(mod[:, a], psum[0:9, b % 2, :], mod[:, a], ALU.add).then_inc(S["ada_sb"], 1)
                for name, ln in (("scale_a", lnm), ("scale_f", lnf)):
                    if b == 2 * MOD[name] + 1:
                        dve.wait_ge(W["ada_sb"], b + 1)
                        a = slice(MOD[name] * D, MOD[name] * D + D)
                        STT(mod[:, a], mod[:, a], 1.0, ln[:, :], ALU.add, ALU.mult).then_inc(S["gain_done"], 1)

            def mod_row(t, which):
                return (which[0] if t < NT - 1 else which[1])[0:rows(t), :]

            def make_h(t):
                n = rows(t)
                dve.wait_ge(W["rstd_done"], t + 1)
                if t >= 2:
                    dve.wait_ge(W["hT_ps"], t - 1)
                h = hrow[t % 2][0:n, :]
                link(STT(h, xin[t % 3][0:n, :], rstd[0:n, t:t + 1], mod_row(t, (scale_p, scale_s)), ALU.mult, ALU.mult))
                TT(h, h, mod_row(t, (shift_p, shift_s)), ALU.add).then_inc(S["h_done"], 1)

            def rotate(t, name, b, row):
                n = rows(t)
                dve.wait_ge(W["qkv_ps"], 3 * t + (1 if name == "q" else 2))
                if t >= 2:
                    dve.wait_ge(W[f"{name}T_ps"], t - 1)
                    if name == "k":
                        dve.wait_ge(W[f"kv_out{t % 2}"], 32 * (t // 2))
                src = psum[0:n, b, :].rearrange("p (s u d) -> p s u d", s=SUBS, u=2)
                dst = row[t % 2][0:n, :].rearrange("p (s u d) -> p s u d", s=SUBS, u=2)
                tmp = ropet[0:n, :].rearrange("p (s u d) -> p s u d", s=SUBS, u=2)
                cos, nsin, sin = (rope[0:n, t, 32 * k:32 * k + 32] for k in range(3))
                TT(dst, src, bc(cos, [n, SUBS, 2, 32], (1, 1)), ALU.mult)
                TT(tmp[:, :, 0, :], src[:, :, 1, :], bc(nsin, [n, SUBS, 32], (1,)), ALU.mult)
                link(TT(tmp[:, :, 1, :], src[:, :, 0, :], bc(sin, [n, SUBS, 32], (1,)), ALU.mult))
                TT(dst, dst, tmp, ALU.add).then_inc(S[f"{name}_done"], 1)
                dve.wait_ge(W[f"{name}_done"], t + 1)

            dve.wait_ge(W["mix_rows_in"], 2 * ROWSEMS)
            make_h(0)
            make_h(1)
            for t in range(NT):
                if t + 2 < NT:
                    make_h(t + 2)
                rotate(t, "q", 2, qrow)
                rotate(t, "k", 3, krow)

            dve.wait_ge(W["state_ps"], 1)
            samples = cuT[:, :, 2 + SEQ:].rearrange("p c (s n) -> p c s n", s=NSEQ)
            nc.vector.memset(cuT[:, :, 0:2], 0.0)
            nc.vector.tensor_copy(samples[:, :, :, 0:2], psum[:, 6, 0:64].rearrange("p (c s n) -> p c s n", c=4, s=NSEQ)).then_inc(S["state_sb_s"], 1)
            nc.vector.tensor_copy(wcvT[:, :, 0:3], psum[:, 6, 64:80].rearrange("p (c k) -> p c k", c=4)[:, :, 0:3]).then_inc(S["state_sb_s"], 1)
            dve.wait_ge(W["state_sb_s"], 2)
            for i in range(4):
                for tb in range(3):
                    n = 3 * i + tb
                    dve.wait_ge(W["gates_sb"], 2 * n + 1)
                    src = psum[:, 3 * (n % 2) + 2, 0:TB]
                    m = TB if tb < 2 else TB - NSAMP
                    dst = cuT[:, i, 2 + TB * tb:2 + TB * tb + m]
                    last = TT(dst, src[:, 0:m], cg_sb[:, 0:m], ALU.mult)
                    if tb == 2:
                        last = TT(samples[:, i, :, 2:], src[:, m:].rearrange("p (s n) -> p s n", s=NSEQ),
                                  cg_sb[:, m:].rearrange("p (s n) -> p s n", s=NSEQ), ALU.mult)
                    last.then_inc(S["cu_done"], 1)
                dve.wait_ge(W["cu_done"], 3 * i + 3)
                dve.wait_ge(W["gates_sb"], 6 * i + 6)
                if i:
                    dve.wait_ge(W["conv_done"], 2 * i)
                for part in range(2):
                    if part == 0:
                        tap = [cuT[:, i, k:k + SEQ] for k in range(3)]
                        acc, gate, dst = ctmp[:, 0:SEQ], bg_sb[:, 0:SEQ], mixC[:, i, 0:SEQ]
                    else:
                        tap = [samples[:, i, :, k:k + LNEW] for k in range(3)]
                        acc, gate, dst = (v.rearrange("p (s n) -> p s n", s=NSEQ) for v in
                                          (ctmp[:, SEQ:TOK], bg_sb[:, SEQ:TOK], mixC[:, i, SEQ:TOK]))
                    link(TS(acc, tap[0], wcvT[:, i, 0:1], None, ALU.mult))
                    link(STT(acc, tap[1], wcvT[:, i, 1:2], acc, ALU.mult, ALU.add))
                    link(STT(acc, tap[2], wcvT[:, i, 2:3], acc, ALU.mult, ALU.add))
                    TT(dst, acc, gate, ALU.mult).then_inc(S["conv_done"], 1)

            scores = psum[:, 0:4, :].rearrange("p (s b) n -> p s (b n)", s=2)

            def maxima(w, u):
                i = w // HEADS
                dve.wait_ge(W["s_ps"], 2 * w + u + 1)
                diag = scores[:, u, P * i:P * i + P]
                TT(diag, diag, C("mask"), ALU.add).then_inc(S["mask_done"], 1)
                dve.wait_ge(W["mask_done"], 2 * w + u + 1)
                k = 2 * (w % 2) + u
                RED(nm[:, k:k + 1], scores[:, u, 0:P * (i + 1)], AX_X, ALU.max, negate=True).then_inc(S["nmax_done"], 1)

            def attention_rows(i):
                dve.wait_ge(W["rstdh_done"], i + 1)
                if i >= 1:
                    dve.wait_ge(W["attT_ps"], i)
                link(TT(hsc, r1s[i % 2], hrs, ALU.mult))
                for h in range(HEADS):
                    last = STT(attrow[:, P * h:P * h + P], psum[:, 6 + i % 2, P * h:P * h + P], hsc[:, h:h + 1], gsub, ALU.mult, ALU.mult)
                last.then_inc(S["att_done"], 1)

            maxima(0, 0)
            maxima(0, 1)
            for w in range(8 * HEADS):
                i, h = divmod(w, HEADS)
                if w + 1 < 8 * HEADS:
                    maxima(w + 1, 0)
                dve.wait_ge(W["exp_done"], 2 * w + 2)
                l0, l1 = ls[:, 2 * (w % 2):2 * (w % 2) + 1], ls[:, 2 * (w % 2) + 1:2 * (w % 2) + 2]
                nc.vector.reciprocal(r1s[i % 2][:, h:h + 1], l0)
                link(nc.vector.reciprocal(rl[:, 0:1], l1))
                link(STT(ratio, rl[:, 0:1], l0, neglam, ALU.mult, ALU.mult))
                if w >= 1:
                    dve.wait_ge(W["adT_ps"], w)
                nk = P * (i + 1)
                p2 = (pexp, pexp2)[w % 2]
                STT(adiff[:, 0:nk], p2[:, 1, 0:nk], ratio, p2[:, 0, 0:nk], ALU.mult, ALU.add).then_inc(S["adiff_done"], 1)
                if w + 1 < 8 * HEADS:
                    maxima(w + 1, 1)
                if w == 0:
                    nc.vector.tensor_copy(ncT[:, :, 0:2], cuT[:, :, SEQ:SEQ + 2])
                    nc.vector.tensor_copy(ncT[:, :, 2:].rearrange("p c (s n) -> p c s n", s=NSEQ), samples[:, :, :, LNEW:]).then_inc(S["ncT_done"], 1)
                if w == 12:
                    dve.wait_ge(W["conv_done"], 8)
                    dve.wait_ge(W["qT_sb"], NT)
                    link(nc.vector.memset(qbd[:, :, :, :], 0.0))
                    for c in range(4):
                        for u in range(2):
                            r = slice(64 * u, 64 * u + 64)
                            a = 8 * c + 4 * u
                            last = nc.vector.tensor_copy(qbd[r, :, c, a:a + LNEW], qTs[r, c, :].rearrange("p (s q) -> p s q", s=NSEQ))
                    last.then_inc(S["qbd_done"], 1)
                if h == 2 and i >= 1:
                    attention_rows(i - 1)
            attention_rows(7)

            def sample_maxima(s):
                b = s % 2
                dve.wait_ge(W["ds_ps"], s + 1)
                TT(snew[b][:, :], psum[0:32, 7, 256:256 + LNEW], C("dmask", 32), ALU.add).then_inc(S["dnew_done"], 1)
                dve.wait_ge(W["dnew_done"], s + 1)
                RED(dmx[:, 0:1], psum[0:32, 2 * b:2 * b + 2, :].rearrange("p b n -> p (b n)"), AX_X, ALU.max)
                link(RED(dmx[:, 1:2], snew[b][:, :], AX_X, ALU.max))
                link(TT(dmx[:, 2:3], dmx[:, 0:1], dmx[:, 1:2], ALU.max))
                TS(dmx[:, 3 + b:4 + b], dmx[:, 2:3], -1.0, None, ALU.mult).then_inc(S["dmax_done"], 1)

            def sample_weights(s):
                b = s % 2
                dve.wait_ge(W["da_ps"], s + 1)
                seq = [aTs[b][:, :, :].rearrange("p n (h x) -> p n h x", h=HEADS)[:, :, :, LNEW * r:LNEW * r + LNEW] for r in (s - 2, s)] if s >= 2 else [
                    None, aTs[b][:, :, :].rearrange("p n (h x) -> p n h x", h=HEADS)[:, :, :, LNEW * s:LNEW * s + LNEW]]
                if s >= 2:
                    dve.wait_ge(W["do_ps"], s - 1)
                    nc.vector.memset(seq[0], 0.0)
                nc.vector.tensor_copy(seq[1][:, 0:PAGES], psum[:, 7, 0:16 * PAGES].rearrange("p (n h q) -> p n h q", n=PAGES, h=HEADS))
                nc.vector.tensor_copy(seq[1][0:LNEW, PAGES], psum[0:LNEW, 7, 16 * PAGES:16 * PAGES + 16].rearrange("p (h q) -> p h q", h=HEADS)).then_inc(S["da_sb"], 1)

            def sample_pairs(s):
                dve.wait_ge(W["dexp_done"], 2 * s + 2)
                link(TT(dl[:, 2:3], dl[:, 0:1], dl[:, 1:2], ALU.add))
                link(nc.vector.reciprocal(dr[:, 0:1], dl[:, 2:3]))
                link(TT(dr[:, 1:2], dr[:, 0:1], sgn, ALU.mult))
                TS(pairs[s % 2][:, :], C("pair", 32), dr[:, 1:2], None, ALU.mult).then_inc(S["pair_done"], 1)

            dve.wait_ge(W["attT_ps"], 8)
            for b in range(2):
                link(nc.vector.memset(aTs[b][:, :, :], 0.0))
            for s in range(NSEQ):
                sample_maxima(s)
                if s >= 1:
                    sample_weights(s - 1)
                sample_pairs(s)
            sample_weights(NSEQ - 1)
            for c in range(DC):
                dve.wait_ge(W["lead_done"], 2 * ADAB + c + 1)
                TT(r32(woutL[:, c, :]), wout[:, c, :], lead_of_wout(c), ALU.subtract).then_inc(S["rest_done"], 1)
            def rest_of_mix(m):
                t, half = divmod(m, 2)
                n = rows(t)
                dve.wait_ge(W["lead_done"], 2 * ADAB + DC + m + 1)
                src = (mixA, mixC)[half][:, :, P * t:P * t + n]
                TT(r32(mixL[m % 3][:, :, 0:n]), src, mixH[m % 3][:, :, 0:n], ALU.subtract).then_inc(S["rest_done"], 1)

            rest_of_mix(0)
            rest_of_mix(1)
            dve.wait_ge(W["rstds_done"], 1)
            for h in range(HEADS):
                last = STT(attrow[0:NSAMP, P * h:P * h + P], orow[:, h, :], hrs[0:NSAMP, h:h + 1],
                           gsub[0:NSAMP, :], ALU.mult, ALU.mult)
            last.then_inc(S["atts_done"], 1)

            def make_h2(t):
                n = rows(t)
                dve.wait_ge(W["rstd2_done"], t + 1)
                if t >= 2:
                    dve.wait_ge(W["h2T_ps"], t - 1)
                    dve.wait_ge(W[f"h2_out{t % 2}"], 16 * (t // 2))
                h = h2row[t % 2][0:n, :]
                link(STT(h, x1[0:n, t, :], rs2[0:n, t:t + 1], mod_row(t, (scale_p, scale_s)), ALU.mult, ALU.mult))
                TT(h, h, mod_row(t, (shift_p, shift_s)), ALU.add).then_inc(S["h2_done"], 1)

            def take_logits(t):
                n = rows(t)
                dve.wait_ge(W["lg_ps"], t + 1)
                TT(logit[0:n, t, :], psum[0:n, 6, 0:NG + NE], brt[0:n, :], ALU.add).then_inc(S["lg_done"], 1)

            dve.wait_ge(W["wout_in"], 80)
            link(nc.vector.memset(logit[:, NT - 1, :], 0.0))
            dve.wait_ge(W["sub2_rows_in"], 3 * ROWSEMS + 16 * NT)
            for t in range(NT):
                n = rows(t)
                if t >= 1:
                    make_h2(t - 1)
                if t + 1 < NT:
                    rest_of_mix(2 * t + 2)
                    rest_of_mix(2 * t + 3)
                for j in range(2):
                    a = slice(512 * j, 512 * j + 512)
                    dve.wait_ge(W["mix_ps"], 2 * t + j + 1)
                    if t or j:
                        dve.wait_ge(W["x1_done"], 2 * t + j)
                    link(TT(otmp[0:n, :], psum[0:n, 2 * (t % 2) + j, :], mod_row(t, (gate_ap, gate_as))[:, a], ALU.mult))
                    TT(x1[0:n, t, a], x1[0:n, t, a], otmp[0:n, :], ALU.add).then_inc(S["x1_done"], 1)
                if t >= 2:
                    take_logits(t - 2)
            make_h2(NT - 1)
            take_logits(NT - 2)
            take_logits(NT - 1)

            dve.wait_ge(W["lg_done"], NT)
            dve.wait_ge(W["h2T_ps"], NT)
            dve.wait_ge(W["h2_out0"], 16 * 5)
            dve.wait_ge(W["h2_out1"], 16 * 4)
            nc.vector.memset(ones[:, :], 1.0)
            r3 = lambda n, k: R[n].rearrange("p (t e) -> p t e", e=k)
            LG, LE = logit[:, :, 0:NG], logit[:, :, NG:NG + NE]
            iota4, iota32 = C("iota")[:, 0:NG], C("iota")[:, 0:NE]

            def first_max(eq, oh, scores_, top, k, iota, mn):
                link(RED(top, scores_, AX_X, ALU.max))
                link(TT(eq, scores_, bc(top, [P, NT, k], (2,)), ALU.is_equal))
                link(STT(eq, eq, -64.0, bc(iota, [P, NT, k], (1,)), ALU.mult, ALU.add))
                link(RED(mn, eq, AX_X, ALU.min))
                link(TT(oh, eq, bc(mn, [P, NT, k], (2,)), ALU.is_equal))

            first_max(r3("eq4", NG), r3("ohg", NG), LG, R["gm"], NG, iota4, R["mn"])
            TT(r3("gs", NG), LG, bc(R["gm"], [P, NT, NG], (2,)), ALU.subtract).then_inc(S["rexp_in"], 1)
            link(TS(R["pen"], R["ohg"], -NEG, NEG, ALU.mult, ALU.add))
            el4 = R["el"].rearrange("p (t g e) -> p t g e", g=NG, e=EPG)
            link(TT(el4, LE.rearrange("p t (g e) -> p t g e", g=NG), bc(r3("pen", NG), [P, NT, NG, EPG], (3,)), ALU.add))
            first_max(r3("ta", NE), r3("oh1", NE), r3("el", NE), R["m1"], NE, iota32, R["mn"])
            link(STT(r3("el", NE), r3("oh1", NE), 2 * NEG, r3("el", NE), ALU.mult, ALU.add))
            first_max(r3("ta", NE), r3("oh2", NE), r3("el", NE), R["m2"], NE, iota32, R["mn"])
            TT(R["dd"], R["m2"], R["m1"], ALU.subtract).then_inc(S["rexp_in"], 1)
            for k in ("oh1", "oh2"):
                link(TT(r3(k, NE), r3(k, NE), bc(C("valid"), [P, NT, NE], (2,)), ALU.mult))
            TT(R["ohs"], R["oh1"], R["oh2"], ALU.add).then_inc(S["oh_done"], 1)
            dve.wait_ge(W["rexp_done"], 1)
            link(RED(R["gsum"], r3("ge", NG), AX_X, ALU.add))
            link(nc.vector.reciprocal(R["gp"], R["gsum"]))
            dve.wait_ge(W["rexp_done"], 2)
            link(TS(R["ws"], R["ee"], 1.0, None, ALU.add))
            link(nc.vector.reciprocal(R["ws"], R["ws"]))
            link(TT(cw[:, 0, :], R["ws"], R["gp"], ALU.mult))
            link(TT(cw[:, 1, :], cw[:, 0, :], R["ee"], ALU.mult))
            dve.wait_ge(W["cnt_ps"], 1)
            base, tot = r3("base", NE), psum[:, 1, 0:NT * NE].rearrange("p (t e) -> p t e", e=NE)
            link(nc.vector.memset(base[:, 0, :], 0.0))
            for t in range(1, NT):
                link(TT(base[:, t, :], tot[:, t - 1, :], base[:, t - 1, :], ALU.add))
            link(TT(R["cnt"], tot[:, NT - 1, :], base[:, NT - 1, :], ALU.add))
            link(nc.vector.memset(R["nt"], 1.0))
            for q in range(1, (TOK + P - 1) // P):
                link(STT(R["nt"], R["cnt"], float(P * q), R["nt"], ALU.is_gt, ALU.add))
            cur, nxt = "inca", "incb"
            link(nc.vector.tensor_copy(R[cur], R["nt"]))
            for d in (1, 2, 4, 8, 16):
                nc.vector.tensor_copy(R[nxt][:, 0:d], R[cur][:, 0:d])
                link(TT(R[nxt][:, d:], R[cur][:, d:], R[cur][:, 0:NE - d], ALU.add))
                cur, nxt = nxt, cur
            inc = R[cur]
            link(TT(R["first"], inc, R["nt"], ALU.subtract))
            link(TT(R["ta"][:, 0:NE], inc, C("tilecol").to_broadcast([P, NE]), ALU.is_le))
            pcol = R["pcol"]
            link(RED(pcol, R["ta"][:, 0:NE], AX_X, ALU.add))
            TS(pcol, pcol, float(NE - 1), None, ALU.min).then_inc(S["tcols_done"], 1)
            link(TS(R["mn"][0:1, 0:1], inc[0:1, NE - 1:NE], -3.0, None, ALU.add))
            link(nc.vector.tensor_copy(plan[0:1, MID + 1:MID + 2], R["mn"][0:1, 0:1]))
            link(TS(plan[0:1, MID:MID + 1], plan[0:1, MID + 1:MID + 2], 1, None, ALU.logical_shift_right))
            nc.vector.tensor_copy(plan[0:1, INC:INC + NE], inc[0:1, :])
            dve.wait_ge(W["plan_ps"], 1)
            nc.vector.tensor_copy(plan[0:1, 0:TCOLS], psum[0:1, 7, 0:TCOLS]).then_inc(S["plan_done"], 1)
            link(TT(base, psum[:, 0, 0:NT * NE].rearrange("p (t e) -> p t e", e=NE), base, ALU.add))
            link(STT(base, bc(R["first"], [P, NT, NE], (1,)), float(P), base, ALU.mult, ALU.add))
            slot = R["slot"].rearrange("p (t k) -> p t k", k=2)
            for k, name in enumerate(("oh1", "oh2")):
                link(TT(r3("ta", NE), r3(name, NE), base, ALU.mult))
                link(RED(slot[:, :, k], r3("ta", NE), AX_X, ALU.add))
            link(nc.vector.tensor_copy(slot_i[:, :], R["slot"]))
            flat_i = slot_i[:, :]
            link(TS(slot_lo[:, :], flat_i, P - 1, None, ALU.bitwise_and))
            link(TS(slot_hi[:, :], flat_i, 7, None, ALU.logical_shift_right))
            link(nc.vector.tensor_copy(R["lo"], slot_lo[:, :]))
            link(nc.vector.tensor_copy(R["hi"], slot_hi[:, :]))
            for n in range(2 * NT):
                if n >= 4:
                    dve.wait_ge(W["map_ps"], n - 3)
                TS(lsel[n % 4][:, :], C("iota"), R["lo"][:, n:n + 1], None, ALU.is_equal)
                TS(hsel[n % 4][:, :], C("iota")[:, 0:TCOLS], R["hi"][:, n:n + 1], C("tokid")[:, n:n + 1],
                   ALU.is_equal, ALU.mult).then_inc(S["sel_done"], 1)
            dve.wait_ge(W["map_ps"], 2 * NT)
            link(TS(vmap[:, 0, :], psum[:, 2, 0:TCOLS], 0.0, float(NOROW), ALU.is_equal, ALU.mult))
            link(TS(vmap[:, 1, :], psum[:, 2, 0:TCOLS], TOK + 0.5, float(-TOK), ALU.is_gt, ALU.mult))
            link(STT(vmap[:, 0, :], psum[:, 2, 0:TCOLS], -1.0, vmap[:, 0, :], ALU.add, ALU.add))
            link(TT(vmap[:, 1, :], vmap[:, 1, :], vmap[:, 0, :], ALU.add))
            link(nc.vector.tensor_copy(xrow[:, :], vmap[:, 1, :]))
            nc.vector.tensor_copy(yidx[:, :], vmap[:, 0, :]).then_inc(S["plan_done"], 1)

            mid = dve.value_load(plan[0:1, MID:MID + 1], min_val=NE // 2 - 2, max_val=MAXT // 2 - 2)

            def rest_gate_up(e, slot, g):
                dve.wait_ge(W["wguH_done"], 2 * e + (g + 1))
                TT(r32(wguL[slot][:, g, :, :]), wgu[slot][:, g, :, :], wguH[slot][:, g, :, :], ALU.subtract).then_inc(S["wguL_done"], 1)

            def rest_down(e, slot):
                dve.wait_ge(W["wdnH_done"], e + 1)
                TT(r32(wdnL[slot][:, :, :]), wdn[slot][:, :, :], wdnH[slot][:, :, :], ALU.subtract).then_inc(S["wdnL_done"], 1)

            def rest_rows(j, b):
                dve.wait_ge(W["xgH_done"], j + 1)
                TT(r32(xgL[b][:, :, :]), psum[:, 0:2, :].rearrange("p b (c n) -> p (b c) n", c=4), xgH[b][:, :, :],
                   ALU.subtract).then_inc(S["xgL_done"], 1)

            def expert_rests(j, b, i, first, left):
                if left:
                    e = expert_of(dve, j + 1)
                    new = step_of(e, expert_of(dve, j))
                    in_slot(dve, e, lambda slot: rest_gate_up(e, slot, 0), new)
                dve.wait_ge(W["th_done"], j + 1)
                STT(gated[b][:, :], th[b][:, :], 1.0, psum[:, 2 + b, 0:FE], ALU.add, ALU.mult).then_inc(S["m_dve_step"], 1)
                dve.wait_ge(S["m_dve_step"], j + 1)
                STT(hid[b][:, :], gated[b][:, :], 0.5, psum[:, 2 + b, FE:2 * FE], ALU.mult, ALU.mult).then_inc(S["hid_done"], 1)
                if left:
                    in_slot(dve, e, lambda slot: rest_gate_up(e, slot, 1), new)
                    rest_rows(j + 1, 1 - b)
                if first and b == 0:
                    rest_down(0, 0)
                else:
                    e = expert_of(dve, j)
                    in_slot(dve, e, lambda slot: rest_down(e, slot), step_of(e, expert_of(dve, j - 1)))
                dve.wait_ge(W["hidH_done"], j + 1)
                TT(r32(hidL[b][:, :, :]), psum[:, 4, 0:FE].rearrange("p (c n) -> p c n", c=FC), hidH[b][:, :, :],
                   ALU.subtract).then_inc(S["hidL_done"], 1)

            for g in range(2):
                rest_gate_up(0, 0, g)
            rest_rows(0, 0)
            expert_steps(dve, expert_rests, mid)

            def finish(t):
                n = rows(t)
                dve.wait_ge(W["rstd3_done"], t + 1)
                if t >= 2:
                    dve.wait_ge(W[f"fin_out{t % 2}"], 16 * (t // 2))
                STT(fin[t % 2][0:n, :], x1[0:n, t, :], rs2[0:n, t:t + 1], lnfin[0:n, :], ALU.mult, ALU.mult).then_inc(S["fin_done"], 1)

            dve.wait_ge(W["fin_rows_in"], ROWSEMS + 16)
            for t in range(NT):
                n = rows(t)
                dve.wait_ge(W["scaled_done"], t + 1)
                y0, y1 = yg[t % 3][0][0:n, :], yg[t % 3][1][0:n, :]
                link(STT(y0, y1, cw[0:n, 1, t:t + 1], y0, ALU.mult, ALU.add))
                link(TT(y0, y0, mod_row(t, (gate_fp, gate_fs)), ALU.mult))
                TT(x1[0:n, t, :], x1[0:n, t, :], y0, ALU.add).then_inc(S["comb_done"], 1)
                if t >= 1:
                    finish(t - 1)
            finish(NT - 1)

        @block.gpsimd
        def _(pool):
            steps = [0]

            def link(ins):
                steps[0] += 1
                ins.then_inc(S["pool_step"], 1)
                pool.wait_ge(S["pool_step"], steps[0])

            def inverse_root(dst, src, width, eps, done):
                link(nc.gpsimd.tensor_scalar(src, src, 1.0 / width, eps, ALU.mult, ALU.add))
                n, m = src.shape
                nc.gpsimd.tensor_tensor(dst, src, C("half", n).to_broadcast([n, m]), ALU.pow).then_inc(done, 1)

            def store_mod(a, b, blocks, gains):
                pool.wait_ge(W["ada_sb"], blocks)
                pool.wait_ge(W["gain_done"], gains)
                pool.dma_start(mod_dram[:, a:b], mod[:, a:b]).then_inc(S["mod_out"], 16)

            store_mod(0, 2 * D, 4, 1)

            def root(t):
                n = rows(t)
                pool.wait_ge(W["ssq_done"], t + 1)
                inverse_root(rstd[0:n, t:t + 1], ssq[0:n, t:t + 1], D, NORM_EPS, S["rstd_done"])

            for t in range(3):
                root(t)
            store_mod(2 * D, 6 * D, 12, 2)
            for t in range(NT):
                n = rows(t)
                if t + 3 < NT:
                    root(t + 3)
                pool.wait_ge(W["k_done"], t + 1)
                pool.wait_ge(W["v_done"], t + 1)
                ko, vo = (kp_out[P * t:P * t + P, :], vp_out[P * t:P * t + P, :]) if t < NT - 1 else (ks_out, vs_out)
                pool.dma_start(ko, krow[t % 2][0:n, :]).then_inc(S[f"kv_out{t % 2}"], 16)
                pool.dma_start(vo, v_sb[:, t, :] if t < NT - 1 else vs_row[0:n, :]).then_inc(S[f"kv_out{t % 2}"], 16)

            def pad_queries(i):
                if i >= 2:
                    pool.wait_ge(W["s_ps"], 8 * (i - 1))
                link(nc.gpsimd.tensor_copy(qz[i % 2][0:64, 0, :, :], qT[0:64, :, P * i:P * i + P]))
                nc.gpsimd.tensor_copy(qz[i % 2][64:P, 1, :, :], qT[64:P, :, P * i:P * i + P]).then_inc(S["qz_done"], 1)
                pool.wait_ge(W["qz_done"], i + 1)

            pool.wait_ge(W["qT_sb"], NT)
            for i in range(2):
                link(nc.gpsimd.memset(qz[i][64:P, 0, :, :], 0.0))
                link(nc.gpsimd.memset(qz[i][0:64, 1, :, :], 0.0))
                pad_queries(i)
            pool.wait_ge(W["nc_sb"], 1)
            pool.dma_start(cp_out, nc_row[0:2, :]).then_inc(S["nc_out"], 16)
            pool.dma_start(cs_out, nc_row[2:18, :]).then_inc(S["nc_out"], 16)
            for i in range(8):
                if i + 2 < 8:
                    if i >= 1:
                        pool.wait_ge(W["rstdh_done"], i)
                    pad_queries(i + 2)
                pool.wait_ge(W["ssqh_done"], 4 * i + 4)
                inverse_root(hrs, hss, P, SUBLN_EPS, S["rstdh_done"])
            pool.wait_ge(W["ssqs_done"], 4)
            inverse_root(hrs[0:NSAMP, :], hss[0:NSAMP, :], P, SUBLN_EPS, S["rstds_done"])

            for t in range(NT):
                n = rows(t)
                pool.wait_ge(W["ssq2_done"], t + 1)
                inverse_root(rs2[0:n, t:t + 1], ss2[0:n, t:t + 1], D, NORM_EPS, S["rstd2_done"])
                pool.wait_ge(W["h2_done"], t + 1)
                pool.dma_start(h2_dram[P * t:P * t + n, :], h2row[t % 2][0:n, :]).then_inc(S[f"h2_out{t % 2}"], 16)

            pool.wait_ge(W["x1_done"], 2 * NT)
            for b in range(2):
                link(nc.gpsimd.memset(xg[b][:, :], 0.0))
            pool.wait_ge(W["h2_out0"], 16 * 5)
            pool.wait_ge(W["h2_out1"], 16 * 4)
            pool.wait_ge(W["plan_done"], 2)
            mid = pool.value_load(plan[0:1, MID:MID + 1], min_val=NE // 2 - 2, max_val=MAXT // 2 - 2)

            def gather_rows(j, b):
                nc.gpsimd.tensor_copy(gidx[b][:, :], xrow[:, bass.ds(j, 1)]).then_inc(S["gidx_done"], 1)
                pool.wait_ge(W["gidx_done"], j + 1)
                pool.sem_inc(S["go_on"], 1)
                nc.gpsimd.indirect_dma_start(xg[b][:, :], None, h2_dram, bass.IndirectOffsetOnAxis(ap=gidx[b][:, 0:1], axis=0),
                                             bounds_check=TOK - 1, oob_is_err=False).then_inc(S[f"xg_in{b}"], 16)

            def scatter_rows(j, b):
                pool.wait_ge(W["y_done"], j + 1)
                pool.sem_inc(S["go_on"], 1)
                nc.gpsimd.tensor_copy(sidx[b][:, :], yidx[:, bass.ds(j, 1)]).then_inc(S["sidx_done"], 1)
                pool.wait_ge(W["sidx_done"], j + 1)
                pool.sem_inc(S["go_on"], 1)
                nc.gpsimd.indirect_dma_start(y_dram, bass.IndirectOffsetOnAxis(ap=sidx[b][:, 0:1], axis=0), yrow[b][:, :], None,
                                             bounds_check=2 * TOK - 1, oob_is_err=False).then_inc(S[f"y_out{b}"], 16)

            def move_rows(j, b, i, first, left):
                if left == 2:
                    pool.wait_ge(W["xgT_ps"], j + 1)
                    pool.sem_inc(S["go_on"], 1)
                    gather_rows(j + 2, b)
                if not (first and b == 0):
                    scatter_rows(j - 1, 1 - b)

            gather_rows(0, 0)
            gather_rows(1, 1)
            expert_steps(pool, move_rows, mid)
            scatter_rows(2 * mid + 3, 1)

            for t in range(NT):
                n = rows(t)
                pool.wait_ge(W["ssq3_done"], t + 1)
                inverse_root(rs2[0:n, t:t + 1], ss2[0:n, t:t + 1], D, NORM_EPS, S["rstd3_done"])


_INS = ['x_prompt', 'x_sample', 'cache_k', 'cache_v', 'state_conv', 'page_table', 'c_prompt', 'c_sample',
        'w_ada', 'b_ada', 'ln_mix', 'w_in', 'lam_q1', 'lam_k1', 'lam_q2', 'lam_k2', 'subln_g', 'w_conv', 'w_out',
        'ln_ffn', 'w_router_grp', 'b_router_grp', 'w_router_exp', 'b_router_exp', 'w_gate', 'w_up', 'w_down', 'ln_final']
_OUTS = [(1, SEQ, D), (NSEQ, LNEW, D), (1, 1, SEQ, SUBS, HD), (1, 1, SEQ, HEADS, 2 * HD), (1, 1, 2, AW),
         (1, NSEQ, LNEW, SUBS, HD), (1, NSEQ, LNEW, HEADS, 2 * HD), (1, NSEQ, 2, AW)]


def kernel(**inputs):
    import concourse.bacc as _bacc
    from concourse.bass_utils import run_bass_kernel_spmd as _run

    nc = _bacc.Bacc("TRN2", target_bir_lowering=False, num_devices=1)
    arrays, args = {"in_consts_dram": constants()}, []
    args.append(nc.dram_tensor("in_consts_dram", [P, NCONST], F32, kind="ExternalInput").ap())
    for name in _INS:
        a = np.ascontiguousarray(inputs[name])
        arrays[f"in_{name}_dram"] = a
        args.append(nc.dram_tensor(f"in_{name}_dram", a.shape, mybir.dt.from_np(a.dtype), kind="ExternalInput").ap())
    for i, shape in enumerate(_OUTS):
        args.append(nc.dram_tensor(f"out_{i}_dram", shape, F32, kind="ExternalOutput").ap())
    args.append(nc.dram_tensor("mod_scratch", [NSEQ + 1, 6 * D], F32, kind="Internal").ap())
    args.append(nc.dram_tensor("h2_scratch", [TOK, D], F32, kind="Internal").ap())
    args.append(nc.dram_tensor("y_scratch", [2 * TOK, D], F32, kind="Internal").ap())
    build(nc, *args)
    r = _run(nc, [arrays], core_ids=[0])
    return tuple(r.results[0][f"out_{i}_dram"] for i in range(len(_OUTS)))
```
